# Optimizing a Trainium2 kernel written in Bass

```python
import jax, jax.numpy as jnp
from jax import lax
import numpy as np

D_MODEL = 1024
BATCH = 1
SEQ = 256
DEPTH = 1

MEM_LEN = 256
MOBA_HEAD_DIM = 64
MOBA_HEADS = (D_MODEL // 2) // MOBA_HEAD_DIM
MOBA_WIDTH = MOBA_HEADS * MOBA_HEAD_DIM
MOBA_BLOCK = 256
MOBA_TOPK = 3
MOBA_Q_CHUNK = 16
GDN_HEAD_DIM = 128
GDN_HEADS = (D_MODEL // 2) // GDN_HEAD_DIM
GDN_WIDTH = GDN_HEADS * GDN_HEAD_DIM
GDN_CONV = 4
GDN_CHUNK = 64
MIX_WIDTH = MOBA_WIDTH + GDN_WIDTH
IN_SPLITS = [MOBA_WIDTH, MOBA_WIDTH, MOBA_WIDTH, 3 * GDN_WIDTH, GDN_WIDTH, GDN_HEADS, GDN_HEADS]
IN_PROJ_WIDTH = sum(IN_SPLITS)
XATTN_HEADS = 4
XATTN_HEAD_DIM = 128
XATTN_WIDTH = XATTN_HEADS * XATTN_HEAD_DIM
N_EXPERTS = 32
TOP_K = 4
D_FF_EXPERT = D_MODEL
SWIGLU_LIMIT = 7.0
SWIGLU_ALPHA = 1.702
MOE_BLOCK = 128
RMS_EPS = 1e-6

kernel_name = 'hybrid_moba_gdn_moe_block'

def rms_norm(x, g):
    xf = x.astype(jnp.float32)
    y = xf * lax.rsqrt(jnp.mean(xf * xf, axis=-1, keepdims=True) + RMS_EPS)
    return (y * g.astype(jnp.float32)).astype(x.dtype)

def l2norm(x):
    xf = x.astype(jnp.float32)
    return (xf * lax.rsqrt(jnp.sum(xf * xf, axis=-1, keepdims=True) + RMS_EPS)).astype(x.dtype)

def split_last(t, sizes):
    return jnp.split(t, np.cumsum(sizes)[:-1].tolist(), axis=-1)

def moba_attention(q, k, v):
    B, S, H, d = q.shape
    s_pad = -(-S // MOBA_BLOCK) * MOBA_BLOCK
    pad = ((0, 0), (0, s_pad - S), (0, 0), (0, 0))
    q, k, v = (jnp.pad(t, pad).transpose(0, 2, 1, 3) for t in (q, k, v))
    nb = s_pad // MOBA_BLOCK
    k_sel_n = min(MOBA_TOPK, nb)
    k_blk = k.reshape(B, H, nb, MOBA_BLOCK, d)
    v_blk = v.reshape(B, H, nb, MOBA_BLOCK, d)
    k_mean = jnp.mean(k_blk.astype(jnp.float32), axis=3)
    gate = jnp.einsum('bhsd,bhnd->bhsn', q.astype(jnp.float32), k_mean)
    q_blk = jnp.arange(s_pad) // MOBA_BLOCK
    past = jnp.arange(nb)[None, :] < q_blk[:, None]
    gate = jnp.where(past[None, None], gate, -jnp.inf)
    _, sel_idx = lax.top_k(gate, k_sel_n)
    sel_valid = jnp.arange(k_sel_n)[None, :] < q_blk[:, None]
    scale = d ** -0.5
    b_ix = jnp.arange(B)[:, None, None, None]
    h_ix = jnp.arange(H)[None, :, None, None]

    def chunk_attend(c):
        start = c * MOBA_Q_CHUNK
        q_c = lax.dynamic_slice_in_dim(q, start, MOBA_Q_CHUNK, axis=2)
        sel_c = lax.dynamic_slice_in_dim(sel_idx, start, MOBA_Q_CHUNK, axis=2)
        valid_c = lax.dynamic_slice_in_dim(sel_valid, start, MOBA_Q_CHUNK, axis=0)
        blk = start // MOBA_BLOCK
        k_own = lax.dynamic_index_in_dim(k_blk, blk, axis=2, keepdims=False)
        v_own = lax.dynamic_index_in_dim(v_blk, blk, axis=2, keepdims=False)
        k_g = k_blk[b_ix, h_ix, sel_c]
        v_g = v_blk[b_ix, h_ix, sel_c]
        s_sel = jnp.einsum('bhqd,bhqkjd->bhqkj', q_c, k_g).astype(jnp.float32) * scale
        s_sel = jnp.where(valid_c[None, None, :, :, None], s_sel, -jnp.inf)
        s_sel = s_sel.reshape(B, H, MOBA_Q_CHUNK, k_sel_n * MOBA_BLOCK)
        q_pos = start + jnp.arange(MOBA_Q_CHUNK)
        k_pos = blk * MOBA_BLOCK + jnp.arange(MOBA_BLOCK)
        s_own = jnp.einsum('bhqd,bhjd->bhqj', q_c, k_own).astype(jnp.float32) * scale
        s_own = jnp.where((k_pos[None, :] <= q_pos[:, None])[None, None], s_own, -jnp.inf)
        p = jax.nn.softmax(jnp.concatenate([s_sel, s_own], axis=-1), axis=-1).astype(v.dtype)
        p_sel = p[..., :k_sel_n * MOBA_BLOCK].reshape(B, H, MOBA_Q_CHUNK, k_sel_n, MOBA_BLOCK)
        p_own = p[..., k_sel_n * MOBA_BLOCK:]
        return (jnp.einsum('bhqkj,bhqkjd->bhqd', p_sel, v_g)
                + jnp.einsum('bhqj,bhjd->bhqd', p_own, v_own))

    out = lax.map(chunk_attend, jnp.arange(s_pad // MOBA_Q_CHUNK))
    out = out.transpose(1, 0, 3, 2, 4).reshape(B, s_pad, H, d)
    return out[:, :S]

def causal_short_conv(x, w):
    S = x.shape[1]
    xp = jnp.pad(x, ((0, 0), (GDN_CONV - 1, 0), (0, 0)))
    return sum(w[j] * xp[:, j:j + S] for j in range(GDN_CONV))

def gated_delta_rule(q, k, v, g, beta):
    B, S, H, dk = q.shape
    dv = v.shape[-1]
    out_dtype = v.dtype
    C = GDN_CHUNK
    N = S // C
    f32 = jnp.float32

    def to_chunks(t):
        t = jnp.moveaxis(t.astype(f32), 2, 1)
        return t.reshape(B, H, N, C, *t.shape[3:])

    q, k, v, g, beta = (to_chunks(t) for t in (q, k, v, g, beta))
    q = q * dk ** -0.5
    g = jnp.cumsum(g, axis=-1)
    idx = jnp.arange(C)
    causal = idx[:, None] >= idx[None, :]
    strict = idx[:, None] > idx[None, :]
    decay = jnp.exp(jnp.where(causal, g[..., :, None] - g[..., None, :], -jnp.inf))
    k_beta = k * beta[..., None]
    a_strict = jnp.where(strict, jnp.einsum('bhnid,bhnjd->bhnij', k_beta, k) * decay, 0.0)
    rhs = jnp.concatenate([v * beta[..., None], k_beta * jnp.exp(g)[..., None]], axis=-1)
    uw = lax.linalg.triangular_solve(a_strict + jnp.eye(C, dtype=f32), rhs,
                                     left_side=True, lower=True, unit_diagonal=True)
    u, w = uw[..., :dv], uw[..., dv:]
    qk = jnp.einsum('bhnid,bhnjd->bhnij', q, k) * decay
    g_last = g[..., -1]
    q_dec = q * jnp.exp(g)[..., None]
    k_dec = k * jnp.exp(g_last[..., None] - g)[..., None]
    xs = tuple(jnp.moveaxis(t, 2, 0) for t in (u, w, qk, q_dec, k_dec, g_last))

    def step(state, inp):
        u_n, w_n, qk_n, qd_n, kd_n, gl_n = inp
        v_new = u_n - jnp.einsum('bhck,bhkv->bhcv', w_n, state)
        o_n = (jnp.einsum('bhck,bhkv->bhcv', qd_n, state)
               + jnp.einsum('bhij,bhjv->bhiv', qk_n, v_new))
        state = state * jnp.exp(gl_n)[..., None, None] + jnp.einsum('bhck,bhcv->bhkv', kd_n, v_new)
        return state, o_n

    _, o = lax.scan(step, jnp.zeros((B, H, dk, dv), f32), xs)
    o = o.transpose(1, 0, 3, 2, 4).reshape(B, S, H, dv)
    return o.astype(out_dtype)

def gated_deltanet(qkv, z, b, a, conv_w, A_log, dt_bias, norm_g):
    B, S, _ = qkv.shape
    qkv = jax.nn.silu(causal_short_conv(qkv, conv_w))
    q, k, v = (t.reshape(B, S, GDN_HEADS, GDN_HEAD_DIM) for t in jnp.split(qkv, 3, axis=-1))
    q, k = l2norm(q), l2norm(k)
    beta = jax.nn.sigmoid(b.astype(jnp.float32))
    g = -jnp.exp(A_log.astype(jnp.float32)) * jax.nn.softplus(a.astype(jnp.float32) + dt_bias.astype(jnp.float32))
    o = gated_delta_rule(q, k, v, g, beta)
    o = rms_norm(o, norm_g) * jax.nn.silu(z).reshape(B, S, GDN_HEADS, GDN_HEAD_DIM)
    return o.reshape(B, S, GDN_WIDTH)

def parallel_mixer(h, w_in, conv_w, A_log, dt_bias, gdn_norm_g, moba_norm_g, w_out):
    B, S, _ = h.shape
    proj = h @ w_in
    mq, mk, mv, gqkv, gz, gb, ga = split_last(proj, IN_SPLITS)
    heads = lambda t: t.reshape(B, S, MOBA_HEADS, MOBA_HEAD_DIM)
    o_moba = moba_attention(heads(mq), heads(mk), heads(mv)).reshape(B, S, MOBA_WIDTH)
    o_moba = rms_norm(o_moba, moba_norm_g)
    o_gdn = gated_deltanet(gqkv, gz, gb, ga, conv_w, A_log, dt_bias, gdn_norm_g)
    return jnp.concatenate([o_moba, o_gdn], axis=-1) @ w_out

def memory_cross_attention(h, m, w_q, w_kv, w_o):
    B, S, _ = h.shape
    M = m.shape[1]
    q = (h @ w_q).reshape(B, S, XATTN_HEADS, XATTN_HEAD_DIM)
    k, v = (t.reshape(B, M, XATTN_HEADS, XATTN_HEAD_DIM) for t in jnp.split(m @ w_kv, 2, axis=-1))
    s = jnp.einsum('bshd,bmhd->bhsm', q, k).astype(jnp.float32) * XATTN_HEAD_DIM ** -0.5
    p = jax.nn.softmax(s, axis=-1).astype(v.dtype)
    o = jnp.einsum('bhsm,bmhd->bshd', p, v).reshape(B, S, XATTN_WIDTH)
    return o @ w_o

def moe_ffn(h, router_w, router_b, w_gate_up, b_gate_up, w_down, b_down):
    B, S, D = h.shape
    T = B * S
    hf = h.reshape(T, D)
    logits = (hf @ router_w + router_b).astype(jnp.float32)
    top_logits, top_idx = lax.top_k(logits, TOP_K)
    gates = jax.nn.softmax(top_logits, axis=-1).astype(h.dtype)
    n_rows = T * TOP_K
    flat_e = top_idx.reshape(-1)
    flat_tok = jnp.arange(n_rows, dtype=jnp.int32) // TOP_K
    flat_gate = gates.reshape(-1)
    order = jnp.argsort(flat_e)
    e_sorted = flat_e[order]
    counts = jnp.bincount(flat_e, length=N_EXPERTS)
    padded = (counts + MOE_BLOCK - 1) // MOE_BLOCK * MOE_BLOCK
    group_start = jnp.cumsum(counts) - counts
    padded_end = jnp.cumsum(padded)
    padded_start = padded_end - padded
    dest = padded_start[e_sorted] + (jnp.arange(n_rows) - group_start[e_sorted])
    n_blocks = -(-n_rows // MOE_BLOCK) + N_EXPERTS
    R = n_blocks * MOE_BLOCK
    row_tok = jnp.zeros((R,), jnp.int32).at[dest].set(flat_tok[order])
    row_gate = jnp.zeros((R,), h.dtype).at[dest].set(flat_gate[order])
    block_expert = jnp.minimum(
        jnp.searchsorted(padded_end, jnp.arange(n_blocks) * MOE_BLOCK, side='right'), N_EXPERTS - 1)
    x_rows = hf[row_tok].reshape(n_blocks, MOE_BLOCK, D)

    def expert_block(args):
        xb, e = args
        gu = xb @ w_gate_up[e] + b_gate_up[e]
        gate, up = gu[..., :D_FF_EXPERT], gu[..., D_FF_EXPERT:]
        gate = jnp.minimum(gate, SWIGLU_LIMIT)
        up = jnp.clip(up, -SWIGLU_LIMIT, SWIGLU_LIMIT)
        act = (up + 1.0) * gate * jax.nn.sigmoid(SWIGLU_ALPHA * gate)
        return act @ w_down[e] + b_down[e]

    y_rows = lax.map(expert_block, (x_rows, block_expert))
    y = jnp.zeros_like(hf).at[row_tok].add(y_rows.reshape(R, D) * row_gate[:, None])
    return y.reshape(B, S, D)

def setup_inputs(seed: int = 0) -> dict:
    key = jax.random.key(seed)
    ks = jax.random.split(key, 32)
    f32 = jnp.float32
    nrm = lambda k, shape, s: jax.random.normal(k, shape, f32) * s
    gain = lambda k, n: 1.0 + 0.01 * jax.random.normal(k, (DEPTH, n), f32)
    L = DEPTH
    dt = jnp.exp(jax.random.uniform(ks[6], (L, GDN_HEADS), f32, np.log(1e-3), np.log(1e-1)))
    return {
        'x': nrm(ks[0], (BATCH, SEQ, D_MODEL), 1.0),
        'mem': nrm(ks[1], (BATCH, MEM_LEN, D_MODEL), 1.0),
        'norm_mix_g': gain(ks[2], D_MODEL),
        'w_in': nrm(ks[3], (L, D_MODEL, IN_PROJ_WIDTH), D_MODEL ** -0.5),
        'gdn_conv_w': nrm(ks[4], (L, GDN_CONV, 3 * GDN_WIDTH), GDN_CONV ** -0.5),
        'gdn_A_log': jnp.log(jax.random.uniform(ks[5], (L, GDN_HEADS), f32, 1.0, 16.0)),
        'gdn_dt_bias': dt + jnp.log(-jnp.expm1(-dt)),
        'gdn_norm_g': gain(ks[7], GDN_HEAD_DIM),
        'moba_norm_g': gain(ks[8], MOBA_WIDTH),
        'w_out': nrm(ks[9], (L, MIX_WIDTH, D_MODEL), MIX_WIDTH ** -0.5),
        'norm_xattn_g': gain(ks[10], D_MODEL),
        'norm_mem_g': gain(ks[11], D_MODEL),
        'xattn_w_q': nrm(ks[12], (L, D_MODEL, XATTN_WIDTH), D_MODEL ** -0.5),
        'xattn_w_kv': nrm(ks[13], (L, D_MODEL, 2 * XATTN_WIDTH), D_MODEL ** -0.5),
        'xattn_w_o': nrm(ks[14], (L, XATTN_WIDTH, D_MODEL), XATTN_WIDTH ** -0.5),
        'norm_ffn_g': gain(ks[15], D_MODEL),
        'router_w': nrm(ks[16], (L, D_MODEL, N_EXPERTS), D_MODEL ** -0.5),
        'router_b': nrm(ks[17], (L, N_EXPERTS), 0.01),
        'w_gate_up': nrm(ks[18], (L, N_EXPERTS, D_MODEL, 2 * D_FF_EXPERT), D_MODEL ** -0.5),
        'b_gate_up': nrm(ks[19], (L, N_EXPERTS, 2 * D_FF_EXPERT), 0.01),
        'w_down': nrm(ks[20], (L, N_EXPERTS, D_FF_EXPERT, D_MODEL), D_FF_EXPERT ** -0.5),
        'b_down': nrm(ks[21], (L, N_EXPERTS, D_MODEL), 0.01),
        'final_norm_g': 1.0 + 0.01 * jax.random.normal(ks[22], (D_MODEL,), f32),
    }

def reference(x, mem, norm_mix_g, w_in, gdn_conv_w, gdn_A_log, gdn_dt_bias, gdn_norm_g,
              moba_norm_g, w_out, norm_xattn_g, norm_mem_g, xattn_w_q, xattn_w_kv, xattn_w_o,
              norm_ffn_g, router_w, router_b, w_gate_up, b_gate_up, w_down, b_down, final_norm_g):
    for l in range(DEPTH):
        x = x + parallel_mixer(rms_norm(x, norm_mix_g[l]), w_in[l], gdn_conv_w[l], gdn_A_log[l],
                               gdn_dt_bias[l], gdn_norm_g[l], moba_norm_g[l], w_out[l])
        x = x + memory_cross_attention(rms_norm(x, norm_xattn_g[l]), rms_norm(mem, norm_mem_g[l]),
                                       xattn_w_q[l], xattn_w_kv[l], xattn_w_o[l])
        x = x + moe_ffn(rms_norm(x, norm_ffn_g[l]), router_w[l], router_b[l], w_gate_up[l],
                        b_gate_up[l], w_down[l], b_down[l])
    return rms_norm(x, final_norm_g)


_drawn_inputs = setup_inputs


def setup_inputs(seed=0):
    import zlib

    import numpy as np

    out = dict(_drawn_inputs(seed))
    spreads = {}
    factors = {'gdn_norm_g': 5.091,
     'moba_norm_g': 2.737,
     'norm_xattn_g': 8.0,
     'norm_mem_g': 8.0,
     'b_gate_up': 64.0,
     'b_down': 64.0,
     'final_norm_g': 180.434,
     'norm_ffn_g': 8.0,
     'router_b': 27.005}
    for name, (base, spread) in spreads.items():
        noise = np.random.default_rng([zlib.crc32(name.encode()), seed]).standard_normal(out[name].shape)
        drawn = base * np.exp(spread * noise) if base else spread * noise
        out[name] = __import__('jax').numpy.asarray(drawn.astype(out[name].dtype))
    for name, factor in factors.items():
        out[name] = (out[name] * factor).astype(out[name].dtype)
    return out
```

```python
from contextlib import ExitStack

import numpy as np

import concourse.bass as bass
from concourse import mybir

F32 = mybir.dt.float32
BF16 = mybir.dt.bfloat16
I32 = mybir.dt.int32
U32 = mybir.dt.uint32
ALU = mybir.AluOpType
ACT = mybir.ActivationFunctionType
AX = mybir.AxisListType

P = 128
HALF = 64
D_MODEL = 1024
SEQ = 256
TILES = SEQ // P
KB = D_MODEL // P
GH = 4
MH = 8
MHD = 64
CHUNK = 64
LEVELS = 6
E = 32
TOPK = 4
SLOTS = 64
PASSES = SEQ // SLOTS
PAIRS = E // 2
RING = 6
SLOT = 4096
PAIR_CHUNKS = 12
PICKS = PAIRS + 1
EPS = 1e-6
NEG = -1.0e30
LIMIT = 7.0
GATHER_BANK, GATED_BANK, GATE_BANK, UP_BANK, ACT_T_BANK, Y_BANK = (0, 5), 6, (1, 3), (2, 4), (0, 5), 6
COMBINE_BANK = {1: 1, 0: 3}
ALPHA = 1.702

W_ORDER = ["gdn_k", "gdn_q", "gdn_v", "moba_q", "moba_k", "moba_v", "gdn_z", "mem_k", "mem_v",
           "out_a", "out_b", "x_q", "x_o"]
PRE = len(W_ORDER)

ROWS = {"mix": 0, "mem": 8, "xattn": 16, "ffn": 24, "moba": 32, "gdn": 36, "conv": 37}
N_ROWS = 37 + 4 * 12

JOBS = ["const_cols", "x_T0", "x_T1", "mem_T0", "mem_T1", "gdn_k", "gdn_q", "gdn_v", "gdn_ba",
        "moba_q", "moba_k", "moba_v", "tok_k", "tok_q", "tok_v", "gdn_z", "mem_k", "mem_v",
        "cum_g", "row_g", "k_T", "q_T", "kk", "qk", "swap0"]
_MOBA = [f"{s}{h}" for h in range(4) for s in ("score", "probs_T", "pv")]
for _l in range(1, LEVELS):
    for _s in ("swap", "solve_T", "solve"):
        if _l == LEVELS - 1 and _s == "solve":
            continue
        JOBS.append(f"{_s}{_l}")
        if _MOBA:
            JOBS.append(_MOBA.pop(0))
JOBS += _MOBA
JOBS += ["u", "w_T", "state0", "v1", "inter1", "state1", "intra0", "v2", "inter2", "state2", "v3", "inter3",
         "intra1", "moba_oT", "gdn_oT", "mix_out0", "mix_out1",
         "x_hT0", "x_hT1", "x_q", "x_score0", "x_score1", "x_probs_T0", "x_probs_T1", "x_pv", "x_out0", "x_out1",
         "f_T0", "f_T1", "logits", "slots", "count"]
JOB = {name: n for n, name in enumerate(JOBS)}


def bass_hybrid_block(nc, x, mem, norm_mix_g, w_in, gdn_conv_w, gdn_A_log, gdn_dt_bias, gdn_norm_g,
                      moba_norm_g, w_out, norm_xattn_g, norm_mem_g, xattn_w_q, xattn_w_kv, xattn_w_o,
                      norm_ffn_g, router_w, router_b, w_gate_up, b_gate_up, w_down, b_down, final_norm_g, out):
    with ExitStack() as ctx:
        sems = {}

        def S(name):
            if name not in sems:
                sems[name] = ctx.enter_context(nc.semaphore(name))
            return sems[name]

        ring = ctx.enter_context(nc.sbuf_tensor("ring", [P, RING * SLOT], F32))
        work = ctx.enter_context(nc.sbuf_tensor("work", [P, 27136], F32))
        small = ctx.enter_context(nc.sbuf_tensor("small", [P, 1440], F32))

        def area(at, *dims):
            n = int(np.prod(dims))
            v = work[:, at:at + n]
            if len(dims) == 2:
                return v.rearrange("p (a b) -> p a b", b=dims[1])
            if len(dims) == 3:
                return v.rearrange("p (a b c) -> p a b c", b=dims[1], c=dims[2])
            return v

        X, HT, M1, M2, M3, TOK, ZZ = 0, 2048, 4096, 8192, 10240, 13312, 16384
        QKT, MQ, MK, MV, OM, KM, VM, PP, PT = 17408, 18432, 20480, 21504, 22528, 23552, 24576, 25600, 26368
        x_sb = area(X, TILES, D_MODEL)
        hT = area(HT, KB, SEQ)
        oT = area(HT, KB, SEQ)
        mem_sb = area(M1, TILES, D_MODEL)
        memT = area(M1 + 2048, KB, SEQ)
        a_mat = area(M1, 8, P)
        level_l = area(M1 + 1024, 8, P)
        inv = area(M1 + 2048, 8, P)
        inv_T = area(M1 + 3072, 8, P)
        decay_T = area(M1 + 2048, 8, P)
        decay = area(M1 + 3072, 8, P)
        u_sb = area(M1, 8, P)
        w_T = area(M1 + 1024, 8, P)
        square = area(M2, 16, P)
        g_rep = area(M2, 8, P)
        kbg = area(M2, 8, P)
        k_dec = area(M2 + 1024, 8, P)
        xn = area(M3, TILES, D_MODEL)
        conv = area(M3, 12, SEQ)
        k_T = area(M3, 8, P)
        q_T = area(M3 + 1024, 8, P)
        swap = area(M3 + 2048, 8, P)
        g_diff = area(M3 + 2048, 8, P)
        state = area(M3 + 2048, 4, P)
        o_tmp = area(M3 + 2560, 4, P)
        tok = area(TOK, 24, P)
        tok_k, tok_q, tok_v = tok[:, 0:8, :], tok[:, 8:16, :], tok[:, 16:24, :]
        o_gdn = tok_q
        rows = area(ZZ, P)
        z_sb = area(ZZ, 8, P)
        router_sb = area(ZZ, KB, E)
        router_bias = area(ZZ + 256, E)
        qk_T = area(QKT, 8, P)
        mq_z = area(MQ, MH, SEQ)
        mk_T = area(MK, 4, SEQ)
        mv_sb = area(MV, TILES, 512)
        o_moba = area(OM, TILES, 512)
        km_T = area(KM, 4, SEQ)
        vm_sb = area(VM, TILES, 512)
        m_p = area(PP, 2, 384)
        m_pT = area(PT, 2, 384)
        xq_T = area(MK, 4, SEQ)
        x_p = [area(M2, 4, SEQ), area(M2 + 1024, 4, SEQ)]
        x_pT = area(M1, 8, SEQ)
        bias_raw = area(TOK, 3072)
        bias_hi = work[:, M1 + 2048:M1 + 2048 + 1536].bitcast(BF16)
        bias_mid = work[:, PP:PP + 1536].bitcast(BF16)
        split = [work[:, MQ + 1024 * s:MQ + 1024 * s + 1024].bitcast(BF16).rearrange("p (a b) -> p a b", b=D_MODEL)
                 for s in range(3)]
        remainder = area(M2, TILES, D_MODEL)
        xg_T = [area(M3 + 512 * s, KB, SLOTS) for s in range(2)]
        act_T = area(M3 + 1024, 4, P)
        gate_sb = area(M3 + 1536, 512)
        up_sb = area(M3 + 2048, 512)
        sig_sb = area(M3 + 2560, 512)
        y_sb = area(MV, 2, 512)
        g_T = area(MV + 1024, 2, SEQ)
        pick_gated = area(MV + 1536, TILES, 3 * SLOTS)
        pick = [work[:, MV + 1920 + 64 * s:MV + 1984 + 64 * s].bitcast(BF16).rearrange("p (a b) -> p a b", b=SLOTS)
                for s in range(2)]
        choose = work[:, MV + 2048:MV + 2112].bitcast(BF16).rearrange("p (a b) -> p a b", b=SLOTS)
        final_gain = area(HT, D_MODEL)
        out_sb = area(M2, TILES, D_MODEL)
        mem_junk = area(M3, D_MODEL)

        at = [0]

        def tiny(n, dt=F32):
            w = n if dt == F32 or dt == I32 or dt == U32 else (n + 1) // 2
            v = small[:, at[0]:at[0] + w]
            at[0] += w
            return v if dt == F32 else v.bitcast(dt)

        ident = tiny(P)
        cols = tiny(N_ROWS)
        tri = tiny(P)
        causal = tiny(384, BF16).rearrange("p (a b) -> p a b", b=P)
        level_mask = tiny(LEVELS * P, BF16).rearrange("p (a b) -> p a b", b=P)
        w_ba = tiny(64).rearrange("p (a b) -> p a b", b=8)
        iota_s = tiny(SLOTS)
        before = tiny(P, BF16)
        ones = tiny(P, BF16)
        ss, rstd = tiny(TILES), tiny(TILES)
        mem_ss, mem_rstd = tiny(TILES), tiny(TILES)
        sum16, r16 = tiny(16), tiny(16)
        a_log, dt_bias = tiny(GH), tiny(GH)
        beta, g_log, g_cum, e_g, beta_eg, k_decay = (tiny(8) for _ in range(6))
        sp_v, sp_n, sp_e = tiny(8), tiny(8), tiny(8)
        e_last = tiny(16)
        m_max, m_bias, m_sum, m_inv = tiny(4), tiny(4), tiny(16), tiny(16)
        x_max, x_bias, x_sum, x_inv = tiny(8), tiny(8), tiny(8), tiny(8)
        expert_no, part_no = tiny(1), tiny(1)
        part_i = tiny(1, I32)
        count_max, count_i = tiny(1), tiny(1, I32)
        rt = [QKT]

        def routing(*dims):
            n = int(np.prod(dims))
            v = area(rt[0], *dims)
            rt[0] += n
            return v

        logits = routing(TILES, E)
        top8 = routing(TILES, 8)
        top_i = routing(TILES * 8).bitcast(U32).rearrange("p (a b) -> p a b", b=8)
        top_f = routing(TILES, 8)
        top_bias = routing(TILES)
        top_e = routing(TILES, 8)
        top_s = routing(TILES)
        top_w = routing(TILES, 8)
        hit = routing(TILES * TOPK, E)
        gates = routing(TILES, E + 2)
        chosen = routing(TILES, E)
        chosen_b = routing(TILES * E // 2).bitcast(BF16).rearrange("p (a b) -> p a b", b=E)
        slot_m = routing(TILES, E + 2)
        iota_e = routing(E)

        def idx_tiles():
            b = M2
            return (work[:, b:b + 128].bitcast(I32), work[:, b + 128:b + 129].bitcast(I32),
                    work[:, b + 256:b + 384].bitcast(I32), work[:, b + 384:b + 390].bitcast(I32),
                    work[:, b + 400:b + 406].bitcast(I32), area(b + 512, P), area(b + 640, 6), area(b + 650, 6))

        ps = ctx.enter_context(nc.psum_tensor("ps", [P, 4096], F32))

        def bank(b):
            return ps[:, 512 * b:512 * b + 512]

        def pair(name):
            p = JOB[name] % 4
            return ps[:, p * 1024:(p + 1) * 1024]

        def blocks(name):
            return pair(name).rearrange("p (b n) -> p b n", n=P)

        def halves(name):
            return pair(name).rearrange("p (b n) -> p b n", n=512)

        def take(pe, name):
            n = JOB[name]
            if n >= 4:
                pe.wait_ge(S(f"pair_drained{n % 4}"), n // 4)

        def fill_done(ins, name):
            ins.then_inc(S(f"pair_filled{JOB[name] % 4}"), 1)

        def filled(eng, name):
            n = JOB[name]
            eng.wait_ge(S(f"pair_filled{n % 4}"), n // 4 + 1)

        def drain_done(ins, name):
            ins.then_inc(S(f"pair_drained{JOB[name] % 4}"), 1)

        def drained(eng, name):
            n = JOB[name]
            eng.wait_ge(S(f"pair_drained{n % 4}"), n // 4 + 1)

        steps = {}

        def own(eng, ins, name):
            steps[name] = steps.get(name, 0) + 1
            ins.then_inc(S(name), 1)
            eng.wait_ge(S(name), steps[name])

        def spread(v, n):
            return v.unsqueeze(2).to_broadcast([v.shape[0], v.shape[1], n])

        def slot(s):
            return ring[:, s * SLOT:(s + 1) * SLOT]

        def weights(name):
            n = W_ORDER.index(name)
            return slot(n % RING)

        def weights_landed(pe, name):
            n = W_ORDER.index(name)
            pe.wait_ge(S(f"slot_loaded{n % RING}"), 16 * (n // RING + 1))

        def weights_used(ins, name):
            ins.then_inc(S(f"slot_free{W_ORDER.index(name) % RING}"), 1)

        def ring_use(c):
            return (PRE + c) % RING, (PRE + c) // RING

        row = lambda v: v.rearrange("a (b n) -> (a b) n", n=P)
        block = ctx.enter_context(nc.Block())

        @block.sync
        def _(sp):
            wi = w_in[0].rearrange("(k p) n -> p k n", p=P)
            kv = xattn_w_kv[0].rearrange("(k p) n -> p k n", p=P)
            wo = w_out[0].rearrange("(k p) n -> p k n", p=P)
            source = {"moba_q": wi[:, :, 0:512], "moba_k": wi[:, :, 512:1024], "moba_v": wi[:, :, 1024:1536],
                      "gdn_q": wi[:, :, 1536:2048], "gdn_k": wi[:, :, 2048:2560], "gdn_v": wi[:, :, 2560:3072],
                      "gdn_z": wi[:, :, 3072:3584], "mem_k": kv[:, :, 0:512], "mem_v": kv[:, :, 512:1024],
                      "out_a": wo[:, :, 0:512], "out_b": wo[:, :, 512:1024],
                      "x_q": xattn_w_q[0].rearrange("(k p) n -> p k n", p=P),
                      "x_o": xattn_w_o[0].rearrange("(k p) n -> p k n", p=P)}
            for n, name in enumerate(W_ORDER):
                s = n % RING
                if n >= RING:
                    sp.wait_ge(S(f"slot_free{s}"), n // RING)
                src = source[name]
                sp.dma_start(slot(s).rearrange("p (k n) -> p k n", n=src.shape[2]), src) \
                    .then_inc(S(f"slot_loaded{s}"), 16)

            def load_pair(i, before):
                gu = [w_gate_up[0, bass.ds(2 * i + k, 1)].rearrange("e (k p) n -> p (e k) n", p=P) for k in range(2)]
                dn = [w_down[0, bass.ds(2 * i + k, 1)].rearrange("e (k p) n -> p (e k) n", p=P) for k in range(2)]
                for c in range(PAIR_CHUNKS):
                    s, use = ring_use(c)
                    if c < 8:
                        src = gu[c // 4][:, 2 * (c % 4):2 * (c % 4) + 2, :]
                    else:
                        src = dn[(c - 8) // 2][:, 4 * (c % 2):4 * (c % 2) + 4, :]
                    sp.wait_ge(S(f"slot_free{s}"), 2 * before + use)
                    sp.dma_start(slot(s).rearrange("p (k n) -> p k n", n=src.shape[2]), src) \
                        .then_inc(S(f"slot_loaded{s}"), 16)

            with sp.Fori(0, PAIRS) as i:
                load_pair(i, i)
            sp.wait_ge(S("count_ready"), 1)
            most = sp.value_load(count_i[0:1, 0:1], min_val=0, max_val=SEQ)
            with sp.Fori(1, PASSES) as r:
                with sp.If(most > r * SLOTS):
                    with sp.Fori(0, PAIRS) as i:
                        load_pair(i, sp.snap(r * PAIRS + i))
            for t in range(TILES):
                sp.wait_ge(S("out_ready"), t + 1)
                sp.dma_start(out[0, t * P:(t + 1) * P, :], out_sb[:, t, :]).then_inc(S("out_stored"), 16)
            sp.wait_ge(S("out_stored"), 16 * TILES)

        @block.gpsimd
        def _(pool):
            p_row, p_col = idx_tiles()[0:2]
            own(pool, nc.gpsimd.memset(ident, 0.0), "pool_step")
            nc.gpsimd.affine_select(out=ident, in_=ident, compare_op=ALU.not_equal, fill=1.0, base=0,
                                    pattern=[[-1, P]], channel_multiplier=1).then_inc(S("ident_ready"), 1)
            nc.gpsimd.iota(p_row, pattern=[[1, P]], base=0, channel_multiplier=0)
            nc.gpsimd.iota(p_col, pattern=[[0, 1]], base=0, channel_multiplier=1).then_inc(S("indices_ready"), 1)
            own(pool, nc.gpsimd.memset(tri, 1.0), "pool_step")
            own(pool, nc.gpsimd.affine_select(out=tri, in_=tri, compare_op=ALU.is_ge, fill=0.0, base=0,
                                              pattern=[[1, P]], channel_multiplier=-1), "pool_step")
            nc.gpsimd.memset(tri[0:HALF, HALF:P], 0.0).then_inc(S("tri_ready"), 1)
            own(pool, nc.gpsimd.memset(causal, 0.0), "pool_step")
            for b in (0, 2):
                nc.gpsimd.affine_select(out=causal[:, b, :], in_=causal[:, b, :], compare_op=ALU.is_ge,
                                        fill=NEG, base=0, pattern=[[-1, P]], channel_multiplier=1) \
                    .then_inc(S("causal_ready"), 1)
            nc.gpsimd.memset(mq_z, 0.0).then_inc(S("mq_zeroed"), 1)
            nc.gpsimd.iota(iota_s, pattern=[[1, SLOTS]], base=0, channel_multiplier=0,
                           allow_small_or_imprecise_dtypes=True).then_inc(S("iota_ready"), 1)
            own(pool, nc.gpsimd.memset(before, 1.0), "pool_step")
            nc.gpsimd.affine_select(out=before, in_=before, compare_op=ALU.is_gt, fill=0.0, base=0,
                                    pattern=[[1, P]], channel_multiplier=-1).then_inc(S("before_ready"), 1)
            nc.gpsimd.memset(ones, 1.0).then_inc(S("before_ready"), 1)
            drained(pool, "intra1")
            drained(pool, "gdn_oT")
            nc.gpsimd.iota(iota_e, pattern=[[1, E]], base=0, channel_multiplier=0,
                           allow_small_or_imprecise_dtypes=True).then_inc(S("iota_e_ready"), 1)
            pool.wait_ge(S("iota_e_ready"), 1)
            for s in range(3):
                nc.gpsimd.iota(part_no[32 * s:32 * s + 32], pattern=[[0, 1]], base=0, channel_multiplier=1,
                               allow_small_or_imprecise_dtypes=True).then_inc(S("part_no_ready"), 1)
                pool.wait_ge(S("part_no_ready"), s + 1)
            for s in range(3):
                pool.dma_start(bias_raw[32 * s:32 * s + E, 0:2048], b_gate_up[0]).then_inc(S("bias_loaded"), 16)
                pool.dma_start(bias_raw[32 * s:32 * s + E, 2048:3072], b_down[0]).then_inc(S("bias_loaded"), 16)
            pool.wait_ge(S("bias_loaded"), 96)
            own(pool, nc.gpsimd.tensor_copy(bias_hi[0:96, :], bias_raw[0:96, :]), "pool_step")
            for part in (bias_hi, bias_mid):
                own(pool, nc.gpsimd.tensor_tensor(bias_raw[0:96, :], bias_raw[0:96, :], part[0:96, :],
                                                  ALU.subtract), "pool_step")
                if part is bias_hi:
                    own(pool, nc.gpsimd.tensor_copy(bias_mid[0:96, :], bias_raw[0:96, :]), "pool_step")
            own(pool, nc.gpsimd.tensor_copy(bias_hi[32:64, :], bias_mid[32:64, :]), "pool_step")
            nc.gpsimd.tensor_copy(bias_hi[64:96, :], bias_raw[64:96, :]).then_inc(S("biases_ready"), 1)

        @block.scalar
        def _(act):
            for t in range(TILES):
                act.dma_start(x_sb[:, t, :], x[0, t * P:(t + 1) * P, :]).then_inc(S(f"x_loaded{t}"), 16)
            for name, src in (("mix", row(norm_mix_g)), ("mem", row(norm_mem_g)), ("xattn", row(norm_xattn_g)),
                              ("ffn", row(norm_ffn_g)), ("moba", row(moba_norm_g)), ("gdn", gdn_norm_g),
                              ("conv", gdn_conv_w[0].rearrange("j (c p) -> (j c) p", p=P))):
                r = ROWS[name]
                act.dma_start(rows[r:r + src.shape[0], :], src).then_inc(S("rows_loaded"), 16)
            act.dma_start(a_log, gdn_A_log[0].partition_broadcast(P)).then_inc(S("ab_loaded"), 16)
            act.dma_start(dt_bias, gdn_dt_bias[0].partition_broadcast(P)).then_inc(S("ab_loaded"), 16)
            act.dma_start(w_ba, w_in[0, :, 3584:3592].rearrange("(k p) n -> p k n", p=P)) \
                .then_inc(S("w_ba_loaded"), 16)
            for t in range(TILES):
                act.dma_start(mem_sb[:, t, :], mem[0, t * P:(t + 1) * P, :]).then_inc(S(f"mem_loaded{t}"), 16)

            def squares(src, junk, acc, name, n=TILES):
                for t in range(n):
                    nc.scalar.activation(junk[:, t, :] if n > 1 else junk, src[:, t, :], ACT.Square,
                                         accum_out=acc[:, t:t + 1]).then_inc(S(name), 1)

            def root(v, after, count, name):
                act.wait_ge(S(after), count)
                nc.scalar.activation(v, v, ACT.Sqrt).then_inc(S(name), 1)

            def evacuate(name, dst, src):
                filled(act, name)
                drain_done(nc.scalar.copy(dst, src), name)

            for t in range(TILES):
                act.wait_ge(S(f"x_loaded{t}"), 16)
                nc.scalar.activation(xn[:, t, :], x_sb[:, t, :], ACT.Square,
                                     accum_out=ss[:, t:t + 1]).then_inc(S("x_squared"), 1)
            for t in range(TILES):
                act.wait_ge(S(f"mem_loaded{t}"), 16)
                if t == 0:
                    act.wait_ge(S("x_squared"), TILES)
                nc.scalar.activation(tok[:, 8 * t:8 * t + 8, :].rearrange("p a b -> p (a b)"), mem_sb[:, t, :],
                                     ACT.Square, accum_out=mem_ss[:, t:t + 1]).then_inc(S("mem_squared"), 1)
            root(rstd, "x_mean", 1, "x_root")
            root(mem_rstd, "mem_mean", 1, "mem_root")
            act.wait_ge(S("ab_loaded"), 32)
            nc.scalar.activation(a_log, a_log, ACT.Exp).then_inc(S("rate_ready"), 1)
            for n, name in enumerate(("gdn_k", "gdn_q", "gdn_v")):
                drained(act, name)
                c = conv[:, 4 * n:4 * n + 4, :]
                nc.scalar.activation(c, c, ACT.Silu).then_inc(S("conv_silu"), 1)
            filled(act, "gdn_ba")
            ba = pair("gdn_ba").rearrange("p (t n) -> p t n", n=512)
            nc.scalar.activation(beta.rearrange("p (t n) -> p t n", n=GH), ba[:, :, 0:GH], ACT.Sigmoid) \
                .then_inc(S("beta_ready"), 1)
            act.wait_ge(S("softplus_arg"), 1)
            nc.scalar.activation(sp_e, sp_n, ACT.Exp).then_inc(S("softplus_exp"), 1)
            act.wait_ge(S("softplus_sum"), 1)
            nc.scalar.activation(sp_e, sp_e, ACT.Ln).then_inc(S("softplus_ln"), 1)
            filled(act, "moba_q")
            act.wait_ge(S("mq_zeroed"), 1)
            mq4 = mq_z.rearrange("p (b h) n -> p b h n", h=2)
            q4 = pair("moba_q").rearrange("p (b n) -> p b n", n=SEQ)
            nc.scalar.copy(mq4[0:HALF, :, 0, :], q4[0:HALF])
            drain_done(nc.scalar.copy(mq4[HALF:P, :, 1, :], q4[HALF:P]), "moba_q")
            evacuate("moba_k", mk_T, pair("moba_k").rearrange("p (b n) -> p b n", n=SEQ))
            evacuate("moba_v", mv_sb, halves("moba_v"))
            for name, dst in (("tok_k", tok_k), ("tok_q", tok_q), ("tok_v", tok_v)):
                evacuate(name, dst, blocks(name))
            filled(act, "gdn_z")
            drain_done(nc.scalar.activation(z_sb, blocks("gdn_z"), ACT.Silu), "gdn_z")
            evacuate("mem_k", km_T, pair("mem_k").rearrange("p (b n) -> p b n", n=SEQ))
            evacuate("mem_v", vm_sb, halves("mem_v"))
            root(r16, "l2_sums", 1, "l2_root")
            drained(act, "cum_g")
            nc.scalar.activation(e_g, g_cum, ACT.Exp).then_inc(S("e_g_ready"), 1)
            act.wait_ge(S("decay_args"), 1)
            nc.scalar.activation(decay, decay, ACT.Exp, scale=-1.0).then_inc(S("decay_ready"), 1)
            nc.scalar.activation(decay_T, decay_T, ACT.Exp).then_inc(S("decay_ready"), 1)
            nc.scalar.activation(k_decay, k_decay, ACT.Exp).then_inc(S("decay_ready"), 1)
            nc.scalar.activation(e_last, e_last, ACT.Exp).then_inc(S("decay_ready"), 1)
            evacuate("k_T", k_T, blocks("k_T"))
            evacuate("q_T", q_T, blocks("q_T"))

            def moba_probs(hp):
                act.wait_ge(S("moba_bias"), hp + 1)
                for h in range(2):
                    n = 2 * (2 * hp + h)
                    nc.scalar.activation(m_p[:, h, 0:P], m_p[:, h, 0:P], ACT.Exp, bias=m_bias[:, 2 * h:2 * h + 1],
                                         scale=MHD ** -0.5, accum_out=m_sum[:, n:n + 1])
                    last = nc.scalar.activation(m_p[:, h, P:384], m_p[:, h, P:384], ACT.Exp,
                                                bias=m_bias[:, 2 * h + 1:2 * h + 2], scale=MHD ** -0.5,
                                                accum_out=m_sum[:, n + 1:n + 2])
                last.then_inc(S("moba_exp"), 1)

            for name in JOBS[JOB["swap0"] + 1:JOB["u"]]:
                if name.startswith("score"):
                    moba_probs(int(name[-1]))
                elif name.startswith("probs_T"):
                    filled(act, name)
                    drain_done(nc.scalar.copy(m_pT, halves(name)[:, :, 0:384]), name)
                elif name.startswith("swap"):
                    evacuate(name, swap, blocks(name))
            evacuate("u", u_sb, blocks("u"))
            evacuate("w_T", w_T, blocks("w_T"))
            root(ss, "moba_mean", 1, "moba_root")
            evacuate("intra0", o_gdn[:, 0:4, :], blocks("intra0")[:, 0:4, :])
            evacuate("intra1", o_gdn[:, 4:8, :], blocks("intra1")[:, 0:4, :])
            root(r16[:, 0:8], "gdn_mean", 1, "gdn_root")
            act.wait_ge(S("gdn_gated"), 1)
            act.dma_start(router_sb, router_w[0].rearrange("(k p) n -> p k n", p=P)).then_inc(S("router_loaded"), 16)
            act.dma_start(router_bias, router_b[0].partition_broadcast(P)).then_inc(S("router_loaded"), 16)
            for t in range(TILES):
                drained(act, f"mix_out{t}")
            squares(x_sb, xn, ss, "x1_squared")
            root(rstd, "x1_mean", 1, "x1_root")
            evacuate("x_q", xq_T, pair("x_q").rearrange("p (b n) -> p b n", n=SEQ))
            for t in range(TILES):
                act.wait_ge(S("x_bias_ready"), t + 1)
                filled(act, f"x_score{t}")
                sc = pair(f"x_score{t}").rearrange("p (b n) -> p b n", n=SEQ)
                for h in range(GH):
                    last = nc.scalar.activation(x_p[t][:, h, :], sc[:, h, :], ACT.Exp,
                                                bias=x_bias[:, 4 * t + h:4 * t + h + 1], scale=P ** -0.5,
                                                accum_out=x_sum[:, 4 * t + h:4 * t + h + 1])
                drain_done(last, f"x_score{t}")
            evacuate("x_pv", oT[:, 0:4, :], pair("x_pv").rearrange("p (b n) -> p b n", n=SEQ))
            for t in range(TILES):
                drained(act, f"x_out{t}")
            squares(x_sb, xn, ss, "x2_squared")
            root(rstd, "x2_mean", 1, "x2_root")
            act.wait_ge(S("top_bias_ready"), 1)
            for t in range(TILES):
                nc.scalar.activation(top_e[:, t, 0:TOPK], top8[:, t, 0:TOPK], ACT.Exp, bias=top_bias[:, t:t + 1],
                                     accum_out=top_s[:, t:t + 1]).then_inc(S("top_exp"), 1)

            def expert(n, b):
                act.wait_ge(S("gate_clipped"), n)
                nc.scalar.activation(sig_sb, gate_sb, ACT.Sigmoid, scale=ALPHA).then_inc(S("gate_sigmoid"), 1)
                act.wait_ge(S("act_T_filled"), n + 1)
                nc.scalar.copy(act_T, bank(b).rearrange("p (b n) -> p b n", n=P)).then_inc(S("act_T_ready"), 1)

            def expert_pairs(base):
                with act.Fori(0, PAIRS) as i:
                    expert(act.snap(base + 2 * i + 1), ACT_T_BANK[0])
                    expert(act.snap(base + 2 * i + 2), ACT_T_BANK[1])

            expert_pairs(0)
            act.wait_ge(S("count_ready"), 1)
            most = act.value_load(count_i[0:1, 0:1], min_val=0, max_val=SEQ)
            with act.Fori(1, PASSES) as r:
                with act.If(most > r * SLOTS):
                    expert_pairs(r * E)
            act.dma_start(final_gain, final_norm_g.partition_broadcast(P)).then_inc(S("final_gain_loaded"), 16)
            act.wait_ge(S("x_final"), 1)
            squares(x_sb, out_sb, ss, "x3_squared")
            root(rstd, "x3_mean", 1, "x3_root")

        @block.vector
        def _(v):
            def step(ins):
                own(v, ins, "dve_step")

            v.wait_ge(S("indices_ready"), 1)
            p_row, p_col, j_sh, i_sh, i_bit, j_f, i_f, b_f = idx_tiles()
            for l in range(LEVELS):
                nc.vector.tensor_single_scalar(i_sh[:, l:l + 1], p_col, l, ALU.logical_shift_right) \
                    .then_inc(S("dve_step"), 1)
            steps["dve_step"] = LEVELS
            v.wait_ge(S("dve_step"), LEVELS)
            step(nc.vector.tensor_single_scalar(i_bit, i_sh, 1, ALU.bitwise_and))
            nc.vector.tensor_copy(i_f, i_sh)
            step(nc.vector.tensor_copy(b_f, i_bit))
            for l in range(LEVELS):
                step(nc.vector.tensor_single_scalar(j_sh, p_row, l, ALU.logical_shift_right))
                step(nc.vector.tensor_copy(j_f, j_sh))
                step(nc.vector.tensor_scalar(j_f, j_f, i_f[:, l:l + 1], -1.0, ALU.subtract, ALU.is_equal))
                step(nc.vector.tensor_scalar(level_mask[:, l, :], j_f, b_f[:, l:l + 1], None, ALU.mult))

            def mean(acc, dst, n, after, count, name):
                v.wait_ge(S(after), count)
                nc.vector.tensor_scalar(dst, acc, 1.0 / n, EPS, ALU.mult, ALU.add).then_inc(S(name), 1)

            def invert(dst, after, count=1):
                v.wait_ge(S(after), count)
                step(nc.vector.reciprocal(dst, dst))

            def normalise(dst, src, r, name):
                for t in range(TILES):
                    nc.vector.tensor_scalar(dst[:, t, :], src[:, t, :], r[:, t:t + 1], None, ALU.mult) \
                        .then_inc(S(name), 1)

            def gained_T(name, dst, t, gain):
                filled(v, name)
                drain_done(nc.vector.tensor_tensor(
                    dst[:, :, t * P:(t + 1) * P], blocks(name),
                    spread(cols[:, ROWS[gain]:ROWS[gain] + KB], P), ALU.mult), name)

            mean(ss, rstd, D_MODEL, "x_squared", TILES, "x_mean")
            filled(v, "const_cols")
            drain_done(nc.vector.tensor_copy(cols, pair("const_cols")[:, 0:N_ROWS]), "const_cols")
            drained(v, "const_cols")
            invert(rstd, "x_root")
            normalise(xn, x_sb, rstd, "xn_ready")
            mean(mem_ss, mem_rstd, D_MODEL, "mem_squared", TILES, "mem_mean")
            gained_T("x_T0", hT, 0, "mix")
            gained_T("x_T1", hT, 1, "mix")
            invert(mem_rstd, "mem_root")
            normalise(mem_sb, mem_sb, mem_rstd, "memn_ready")
            gained_T("mem_T0", memT, 0, "mem")
            gained_T("mem_T1", memT, 1, "mem")
            for n, name in enumerate(("gdn_k", "gdn_q", "gdn_v")):
                filled(v, name)
                src = pair(name).rearrange("p (b n) -> p b n", n=SEQ)
                for j in (3, 2, 1, 0):
                    back = 3 - j
                    for b in range(4):
                        blk = {"gdn_q": 0, "gdn_k": 4, "gdn_v": 8}[name] + b
                        c = ROWS["conv"] + 12 * j + blk
                        w = cols[:, c:c + 1]
                        dst = conv[:, 4 * n + b, back:SEQ]
                        if j == 3:
                            ins = nc.vector.tensor_scalar(dst, src[:, b, :], w, None, ALU.mult)
                        else:
                            ins = nc.vector.scalar_tensor_tensor(dst, src[:, b, 0:SEQ - back], w, dst,
                                                                 ALU.mult, ALU.add)
                        if b == 3 and j > 0:
                            step(ins)
                        elif b == 3:
                            drain_done(ins, name)
            filled(v, "gdn_ba")
            ba = pair("gdn_ba").rearrange("p (t n) -> p t n", n=512)
            v.wait_ge(S("ab_loaded"), 32)
            v.wait_ge(S("beta_ready"), 1)
            t8 = lambda q: q.rearrange("p (t n) -> p t n", n=GH)
            over_t = lambda q: q.unsqueeze(1).to_broadcast([P, TILES, GH])
            drain_done(nc.vector.tensor_tensor(t8(sp_v), ba[:, :, GH:2 * GH], over_t(dt_bias), ALU.add), "gdn_ba")
            drained(v, "gdn_ba")
            nc.vector.scalar_tensor_tensor(sp_n, sp_v, -1.0, sp_v, ALU.mult, ALU.min).then_inc(S("softplus_arg"), 1)
            v.wait_ge(S("softplus_exp"), 1)
            nc.vector.tensor_scalar(sp_e, sp_e, 1.0, None, ALU.add).then_inc(S("softplus_sum"), 1)
            v.wait_ge(S("softplus_ln"), 1)
            step(nc.vector.scalar_tensor_tensor(sp_v, sp_v, 0.0, sp_e, ALU.max, ALU.add))
            v.wait_ge(S("rate_ready"), 1)
            nc.vector.scalar_tensor_tensor(t8(g_log), t8(sp_v), -1.0, over_t(a_log), ALU.mult, ALU.mult) \
                .then_inc(S("g_ready"), 1)
            v.wait_ge(S("g_ready"), 1)
            drained(v, "tok_k")
            drained(v, "tok_q")
            step(nc.vector.tensor_tensor(square, tok[:, 0:16, :], tok[:, 0:16, :], ALU.mult))
            step(nc.vector.tensor_reduce(sum16, square, AX.X, ALU.add))
            nc.vector.tensor_scalar(r16, sum16, EPS, None, ALU.add).then_inc(S("l2_sums"), 1)
            nc.vector.tensor_copy(g_rep, spread(g_log, P)).then_inc(S("g_rep_ready"), 1)
            filled(v, "cum_g")
            drain_done(nc.vector.tensor_copy(g_cum, pair("cum_g")[:, 0:8]), "cum_g")
            drained(v, "cum_g")
            invert(r16, "l2_root")
            step(nc.vector.tensor_scalar(r16[:, 8:16], r16[:, 8:16], P ** -0.5, None, ALU.mult))
            nc.vector.tensor_tensor(tok[:, 0:16, :], tok[:, 0:16, :], spread(r16, P), ALU.mult) \
                .then_inc(S("qk_normed"), 1)
            filled(v, "row_g")
            rg = blocks("row_g")
            step(nc.vector.tensor_tensor(g_diff, rg, spread(g_cum, P), ALU.subtract))
            nc.vector.tensor_tensor(k_decay[0:HALF].unsqueeze(2), rg[0:HALF, :, HALF - 1:HALF],
                                    g_cum[0:HALF].unsqueeze(2), ALU.subtract)
            nc.vector.tensor_tensor(k_decay[HALF:P].unsqueeze(2), rg[HALF:P, :, P - 1:P],
                                    g_cum[HALF:P].unsqueeze(2), ALU.subtract)
            drain_done(nc.vector.tensor_copy(e_last.rearrange("p (a b) -> p a b", b=2), rg[:, :, HALF - 1:P:HALF]),
                       "row_g")
            drained(v, "row_g")
            nc.vector.tensor_scalar(decay, g_diff, 0.0, None, ALU.max)
            nc.vector.tensor_scalar(decay_T, g_diff, 0.0, None, ALU.min).then_inc(S("decay_args"), 1)
            v.wait_ge(S("e_g_ready"), 1)
            step(nc.vector.tensor_tensor(beta_eg, beta, e_g, ALU.mult))
            v.wait_ge(S("decay_ready"), 4)
            v.wait_ge(S("qk_normed"), 1)
            nc.vector.tensor_tensor(kbg, tok_k, spread(beta_eg, P), ALU.mult).then_inc(S("kbg_ready"), 1)
            nc.vector.tensor_tensor(k_dec, tok_k, spread(k_decay, P), ALU.mult).then_inc(S("k_dec_ready"), 1)
            drained(v, "tok_v")
            nc.vector.tensor_tensor(tok_v, tok_v, spread(beta, P), ALU.mult).then_inc(S("vb_ready"), 1)
            step(nc.vector.tensor_tensor(decay, decay, spread(beta, P), ALU.mult))
            filled(v, "kk")
            drain_done(nc.vector.tensor_tensor(a_mat, blocks("kk"), decay, ALU.mult), "kk")
            drained(v, "kk")
            v.wait_ge(S("tri_ready"), 1)
            step(nc.vector.tensor_tensor(decay_T, decay_T, tri.unsqueeze(1).to_broadcast([P, 8, P]), ALU.mult))
            filled(v, "qk")
            drain_done(nc.vector.tensor_tensor(qk_T, blocks("qk"), decay_T, ALU.mult), "qk")

            def level_part(l):
                nc.vector.tensor_tensor(level_l, a_mat, level_mask[:, l, :].unsqueeze(1).to_broadcast([P, 8, P]),
                                        ALU.mult).then_inc(S("level_ready"), 1)

            drained(v, "qk")
            level_part(0)
            v.wait_ge(S("level_ready"), 1)
            eye = ident.unsqueeze(1).to_broadcast([P, 8, P])
            v.wait_ge(S("ident_ready"), 1)
            nc.vector.tensor_tensor(inv, eye, level_l, ALU.subtract).then_inc(S("solved"), 1)
            filled(v, "swap0")
            drain_done(nc.vector.tensor_tensor(inv_T, eye, blocks("swap0"), ALU.subtract), "swap0")
            v.wait_ge(S("causal_ready"), 2)
            v.wait_ge(S("solved"), 1)
            level_part(1)
            drained(v, "swap0")
            for name in JOBS[JOB["swap0"] + 1:JOB["u"]]:
                n = int(name[-1])
                if name.startswith("solve_T"):
                    filled(v, name)
                    drain_done(nc.vector.tensor_tensor(inv_T, inv_T, blocks(name), ALU.subtract), name)
                    drained(v, name)
                elif name.startswith("solve"):
                    filled(v, name)
                    drain_done(nc.vector.tensor_tensor(inv, inv, blocks(name), ALU.subtract), name)
                    level_part(n + 1)
                    drained(v, name)
                elif name.startswith("score"):
                    filled(v, name)
                    s3 = halves(name)[:, :, 0:384].rearrange("p h (b n) -> p h b n", n=P)
                    p3 = m_p.rearrange("p h (b n) -> p h b n", n=P)
                    if n:
                        drained(v, f"probs_T{n - 1}")
                    for h in range(2):
                        ins = nc.vector.tensor_tensor(p3[:, h], s3[:, h], causal, ALU.add)
                    drain_done(ins, name)
                    drained(v, name)
                    if n:
                        v.wait_ge(S("moba_exp"), n)
                    nc.vector.tensor_reduce(m_max[:, 0:4:2], m_p[:, :, 0:P], AX.X, ALU.max)
                    step(nc.vector.tensor_reduce(m_max[:, 1:4:2], m_p[:, :, P:384], AX.X, ALU.max))
                    nc.vector.tensor_scalar(m_bias, m_max, -(MHD ** -0.5), None, ALU.mult) \
                        .then_inc(S("moba_bias"), 1)
                elif name.startswith("pv"):
                    v.wait_ge(S("moba_exp"), n + 1)
                    step(nc.vector.reciprocal(m_inv[:, 4 * n:4 * n + 4], m_sum[:, 4 * n:4 * n + 4]))
                    filled(v, name)
                    for t in range(TILES):
                        dst = o_moba[:, t, P * n:P * n + P].rearrange("p (h d) -> p h d", d=MHD)
                        src = halves(name)[:, t, 0:P].rearrange("p (h d) -> p h d", d=MHD)
                        ins = nc.vector.tensor_tensor(dst, src, spread(m_inv[:, 4 * n + t:4 * n + 4:2], MHD),
                                                      ALU.mult)
                    drain_done(ins, name)
            drained(v, "pv3")
            sq = m_pT.rearrange("p a b -> p (a b)")[:, 0:512]
            drained(v, "probs_T3")
            for t in range(TILES):
                step(nc.vector.tensor_tensor(sq, o_moba[:, t, :], o_moba[:, t, :], ALU.mult))
                step(nc.vector.tensor_reduce(sum16[:, t:t + 1], sq, AX.X, ALU.add))
            mean(sum16[:, 0:TILES], ss, 512, "dve_step", steps["dve_step"], "moba_mean")

            def new_values(n):
                p = slice(HALF * (n % 2), HALF * (n % 2) + HALF)
                us = u_sb[p, 4 * (n // 2):4 * (n // 2) + 4, :]
                filled(v, f"v{n}")
                drain_done(nc.vector.tensor_tensor(us, us, blocks(f"v{n}")[p, 0:4, :], ALU.subtract), f"v{n}")

            def next_state(n):
                if n:
                    t0 = 4 * (n // 2)
                    el = e_last.rearrange("p (a b) -> p a b", b=2)[:, t0:t0 + 4, n % 2]
                    step(nc.vector.tensor_tensor(state, state, spread(el, P), ALU.mult))
                    filled(v, f"state{n}")
                    drain_done(nc.vector.tensor_tensor(state, state, blocks(f"state{n}")[:, 0:4, :], ALU.add),
                               f"state{n}")
                else:
                    filled(v, "state0")
                    drain_done(nc.vector.tensor_copy(state, blocks("state0")[:, 0:4, :]), "state0")
                drained(v, f"state{n}")

            def inter(n):
                p = slice(HALF * (n % 2), HALF * (n % 2) + HALF)
                t0 = 4 * (n // 2)
                filled(v, f"inter{n}")
                drain_done(nc.vector.tensor_tensor(o_tmp[p], blocks(f"inter{n}")[p, 0:4, :],
                                                   spread(e_g[p, t0:t0 + 4], P), ALU.mult), f"inter{n}")
                drained(v, f"inter{n}")

            def add_inter(n):
                p = slice(HALF * (n % 2), HALF * (n % 2) + HALF)
                t0 = 4 * (n // 2)
                step(nc.vector.tensor_tensor(o_gdn[p, t0:t0 + 4, :], o_gdn[p, t0:t0 + 4, :], o_tmp[p], ALU.add))

            next_state(0)
            drained(v, "u")
            new_values(1)
            inter(1)
            next_state(1)
            drained(v, "intra0")
            add_inter(1)
            new_values(2)
            inter(2)
            next_state(2)
            new_values(3)
            inter(3)
            drained(v, "intra1")
            add_inter(2)
            add_inter(3)
            invert(ss, "moba_root")
            normalise(o_moba, o_moba, ss, "moba_normed")
            step(nc.vector.tensor_tensor(square[:, 0:8, :], o_gdn, o_gdn, ALU.mult))
            step(nc.vector.tensor_reduce(sum16[:, 0:8], square[:, 0:8, :], AX.X, ALU.add))
            nc.vector.tensor_scalar(r16[:, 0:8], sum16[:, 0:8], 1.0 / P, EPS, ALU.mult, ALU.add) \
                .then_inc(S("gdn_mean"), 1)
            drained(v, "gdn_z")
            filled(v, "moba_oT")
            drain_done(nc.vector.tensor_tensor(oT[:, 0:4, :], pair("moba_oT").rearrange("p (b n) -> p b n", n=SEQ),
                                               spread(cols[:, ROWS["moba"]:ROWS["moba"] + 4], SEQ), ALU.mult),
                       "moba_oT")
            invert(r16[:, 0:8], "gdn_root")
            step(nc.vector.tensor_tensor(o_gdn, o_gdn, spread(r16[:, 0:8], P), ALU.mult))
            nc.vector.tensor_tensor(o_gdn, o_gdn, z_sb, ALU.mult).then_inc(S("gdn_gated"), 1)
            filled(v, "gdn_oT")
            drain_done(nc.vector.tensor_scalar(oT[:, 4:8, :], pair("gdn_oT").rearrange("p (b n) -> p b n", n=SEQ),
                                               cols[:, ROWS["gdn"]:ROWS["gdn"] + 1], None, ALU.mult), "gdn_oT")

            def residual(name, t):
                filled(v, name)
                drain_done(nc.vector.tensor_tensor(x_sb[:, t, :], x_sb[:, t, :], pair(name), ALU.add), name)

            for t in range(TILES):
                residual(f"mix_out{t}", t)
            mean(ss, rstd, D_MODEL, "x1_squared", TILES, "x1_mean")
            invert(rstd, "x1_root")
            normalise(xn, x_sb, rstd, "x1_normed")
            for t in range(TILES):
                gained_T(f"x_hT{t}", hT, t, "xattn")
            for t in range(TILES):
                filled(v, f"x_score{t}")
                sc = pair(f"x_score{t}").rearrange("p (b n) -> p b n", n=SEQ)
                step(nc.vector.tensor_reduce(x_max[:, 4 * t:4 * t + 4], sc, AX.X, ALU.max))
                nc.vector.tensor_scalar(x_bias[:, 4 * t:4 * t + 4], x_max[:, 4 * t:4 * t + 4], -(P ** -0.5), None,
                                        ALU.mult).then_inc(S("x_bias_ready"), 1)
            for t in range(TILES):
                drained(v, f"x_score{t}")
                step(nc.vector.reciprocal(x_inv[:, 4 * t:4 * t + 4], x_sum[:, 4 * t:4 * t + 4]))
                nc.vector.tensor_tensor(x_p[t], x_p[t], spread(x_inv[:, 4 * t:4 * t + 4], SEQ), ALU.mult) \
                    .then_inc(S("x_probs_ready"), 1)
            for t in range(TILES):
                filled(v, f"x_probs_T{t}")
                drain_done(nc.vector.tensor_copy(x_pT[:, :, t * P:(t + 1) * P], blocks(f"x_probs_T{t}")),
                           f"x_probs_T{t}")
            for t in range(TILES):
                residual(f"x_out{t}", t)
            mean(ss, rstd, D_MODEL, "x2_squared", TILES, "x2_mean")
            invert(rstd, "x2_root")
            normalise(xn, x_sb, rstd, "x2_normed")
            for t in range(TILES):
                gained_T(f"f_T{t}", hT, t, "ffn")
            v.wait_ge(S("x2_normed"), TILES)
            step(nc.vector.tensor_copy(split[0], xn))
            step(nc.vector.tensor_tensor(remainder, xn, split[0], ALU.subtract))
            step(nc.vector.tensor_copy(split[1], remainder))
            step(nc.vector.tensor_tensor(split[2], remainder, split[1], ALU.subtract))
            v.wait_ge(S("router_loaded"), 32)
            v.wait_ge(S("iota_e_ready"), 1)
            filled(v, "logits")
            drain_done(nc.vector.tensor_tensor(logits, pair("logits")[:, 0:TILES * E].rearrange(
                "p (t e) -> p t e", e=E), router_bias.unsqueeze(1).to_broadcast([P, TILES, E]), ALU.add), "logits")
            drained(v, "logits")
            for t in range(TILES):
                step(nc.vector.max(top8[:, t, :], logits[:, t, :]))
                step(nc.vector.max_index(top_i[:, t, :], top8[:, t, :], logits[:, t, :]))
            nc.vector.tensor_scalar(top_bias, top8[:, :, 0], -1.0, None, ALU.mult).then_inc(S("top_bias_ready"), 1)
            step(nc.vector.tensor_copy(top_f, top_i))
            for t in range(TILES):
                for j in range(TOPK):
                    ins = nc.vector.tensor_scalar(hit[:, TOPK * t + j, :], iota_e, top_f[:, t, j:j + 1], None,
                                                  ALU.is_equal)
            step(ins)
            h4 = hit.rearrange("p (t j) e -> p t j e", j=TOPK)
            step(nc.vector.tensor_tensor(chosen, h4[:, :, 0, :], h4[:, :, 1, :], ALU.add))
            step(nc.vector.tensor_tensor(chosen, chosen, h4[:, :, 2, :], ALU.add))
            step(nc.vector.tensor_tensor(chosen, chosen, h4[:, :, 3, :], ALU.add))
            nc.vector.tensor_copy(chosen_b, chosen).then_inc(S("chosen_ready"), 1)
            v.wait_ge(S("top_exp"), TILES)
            step(nc.vector.reciprocal(top_s, top_s))
            step(nc.vector.tensor_tensor(top_w[:, :, 0:TOPK], top_e[:, :, 0:TOPK], spread(top_s, TOPK), ALU.mult))
            for t in range(TILES):
                step(nc.vector.tensor_scalar(gates[:, t, 0:E], hit[:, TOPK * t, :], top_w[:, t, 0:1], None, ALU.mult))
                for j in range(1, TOPK):
                    step(nc.vector.scalar_tensor_tensor(gates[:, t, 0:E], hit[:, TOPK * t + j, :],
                                                        top_w[:, t, j:j + 1], gates[:, t, 0:E], ALU.mult, ALU.add))
            step(nc.vector.memset(gates[:, :, E:E + 2], 0.0))
            step(nc.vector.memset(slot_m[:, :, E:E + 2], 0.0))
            filled(v, "slots")
            drain_done(nc.vector.scalar_tensor_tensor(
                slot_m[:, :, 0:E], pair("slots")[:, 0:TILES * E].rearrange("p (t e) -> p t e", e=E), 1.0, chosen,
                ALU.add, ALU.mult), "slots")
            drained(v, "slots")
            step(nc.vector.tensor_scalar(slot_m, slot_m, 1.0, None, ALU.subtract))
            filled(v, "count")
            drain_done(nc.vector.tensor_reduce(count_max, pair("count")[:, 0:E], AX.X, ALU.max), "count")
            drained(v, "count")
            nc.vector.tensor_copy(count_i, count_max).then_inc(S("count_ready"), 1)
            v.wait_ge(S("count_ready"), 1)
            v.wait_ge(S("part_no_ready"), 3)
            v.wait_ge(S("iota_ready"), 1)

            def pick_pair(i):
                for k in range(2):
                    for t in range(TILES):
                        ins = nc.vector.tensor_scalar(pick[k][:, t, :], iota_s, slot_m[:, t, bass.ds(2 * i + k, 1)],
                                                      None, ALU.is_equal)
                ins.then_inc(S("picked"), 1)
                for t in range(TILES):
                    for q, k in enumerate((0, 1, 0)):
                        ins = nc.vector.tensor_scalar(
                            pick_gated[:, t, SLOTS * q:SLOTS * q + SLOTS], iota_s,
                            slot_m[:, t, bass.ds(2 * i + k, 1)], gates[:, t, bass.ds(2 * i + k, 1)],
                            ALU.is_equal, ALU.mult)
                ins.then_inc(S("gated_picked"), 1)

            def choose_pair(done):
                for k in range(2):
                    nc.vector.tensor_scalar(choose[0:96, k, :], part_no[0:96].to_broadcast([96, SLOTS]),
                                            expert_no[0:96], float(k), ALU.subtract, ALU.is_equal) \
                        .then_inc(S("expert_chosen"), 1)
                nc.vector.tensor_scalar(expert_no[0:96], expert_no[0:96], 2.0, None, ALU.add) \
                    .then_inc(S("expert_stepped"), 1)

            def gathered(k, n):
                v.wait_ge(S("gather_filled"), n)
                nc.vector.tensor_tensor(xg_T[k], bank(GATHER_BANK[k]).rearrange("p (b n) -> p b n", n=SLOTS),
                                        spread(cols[:, ROWS["ffn"]:ROWS["ffn"] + KB], SLOTS), ALU.mult) \
                    .then_inc(S("gathered"), 1)

            def swiglu(k, n):
                v.wait_ge(S("gate_up_filled"), n)
                v.wait_ge(S("act_T_filled"), n)
                nc.vector.tensor_scalar(gate_sb, bank(GATE_BANK[k]), LIMIT, None, ALU.min) \
                    .then_inc(S("gate_clipped"), 1)
                nc.vector.tensor_scalar(up_sb, bank(UP_BANK[k]), LIMIT, -LIMIT, ALU.min, ALU.max) \
                    .then_inc(S("up_clipped"), 1)
                v.wait_ge(S("gate_clipped"), n)
                v.wait_ge(S("up_clipped"), n)
                nc.vector.scalar_tensor_tensor(up_sb, up_sb, 1.0, gate_sb, ALU.add, ALU.mult) \
                    .then_inc(S("up_gated"), 1)
                v.wait_ge(S("up_gated"), n)
                v.wait_ge(S("gate_sigmoid"), n)
                nc.vector.tensor_tensor(up_sb, up_sb, sig_sb, ALU.mult).then_inc(S("act_ready"), 1)

            def expert_pass(r):
                first = 2 * PICKS * r
                nc.vector.memset(expert_no[0:96], 0.0).then_inc(S("expert_reset"), 1)
                v.wait_ge(S("expert_reset"), r + 1)
                v.wait_ge(S("slots_moved"), r)
                pick_pair(0)
                choose_pair(0)
                gathered(0, v.snap(first + 1))
                gathered(1, v.snap(first + 2))
                with v.Fori(0, PAIRS) as i:
                    n = v.snap(r * E + 2 * i + 1)
                    m = v.snap(r * E + 2 * i + 2)
                    before = v.snap(r * PAIRS + i)
                    v.wait_ge(S("gated_T_filled"), before + 1)
                    nc.vector.tensor_copy(g_T, bank(GATED_BANK).rearrange("p (a b) -> p a b", b=SEQ)) \
                        .then_inc(S("gated_T_ready"), 1)
                    swiglu(0, n)
                    swiglu(1, m)
                    pick_pair(i + 1)
                    v.wait_ge(S("down_filled"), m)
                    nc.vector.tensor_copy(y_sb, ps[:, 512 * Y_BANK:512 * Y_BANK + 1024].rearrange(
                        "p (a b) -> p a b", b=512)).then_inc(S("y_ready"), 1)
                    v.wait_ge(S("expert_stepped"), PICKS * r + i + 1)
                    choose_pair(i + 1)
                    gathered(0, v.snap(first + 2 * i + 3))
                    gathered(1, v.snap(first + 2 * i + 4))
                    for k, t in enumerate((1, 0)):
                        v.wait_ge(S("combine_filled"), 2 * before + k + 1)
                        b = COMBINE_BANK[t]
                        nc.vector.tensor_tensor(x_sb[:, t, :], x_sb[:, t, :], ps[:, 512 * b:512 * b + 1024],
                                                ALU.add).then_inc(S("combined"), 1)
                        v.wait_ge(S("combined"), 2 * before + k + 2)
                nc.vector.tensor_scalar(slot_m, slot_m, float(SLOTS), None, ALU.subtract) \
                    .then_inc(S("slots_moved"), 1)

            v.sem_inc(S("y_ready"), 1)
            v.sem_inc(S("combined"), 1)
            expert_pass(0)
            most = v.value_load(count_i[0:1, 0:1], min_val=0, max_val=SEQ)
            with v.Fori(1, PASSES) as r:
                with v.If(most > r * SLOTS):
                    expert_pass(r)
            nc.vector.memset(count_max, 0.0).then_inc(S("x_final"), 1)
            mean(ss, rstd, D_MODEL, "x3_squared", TILES, "x3_mean")
            invert(rstd, "x3_root")
            v.wait_ge(S("final_gain_loaded"), 16)
            for t in range(TILES):
                nc.vector.scalar_tensor_tensor(out_sb[:, t, :], x_sb[:, t, :], rstd[:, t:t + 1], final_gain,
                                               ALU.mult, ALU.mult).then_inc(S("out_ready"), 1)

        @block.tensor
        def _(pe):
            def turn(name, dst, src, n_in=P):
                return nc.tensor.transpose(dst, src, ident[0:n_in, 0:n_in])

            def turn_tokens(name, src, after, count):
                take(pe, name)
                pe.wait_ge(S(after), count)
                t = int(name[-1])
                for k in range(KB):
                    last = turn(name, blocks(name)[:, k, :], src[:, t, k * P:(k + 1) * P])
                fill_done(last, name)

            def project_T(name, moving):
                take(pe, name)
                weights_landed(pe, name)
                w = weights(name).rearrange("p (k n) -> p k n", n=512)
                for b in range(4):
                    for k in range(KB):
                        last = nc.tensor.matmul(pair(name)[:, SEQ * b:SEQ * b + SEQ], w[:, k, b * P:(b + 1) * P],
                                                moving[:, k, :], start=(k == 0), stop=(k == KB - 1))
                return last

            def project(name, still):
                take(pe, name)
                weights_landed(pe, name)
                w = weights(name).rearrange("p (k n) -> p k n", n=512)
                for t in range(TILES):
                    for k in range(KB):
                        last = nc.tensor.matmul(halves(name)[:, t, :], still[:, k, t * P:(t + 1) * P], w[:, k, :],
                                                start=(k == 0), stop=(k == KB - 1))
                return last

            pe.wait_ge(S("ident_ready"), 1)
            take(pe, "const_cols")
            pe.wait_ge(S("rows_loaded"), 16 * len(ROWS))
            fill_done(turn("const_cols", pair("const_cols")[:, 0:N_ROWS], rows[0:N_ROWS, :], N_ROWS), "const_cols")
            for t in range(TILES):
                turn_tokens(f"x_T{t}", xn, "xn_ready", TILES)
            for t in range(TILES):
                turn_tokens(f"mem_T{t}", mem_sb, "memn_ready", TILES)

            def projection(name, form, operand):
                last = form(name, operand)
                fill_done(last, name)
                pe.wait_ge(S(f"pair_filled{JOB[name] % 4}"), JOB[name] // 4 + 1)
                pe.sem_inc(S(f"slot_free{W_ORDER.index(name) % RING}"), 1)

            for t in range(TILES):
                drained(pe, f"x_T{t}")
            for name in ("gdn_k", "gdn_q", "gdn_v"):
                projection(name, project_T, hT)
            take(pe, "gdn_ba")
            pe.wait_ge(S("w_ba_loaded"), 16)
            for t in range(TILES):
                for k in range(KB):
                    last = nc.tensor.matmul(halves("gdn_ba")[:, t, 0:8], hT[:, k, t * P:(t + 1) * P], w_ba[:, k, :],
                                            start=(k == 0), stop=(k == KB - 1))
            fill_done(last, "gdn_ba")
            projection("moba_q", project_T, hT)
            projection("moba_k", project_T, hT)
            projection("moba_v", project, hT)
            for n, name in enumerate(("tok_k", "tok_q", "tok_v")):
                take(pe, name)
                pe.wait_ge(S("conv_silu"), n + 1)
                for t in range(TILES):
                    for h in range(GH):
                        last = turn(name, blocks(name)[:, 4 * t + h, :], conv[:, 4 * n + h, t * P:(t + 1) * P])
                fill_done(last, name)
            projection("gdn_z", project, hT)
            for t in range(TILES):
                drained(pe, f"mem_T{t}")
            projection("mem_k", project_T, memT)
            projection("mem_v", project, memT)
            pe.wait_ge(S("tri_ready"), 1)
            take(pe, "cum_g")
            pe.wait_ge(S("g_ready"), 1)
            fill_done(nc.tensor.matmul(pair("cum_g")[:, 0:8], tri, g_log, start=True, stop=True), "cum_g")

            def eight(name, product, n=8):
                take(pe, name)
                for b in range(n):
                    last = product(b, blocks(name)[:, b, :])
                fill_done(last, name)

            def mm(dst, still, moving):
                return nc.tensor.matmul(dst, still, moving, start=True, stop=True)

            pe.wait_ge(S("g_rep_ready"), 1)
            eight("row_g", lambda b, dst: mm(dst, g_rep[:, b, :], tri))
            pe.wait_ge(S("qk_normed"), 1)
            eight("k_T", lambda b, dst: turn("k_T", dst, tok_k[:, b, :]))
            eight("q_T", lambda b, dst: turn("q_T", dst, tok_q[:, b, :]))
            drained(pe, "k_T")
            eight("kk", lambda b, dst: mm(dst, k_T[:, b, :], k_T[:, b, :]))
            drained(pe, "q_T")
            eight("qk", lambda b, dst: mm(dst, k_T[:, b, :], q_T[:, b, :]))
            pe.wait_ge(S("level_ready"), 1)
            eight("swap0", lambda b, dst: mm(dst, level_l[:, b, :], ident))
            for name in JOBS[JOB["swap0"] + 1:JOB["u"]]:
                n = int(name[-1])
                if name.startswith("swap"):
                    pe.wait_ge(S("level_ready"), n + 1)
                    drained(pe, "swap0" if n == 1 else f"solve_T{n - 1}")
                    eight(name, lambda b, dst: mm(dst, level_l[:, b, :], inv_T[:, b, :]))
                elif name.startswith("solve_T"):
                    drained(pe, f"swap{n}")
                    if n == 1:
                        pe.wait_ge(S("solved"), 1)
                    else:
                        drained(pe, f"solve{n - 1}")
                    eight(name, lambda b, dst: mm(dst, inv[:, b, :], swap[:, b, :]))
                elif name.startswith("solve"):
                    eight(name, lambda b, dst: mm(dst, swap[:, b, :], inv[:, b, :]))
                elif name.startswith("score"):
                    take(pe, name)
                    if n == 0:
                        drained(pe, "moba_q")
                        drained(pe, "moba_k")
                    for h in range(2):
                        q = mq_z[:, 2 * n + h, :]
                        mm(halves(name)[:, h, 0:P], q[:, 0:P], mk_T[:, n, 0:P])
                        last = mm(halves(name)[:, h, P:384], q[:, P:SEQ], mk_T[:, n, :])
                    fill_done(last, name)
                elif name.startswith("probs_T"):
                    take(pe, name)
                    pe.wait_ge(S("moba_exp"), n + 1)
                    for h in range(2):
                        for b in range(3):
                            last = turn(name, halves(name)[:, h, P * b:P * b + P], m_p[:, h, P * b:P * b + P])
                    fill_done(last, name)
                else:
                    take(pe, name)
                    drained(pe, f"probs_T{n}")
                    if n == 0:
                        drained(pe, "moba_v")
                    for h in range(2):
                        c = MHD * (2 * n + h)
                        o = slice(MHD * h, MHD * h + MHD)
                        mm(halves(name)[:, 0, o], m_pT[:, h, 0:P], mv_sb[:, 0, c:c + MHD])
                        nc.tensor.matmul(halves(name)[:, 1, o], m_pT[:, h, P:2 * P], mv_sb[:, 0, c:c + MHD],
                                         start=True, stop=False)
                        last = nc.tensor.matmul(halves(name)[:, 1, o], m_pT[:, h, 2 * P:384],
                                                mv_sb[:, 1, c:c + MHD], start=False, stop=True)
                    fill_done(last, name)
            drained(pe, f"solve_T{LEVELS - 1}")
            pe.wait_ge(S("vb_ready"), 1)
            pe.wait_ge(S("kbg_ready"), 1)
            eight("u", lambda b, dst: mm(dst, inv_T[:, b, :], tok_v[:, b, :]))
            eight("w_T", lambda b, dst: mm(dst, kbg[:, b, :], inv_T[:, b, :]))
            pe.wait_ge(S("k_dec_ready"), 1)

            def part(n):
                return slice(HALF * (n % 2), HALF * (n % 2) + HALF), 4 * (n // 2)

            def chunk_state(n):
                p, t0 = part(n)
                drained(pe, "u" if n == 0 else f"v{n}")
                eight(f"state{n}", lambda b, dst: mm(dst, k_dec[p, t0 + b, :], u_sb[p, t0 + b, :]), GH)

            def chunk_reads(n):
                p, t0 = part(n)
                drained(pe, f"state{n - 1}")
                eight(f"v{n}", lambda b, dst: mm(dst[p], w_T[:, t0 + b, p], state[:, b, :]), GH)
                eight(f"inter{n}", lambda b, dst: mm(dst[p], q_T[:, t0 + b, p], state[:, b, :]), GH)

            def intra(tile):
                drained(pe, f"v{2 * tile + 1}")
                eight(f"intra{tile}", lambda b, dst: mm(dst, qk_T[:, 4 * tile + b, :], u_sb[:, 4 * tile + b, :]), GH)

            chunk_state(0)
            drained(pe, "w_T")
            chunk_reads(1)
            chunk_state(1)
            intra(0)
            chunk_reads(2)
            chunk_state(2)
            chunk_reads(3)
            intra(1)

            def turn_out(name, src):
                take(pe, name)
                for b in range(4):
                    for t in range(TILES):
                        last = turn(name, pair(name)[:, SEQ * b + t * P:SEQ * b + (t + 1) * P], src(b, t))
                fill_done(last, name)

            pe.wait_ge(S("moba_normed"), TILES)
            turn_out("moba_oT", lambda b, t: o_moba[:, t, b * P:(b + 1) * P])
            pe.wait_ge(S("gdn_gated"), 1)
            turn_out("gdn_oT", lambda b, t: o_gdn[:, 4 * t + b, :])
            drained(pe, "moba_oT")
            drained(pe, "gdn_oT")
            weights_landed(pe, "out_a")
            weights_landed(pe, "out_b")
            for t in range(TILES):
                name = f"mix_out{t}"
                take(pe, name)
                for half, w in enumerate(("out_a", "out_b")):
                    wv = weights(w).rearrange("p (k n) -> p k n", n=512)
                    for k in range(KB):
                        last = nc.tensor.matmul(halves(name)[:, half, :], oT[:, k, t * P:(t + 1) * P], wv[:, k, :],
                                                start=(k == 0), stop=(k == KB - 1))
                fill_done(last, name)
            filled(pe, "mix_out1")
            for w in ("out_a", "out_b"):
                pe.sem_inc(S(f"slot_free{W_ORDER.index(w) % RING}"), 1)
            for t in range(TILES):
                turn_tokens(f"x_hT{t}", xn, "x1_normed", TILES)
            for t in range(TILES):
                drained(pe, f"x_hT{t}")
            projection("x_q", project_T, hT)
            drained(pe, "mem_k")
            drained(pe, "x_q")
            for t in range(TILES):
                name = f"x_score{t}"
                take(pe, name)
                for h in range(GH):
                    last = mm(pair(name)[:, SEQ * h:SEQ * h + SEQ], xq_T[:, h, t * P:(t + 1) * P], km_T[:, h, :])
                fill_done(last, name)
            for t in range(TILES):
                name = f"x_probs_T{t}"
                take(pe, name)
                pe.wait_ge(S("x_probs_ready"), t + 1)
                for h in range(GH):
                    for mt in range(TILES):
                        last = turn(name, blocks(name)[:, 2 * h + mt, :], x_p[t][:, h, mt * P:(mt + 1) * P])
                fill_done(last, name)
            take(pe, "x_pv")
            drained(pe, "mem_v")
            for t in range(TILES):
                drained(pe, f"x_probs_T{t}")
            for h in range(GH):
                for mt in range(TILES):
                    last = nc.tensor.matmul(pair("x_pv")[:, SEQ * h:SEQ * h + SEQ], vm_sb[:, mt, h * P:(h + 1) * P],
                                            x_pT[:, 2 * h + mt, :], start=(mt == 0), stop=(mt == TILES - 1))
            fill_done(last, "x_pv")
            drained(pe, "x_pv")
            weights_landed(pe, "x_o")
            wv = weights("x_o").rearrange("p (k n) -> p k n", n=D_MODEL)
            for t in range(TILES):
                name = f"x_out{t}"
                take(pe, name)
                for half in range(2):
                    for h in range(GH):
                        last = nc.tensor.matmul(halves(name)[:, half, :], oT[:, h, t * P:(t + 1) * P],
                                                wv[:, h, 512 * half:512 * half + 512],
                                                start=(h == 0), stop=(h == GH - 1))
                fill_done(last, name)
            filled(pe, "x_out1")
            pe.sem_inc(S(f"slot_free{W_ORDER.index('x_o') % RING}"), 1)
            for t in range(TILES):
                turn_tokens(f"f_T{t}", xn, "x2_normed", TILES)
            take(pe, "logits")
            pe.wait_ge(S("router_loaded"), 32)
            for t in range(TILES):
                drained(pe, f"f_T{t}")
            for t in range(TILES):
                for k in range(KB):
                    last = nc.tensor.matmul(pair("logits")[:, E * t:E * t + E], hT[:, k, t * P:(t + 1) * P],
                                            router_sb[:, k, :], start=(k == 0), stop=(k == KB - 1))
            fill_done(last, "logits")
            pe.wait_ge(S("before_ready"), 2)
            pe.wait_ge(S("chosen_ready"), 1)
            take(pe, "slots")
            mm(pair("slots")[:, 0:E], before, chosen_b[:, 0, :])
            nc.tensor.matmul(pair("slots")[:, E:2 * E], ones, chosen_b[:, 0, :], start=True, stop=False)
            fill_done(nc.tensor.matmul(pair("slots")[:, E:2 * E], before, chosen_b[:, 1, :],
                                       start=False, stop=True), "slots")
            take(pe, "count")
            for t in range(TILES):
                last = nc.tensor.matmul(pair("count")[:, 0:E], ones, chosen_b[:, t, :],
                                        start=(t == 0), stop=(t == TILES - 1))
            fill_done(last, "count")
            for name in JOBS[-4:]:
                drained(pe, name)
            pe.wait_ge(S("biases_ready"), 1)

            def gather(k, n):
                dst = bank(GATHER_BANK[k])
                for b in range(KB):
                    for s in range(3):
                        for t in range(TILES):
                            last = nc.tensor.matmul(dst[:, SLOTS * b:SLOTS * b + SLOTS],
                                                    split[s][:, t, b * P:(b + 1) * P], pick[k][:, t, :],
                                                    start=(s == 0 and t == 0), stop=(s == 2 and t == TILES - 1))
                last.then_inc(S("gather_filled"), 1)

            low, high = slice(0, HALF), slice(HALF, P)

            def gate_up(k, before):
                for c in range(4):
                    s, use = ring_use(4 * k + c)
                    pe.wait_ge(S(f"slot_loaded{s}"), 32 * before + 16 * (use + 1))
                    w = slot(s).rearrange("p (k n) -> p k n", n=2 * D_MODEL)
                    for kk in range(2):
                        kb = 2 * c + kk
                        for q, (b, p) in enumerate(((GATE_BANK[k], low), (GATE_BANK[k], high),
                                                    (UP_BANK[k], low), (UP_BANK[k], high))):
                            last = nc.tensor.matmul(bank(b)[p], xg_T[k][:, kb, :], w[:, kk, 512 * q:512 * q + 512],
                                                    start=(kb == 0), stop=False)
                    last.then_inc(S(f"slot_free{s}"), 1)
                for q, (b, p) in enumerate(((GATE_BANK[k], low), (GATE_BANK[k], high),
                                            (UP_BANK[k], low), (UP_BANK[k], high))):
                    last = nc.tensor.matmul(bank(b)[p], choose[0:96, k, :], bias_hi[0:96, 512 * q:512 * q + 512],
                                            start=False, stop=True)
                last.then_inc(S("gate_up_filled"), 1)

            def act_turned(k, n):
                pe.wait_ge(S("act_ready"), n)
                for b in range(4):
                    last = turn("", bank(ACT_T_BANK[k])[:, P * b:P * b + P], up_sb[:, P * b:P * b + P])
                last.then_inc(S("act_T_filled"), 1)

            def down(k, n, before):
                pe.wait_ge(S("act_T_ready"), n)
                places = ((0, low), (1, high)) if k == 0 else ((0, high), (1, low))
                for c in range(2):
                    s, use = ring_use(8 + 2 * k + c)
                    pe.wait_ge(S(f"slot_loaded{s}"), 32 * before + 16 * (use + 1))
                    w = slot(s).rearrange("p (k n) -> p k n", n=D_MODEL)
                    for b in range(4):
                        for q, (y, p) in enumerate(places):
                            last = nc.tensor.matmul(bank(Y_BANK + y)[p], act_T[:, b, HALF * c:HALF * c + HALF],
                                                    w[:, b, 512 * q:512 * q + 512],
                                                    start=(c == 0 and b == 0), stop=False)
                    last.then_inc(S(f"slot_free{s}"), 1)
                for q, (y, p) in enumerate(places):
                    last = nc.tensor.matmul(bank(Y_BANK + y)[p], choose[0:96, k, :],
                                            bias_hi[0:96, 2048 + 512 * q:2560 + 512 * q], start=False, stop=True)
                last.then_inc(S("down_filled"), 1)

            def expert_pass(r):
                pe.wait_ge(S("picked"), PICKS * r + 1)
                gather(0, 0)
                gather(1, 0)
                with pe.Fori(0, PAIRS) as i:
                    before = pe.snap(r * PAIRS + i)
                    n = pe.snap(r * E + 2 * i + 1)
                    m = pe.snap(r * E + 2 * i + 2)
                    pe.wait_ge(S("gated_picked"), PICKS * r + i + 1)
                    pe.wait_ge(S("y_ready"), before + 1)
                    for o in range(2):
                        for t in range(TILES):
                            last = turn("", bank(GATED_BANK)[:, SEQ * o + P * t:SEQ * o + P * t + P],
                                        pick_gated[:, t, HALF * o:HALF * o + P])
                    last.then_inc(S("gated_T_filled"), 1)
                    pe.wait_ge(S("gathered"), 2 * PICKS * r + 2 * i + 1)
                    pe.wait_ge(S("expert_chosen"), 2 * PICKS * r + 2 * i + 2)
                    pe.wait_ge(S("combined"), 2 * before + 1)
                    gate_up(0, before)
                    pe.wait_ge(S("gathered"), 2 * PICKS * r + 2 * i + 2)
                    gate_up(1, before)
                    act_turned(0, n)
                    pe.wait_ge(S("gated_T_ready"), before + 1)
                    down(0, n, before)
                    act_turned(1, m)
                    down(1, m, before)
                    pe.wait_ge(S("picked"), PICKS * r + i + 2)
                    gather(0, 0)
                    gather(1, 0)
                    pe.wait_ge(S("y_ready"), before + 2)
                    for t in (1, 0):
                        b = COMBINE_BANK[t]
                        for q in range(2):
                            last = nc.tensor.matmul(bank(b + q), g_T[:, q, P * t:P * t + P], y_sb[:, q, :],
                                                    start=True, stop=True)
                        last.then_inc(S("combine_filled"), 1)

            pe.sem_inc(S("act_T_filled"), 1)
            expert_pass(0)
            pe.wait_ge(S("count_ready"), 1)
            most = pe.value_load(count_i[0:1, 0:1], min_val=0, max_val=SEQ)
            with pe.Fori(1, PASSES) as r:
                with pe.If(most > r * SLOTS):
                    expert_pass(r)


_INS = ["x", "mem", "norm_mix_g", "w_in", "gdn_conv_w", "gdn_A_log", "gdn_dt_bias", "gdn_norm_g", "moba_norm_g",
        "w_out", "norm_xattn_g", "norm_mem_g", "xattn_w_q", "xattn_w_kv", "xattn_w_o", "norm_ffn_g", "router_w",
        "router_b", "w_gate_up", "b_gate_up", "w_down", "b_down", "final_norm_g"]
_OUTS = [((1, SEQ, D_MODEL), "float32")]


def kernel(**inputs):
    import concourse.bacc as bacc
    from concourse.bass_utils import run_bass_kernel_spmd

    nc = bacc.Bacc("TRN2", target_bir_lowering=False, num_devices=1)
    arrays, args = {}, []
    for name in _INS:
        a = np.ascontiguousarray(inputs[name])
        arrays[f"in_{name}"] = a
        args.append(nc.dram_tensor(f"in_{name}", a.shape, mybir.dt.from_np(a.dtype), kind="ExternalInput").ap())
    for i, (shape, dtype) in enumerate(_OUTS):
        args.append(nc.dram_tensor(f"out_{i}", shape, mybir.dt.from_np(np.dtype(dtype)), kind="ExternalOutput").ap())
    bass_hybrid_block(nc, *args)
    r = run_bass_kernel_spmd(nc, [arrays], core_ids=[0])
    return r.results[0]["out_0"]
```

```python
from contextlib import ExitStack

import numpy as np

import concourse.bass as bass
from concourse import mybir

F32 = mybir.dt.float32
BF16 = mybir.dt.bfloat16
I32 = mybir.dt.int32
U32 = mybir.dt.uint32
ALU = mybir.AluOpType
ACT = mybir.ActivationFunctionType
AX = mybir.AxisListType

P = 128
HALF = 64
D_MODEL = 1024
SEQ = 256
TILES = SEQ // P
KB = D_MODEL // P
GH = 4
MH = 8
MHD = 64
CHUNK = 64
LEVELS = 6
E = 32
TOPK = 4
SLOTS = 64
PASSES = SEQ // SLOTS
PAIRS = E // 2
RING = 6
SLOT = 4096
PAIR_CHUNKS = 12
PICKS = PAIRS + 1
EPS = 1e-6
NEG = -1.0e30
LIMIT = 7.0
GATHER_BANK, GATED_BANK, GATE_BANK, UP_BANK, ACT_T_BANK, Y_BANK = (0, 5), 6, (1, 3), (2, 4), (0, 5), 6
COMBINE_BANK = {1: 1, 0: 3}
ALPHA = 1.702

W_ORDER = ["gdn_k", "gdn_q", "gdn_v", "mem_k", "mem_v", "moba_v", "moba_q", "moba_k", "gdn_z",
           "out_a", "out_b", "x_q", "x_o"]
PRE = len(W_ORDER)

ROWS = {"mix": 0, "mem": 8, "xattn": 16, "ffn": 24, "moba": 32, "gdn": 36, "conv": 37}
N_ROWS = 37 + 4 * 12

EARLY = [("const_cols", 3), ("x_T0", 0), ("x_T1", 1), ("gdn_k", 2), ("gdn_q", 3), ("gdn_ba", 0), ("mem_T0", 1),
         ("mem_T1", 0), ("gdn_v", 2), ("tok_k", 3), ("tok_q", 1), ("mem_k", 0), ("tok_v", 2), ("cum_g", 3),
         ("row_g", 1), ("k_T", 0), ("q_T", 2), ("mem_v", 3), ("kk", 0), ("qk", 1)]
MIDDLE = ["swap0", "moba_v.0", "swap1", "moba_v.1", "solve_T1", "solve1", "moba_v.2", "swap2", "moba_v.3",
          "solve_T2", "solve2", "moba_q.0", "swap3", "moba_q.1", "solve_T3", "solve3", "moba_q.2", "swap4",
          "moba_q.3", "solve_T4", "solve4", "moba_k.0", "moba_k.1", "swap5", "moba_k.2", "solve_T5", "moba_k.3",
          "u", "w_T", "score0", "state0", "gdn_z.0", "v1", "inter1", "probs_T0", "state1", "pv0", "score1",
          "intra0", "v2", "inter2", "gdn_z.1", "state2", "probs_T1", "pv1", "score2", "v3", "inter3", "gdn_z.2",
          "intra1", "probs_T2", "pv2", "score3", "gdn_z.3", "probs_T3", "pv3", "gdn_oT", "moba_oT"]
LATE = ["mix_out0", "mix_out1", "x_hT0", "x_q0", "x_hT1", "x_q1", "x_score0", "x_score1", "x_probs_T0", "x_pv0",
        "x_out0", "x_probs_T1", "x_pv1", "x_out1", "f_T0", "logits0", "f_T1", "logits1", "slots", "count"]


def lay_out_jobs():
    jobs, chain = list(EARLY), 0
    for name in MIDDLE:
        base, _, quarter = name.partition(".")
        if quarter:
            if quarter == "0":
                jobs.append((base, 3))
        elif base.startswith(("score", "probs_T", "pv")):
            jobs.append((base, 2))
        else:
            jobs.append((base, chain % 2))
            chain += 1
    jobs += [(name, (n + 2) % 4) for n, name in enumerate(LATE)]
    uses, placed = [0] * 4, {}
    for name, p in jobs:
        placed[name] = (p, uses[p])
        uses[p] += 1
    return placed


JOBS = lay_out_jobs()


def bass_hybrid_block(nc, x, mem, norm_mix_g, w_in, gdn_conv_w, gdn_A_log, gdn_dt_bias, gdn_norm_g,
                      moba_norm_g, w_out, norm_xattn_g, norm_mem_g, xattn_w_q, xattn_w_kv, xattn_w_o,
                      norm_ffn_g, router_w, router_b, w_gate_up, b_gate_up, w_down, b_down, final_norm_g, out):
    with ExitStack() as ctx:
        sems = {}

        def S(name):
            if name not in sems:
                sems[name] = ctx.enter_context(nc.semaphore(name))
            return sems[name]

        ring = ctx.enter_context(nc.sbuf_tensor("ring", [P, RING * SLOT], F32))
        work = ctx.enter_context(nc.sbuf_tensor("work", [P, 27136], F32))
        small = ctx.enter_context(nc.sbuf_tensor("small", [P, 1440], F32))

        def area(at, *dims):
            n = int(np.prod(dims))
            v = work[:, at:at + n]
            if len(dims) == 2:
                return v.rearrange("p (a b) -> p a b", b=dims[1])
            if len(dims) == 3:
                return v.rearrange("p (a b c) -> p a b c", b=dims[1], c=dims[2])
            return v

        X, HT, M1, M2, M3, TOK, ZZ = 0, 2048, 4096, 8192, 10240, 13312, 16384
        QKT, MQ, MK, MV, OM, KM, VM, PP, PT = 17408, 18432, 20480, 21504, 22528, 23552, 24576, 25600, 26368
        x_sb = area(X, TILES, D_MODEL)
        hT = area(HT, KB, SEQ)
        oT = area(HT, KB, SEQ)
        mem_sb = area(M1, TILES, D_MODEL)
        memT = area(M1 + 2048, KB, SEQ)
        a_mat = area(M1, 8, P)
        level_l = area(M1 + 1024, 8, P)
        inv = area(M1 + 2048, 8, P)
        inv_T = area(M1 + 3072, 8, P)
        decay_T = area(M1 + 2048, 8, P)
        decay = area(M1 + 3072, 8, P)
        u_sb = area(M1, 8, P)
        w_T = area(M1 + 1024, 8, P)
        square = area(M2, 16, P)
        g_rep = area(M2, 8, P)
        kbg = area(M2, 8, P)
        k_dec = area(M2 + 1024, 8, P)
        xn = area(M3, TILES, D_MODEL)
        conv = area(M3, 12, SEQ)
        k_T = area(M3, 8, P)
        q_T = area(M3 + 1024, 8, P)
        swap = area(M3 + 2048, 8, P)
        g_diff = area(M3 + 2048, 8, P)
        state = area(M3 + 2048, 4, P)
        o_tmp = area(M3 + 2560, 4, P)
        tok = area(TOK, 24, P)
        tok_k, tok_q, tok_v = tok[:, 0:8, :], tok[:, 8:16, :], tok[:, 16:24, :]
        o_gdn = tok_q
        rows = area(ZZ, P)
        z_sb = area(ZZ, 8, P)
        router_sb = area(ZZ, KB, E)
        router_bias = area(ZZ + 256, E)
        qk_T = area(QKT, 8, P)
        mq_z = area(MQ, MH, SEQ)
        mk_T = area(MK, 4, SEQ)
        mv_sb = area(MV, TILES, 512)
        o_moba = area(OM, TILES, 512)
        km_T = area(KM, 4, SEQ)
        vm_sb = area(VM, TILES, 512)
        m_p = area(PP, 2, 384)
        m_pT = area(PT, 2, 384)
        xq_T = area(MK, 4, SEQ)
        x_p = [area(M2, 4, SEQ), area(M2 + 1024, 4, SEQ)]
        x_pT = area(M1, 8, SEQ)
        bias_raw = area(TOK, 3072)
        bias_hi = work[:, M1 + 2048:M1 + 2048 + 1536].bitcast(BF16)
        bias_mid = work[:, PP:PP + 1536].bitcast(BF16)
        split = [work[:, MQ + 1024 * s:MQ + 1024 * s + 1024].bitcast(BF16).rearrange("p (a b) -> p a b", b=D_MODEL)
                 for s in range(3)]
        remainder = area(M2, TILES, D_MODEL)
        xg_T = [area(M3 + 512 * s, KB, SLOTS) for s in range(2)]
        act_T = area(M3 + 1024, 4, P)
        gate_sb = area(M3 + 1536, 512)
        up_sb = area(M3 + 2048, 512)
        sig_sb = area(M3 + 2560, 512)
        y_sb = area(MV, 2, 512)
        g_T = area(MV + 1024, 2, SEQ)
        pick_gated = area(MV + 1536, TILES, 3 * SLOTS)
        pick = [work[:, MV + 1920 + 64 * s:MV + 1984 + 64 * s].bitcast(BF16).rearrange("p (a b) -> p a b", b=SLOTS)
                for s in range(2)]
        choose = work[:, MV + 2048:MV + 2112].bitcast(BF16).rearrange("p (a b) -> p a b", b=SLOTS)
        final_gain = area(HT, D_MODEL)
        out_sb = area(M2, TILES, D_MODEL)
        mem_junk = area(M3, D_MODEL)

        at = [0]

        def tiny(n, dt=F32):
            w = n if dt == F32 or dt == I32 or dt == U32 else (n + 1) // 2
            v = small[:, at[0]:at[0] + w]
            at[0] += w
            return v if dt == F32 else v.bitcast(dt)

        ident = tiny(P)
        cols = tiny(N_ROWS)
        tri = tiny(P)
        causal = tiny(384, BF16).rearrange("p (a b) -> p a b", b=P)
        level_mask = tiny(LEVELS * P, BF16).rearrange("p (a b) -> p a b", b=P)
        w_ba = tiny(64).rearrange("p (a b) -> p a b", b=8)
        iota_s = tiny(SLOTS)
        before = tiny(P, BF16)
        ones = tiny(P, BF16)
        ss, rstd = tiny(TILES), tiny(TILES)
        mem_ss, mem_rstd = tiny(TILES), tiny(TILES)
        sum16, r16 = tiny(16), tiny(16)
        a_log, dt_bias = tiny(GH), tiny(GH)
        beta, g_log, g_cum, e_g, beta_eg, k_decay = (tiny(8) for _ in range(6))
        sp_v, sp_n, sp_e = tiny(8), tiny(8), tiny(8)
        e_last = tiny(16)
        m_max, m_bias, m_sum, m_inv = tiny(4), tiny(4), tiny(16), tiny(16)
        x_max, x_bias, x_sum, x_inv = tiny(8), tiny(8), tiny(8), tiny(8)
        expert_no, part_no = tiny(1), tiny(1)
        table_out = tiny(1)
        count_max, count_i = tiny(1), tiny(1, I32)
        rt = [QKT]

        def routing(*dims):
            n = int(np.prod(dims))
            v = area(rt[0], *dims)
            rt[0] += n
            return v

        logits = routing(TILES, E)
        top8 = routing(TILES, 8)
        top_i = routing(TILES * 8).bitcast(U32).rearrange("p (a b) -> p a b", b=8)
        top_f = routing(TILES, 8)
        top_bias = routing(TILES)
        top_e = routing(TILES, 8)
        top_s = routing(TILES)
        top_w = routing(TILES, 8)
        hit = routing(TILES * TOPK, E)
        gates = routing(TILES, E + 2)
        chosen = routing(TILES, E)
        chosen_b = routing(TILES * E // 2).bitcast(BF16).rearrange("p (a b) -> p a b", b=E)
        slot_m = routing(TILES, E + 2)
        iota_e = routing(E)

        def idx_tiles():
            b = M2
            return (work[:, b:b + 128].bitcast(I32), work[:, b + 128:b + 129].bitcast(I32),
                    work[:, b + 256:b + 384].bitcast(I32), work[:, b + 384:b + 390].bitcast(I32),
                    work[:, b + 400:b + 406].bitcast(I32), area(b + 512, P), area(b + 640, 6), area(b + 650, 6))

        ps = ctx.enter_context(nc.psum_tensor("ps", [P, 4096], F32))

        def bank(b):
            return ps[:, 512 * b:512 * b + 512]

        def pair(name):
            p = JOBS[name][0]
            return ps[:, p * 1024:(p + 1) * 1024]

        def blocks(name):
            return pair(name).rearrange("p (b n) -> p b n", n=P)

        def halves(name):
            return pair(name).rearrange("p (b n) -> p b n", n=512)

        def take(pe, name):
            p, use = JOBS[name]
            if use:
                pe.wait_ge(S(f"pair_drained{p}"), use)

        def fill_done(ins, name):
            ins.then_inc(S(f"pair_filled{JOBS[name][0]}"), 1)

        def filled(eng, name):
            p, use = JOBS[name]
            eng.wait_ge(S(f"pair_filled{p}"), use + 1)

        def drain_done(ins, name):
            ins.then_inc(S(f"pair_drained{JOBS[name][0]}"), 1)

        def drained(eng, name):
            p, use = JOBS[name]
            eng.wait_ge(S(f"pair_drained{p}"), use + 1)

        steps = {}

        def own(eng, ins, name):
            steps[name] = steps.get(name, 0) + 1
            ins.then_inc(S(name), 1)
            eng.wait_ge(S(name), steps[name])

        def spread(v, n):
            return v.unsqueeze(2).to_broadcast([v.shape[0], v.shape[1], n])

        def slot(s):
            return ring[:, s * SLOT:(s + 1) * SLOT]

        def weights(name):
            n = W_ORDER.index(name)
            return slot(n % RING)

        def weights_landed(pe, name):
            n = W_ORDER.index(name)
            pe.wait_ge(S(f"slot_loaded{n % RING}"), 16 * (n // RING + 1))

        def weights_used(ins, name):
            ins.then_inc(S(f"slot_free{W_ORDER.index(name) % RING}"), 1)

        def ring_use(c):
            return (PRE + c) % RING, (PRE + c) // RING

        row = lambda v: v.rearrange("a (b n) -> (a b) n", n=P)
        block = ctx.enter_context(nc.Block())

        @block.sync
        def _(sp):
            wi = w_in[0].rearrange("(k p) n -> p k n", p=P)
            kv = xattn_w_kv[0].rearrange("(k p) n -> p k n", p=P)
            wo = w_out[0].rearrange("(k p) n -> p k n", p=P)
            source = {"moba_q": wi[:, :, 0:512], "moba_k": wi[:, :, 512:1024], "moba_v": wi[:, :, 1024:1536],
                      "gdn_q": wi[:, :, 1536:2048], "gdn_k": wi[:, :, 2048:2560], "gdn_v": wi[:, :, 2560:3072],
                      "gdn_z": wi[:, :, 3072:3584], "mem_k": kv[:, :, 0:512], "mem_v": kv[:, :, 512:1024],
                      "out_a": wo[:, :, 0:512], "out_b": wo[:, :, 512:1024],
                      "x_q": xattn_w_q[0].rearrange("(k p) n -> p k n", p=P),
                      "x_o": xattn_w_o[0].rearrange("(k p) n -> p k n", p=P)}
            for t in range(TILES):
                sp.dma_start(x_sb[:, t, :], x[0, t * P:(t + 1) * P, :]).then_inc(S(f"x_loaded{t}"), 16)
            sp.wait_ge(S("rows_loaded"), 16 * len(ROWS))
            for n, name in enumerate(W_ORDER):
                s = n % RING
                if n >= RING:
                    sp.wait_ge(S(f"slot_free{s}"), n // RING)
                src = source[name]
                sp.dma_start(slot(s).rearrange("p (k n) -> p k n", n=src.shape[2]), src) \
                    .then_inc(S(f"slot_loaded{s}"), 16)

            def load_pair(i, before):
                gu = [w_gate_up[0, bass.ds(2 * i + k, 1)].rearrange("e (k p) n -> p (e k) n", p=P) for k in range(2)]
                dn = [w_down[0, bass.ds(2 * i + k, 1)].rearrange("e (k p) n -> p (e k) n", p=P) for k in range(2)]
                for c in range(PAIR_CHUNKS):
                    s, use = ring_use(c)
                    if c < 8:
                        src = gu[c // 4][:, 2 * (c % 4):2 * (c % 4) + 2, :]
                    else:
                        src = dn[(c - 8) // 2][:, 4 * (c % 2):4 * (c % 2) + 4, :]
                    sp.wait_ge(S(f"slot_free{s}"), 2 * before + use)
                    sp.dma_start(slot(s).rearrange("p (k n) -> p k n", n=src.shape[2]), src) \
                        .then_inc(S(f"slot_loaded{s}"), 16)

            with sp.Fori(0, PAIRS) as i:
                load_pair(i, i)
            sp.wait_ge(S("count_ready"), 1)
            most = sp.value_load(count_i[0:1, 0:1], min_val=0, max_val=SEQ)
            with sp.If(most > SLOTS):
                with sp.Fori(1, PASSES) as r:
                    with sp.If(most > r * SLOTS):
                        with sp.Fori(0, PAIRS) as i:
                            load_pair(i, sp.snap(r * PAIRS + i))
            for t in range(TILES):
                sp.wait_ge(S("out_ready"), t + 1)
                sp.dma_start(out[0, t * P:(t + 1) * P, :], out_sb[:, t, :]).then_inc(S("out_stored"), 16)
            sp.wait_ge(S("out_stored"), 16 * TILES)

        @block.gpsimd
        def _(pool):
            p_row, p_col = idx_tiles()[0:2]
            own(pool, nc.gpsimd.memset(ident, 0.0), "pool_step")
            nc.gpsimd.affine_select(out=ident, in_=ident, compare_op=ALU.not_equal, fill=1.0, base=0,
                                    pattern=[[-1, P]], channel_multiplier=1).then_inc(S("ident_ready"), 1)
            nc.gpsimd.iota(p_row, pattern=[[1, P]], base=0, channel_multiplier=0)
            nc.gpsimd.iota(p_col, pattern=[[0, 1]], base=0, channel_multiplier=1).then_inc(S("indices_ready"), 1)
            own(pool, nc.gpsimd.memset(tri, 1.0), "pool_step")
            own(pool, nc.gpsimd.affine_select(out=tri, in_=tri, compare_op=ALU.is_ge, fill=0.0, base=0,
                                              pattern=[[1, P]], channel_multiplier=-1), "pool_step")
            nc.gpsimd.memset(tri[0:HALF, HALF:P], 0.0).then_inc(S("tri_ready"), 1)
            own(pool, nc.gpsimd.memset(causal, 0.0), "pool_step")
            for b in (0, 2):
                nc.gpsimd.affine_select(out=causal[:, b, :], in_=causal[:, b, :], compare_op=ALU.is_ge,
                                        fill=NEG, base=0, pattern=[[-1, P]], channel_multiplier=1) \
                    .then_inc(S("causal_ready"), 1)
            nc.gpsimd.memset(mq_z, 0.0).then_inc(S("mq_zeroed"), 1)
            nc.gpsimd.iota(iota_s, pattern=[[1, SLOTS]], base=0, channel_multiplier=0,
                           allow_small_or_imprecise_dtypes=True).then_inc(S("iota_ready"), 1)
            own(pool, nc.gpsimd.memset(before, 1.0), "pool_step")
            nc.gpsimd.affine_select(out=before, in_=before, compare_op=ALU.is_gt, fill=0.0, base=0,
                                    pattern=[[1, P]], channel_multiplier=-1).then_inc(S("before_ready"), 1)
            nc.gpsimd.memset(ones, 1.0).then_inc(S("before_ready"), 1)
            drained(pool, "intra1")
            drained(pool, "gdn_oT")
            nc.gpsimd.iota(iota_e, pattern=[[1, E]], base=0, channel_multiplier=0,
                           allow_small_or_imprecise_dtypes=True).then_inc(S("iota_e_ready"), 1)
            pool.wait_ge(S("iota_e_ready"), 1)
            for s in range(3):
                nc.gpsimd.iota(part_no[32 * s:32 * s + 32], pattern=[[0, 1]], base=0, channel_multiplier=1,
                               allow_small_or_imprecise_dtypes=True).then_inc(S("part_no_ready"), 1)
                pool.wait_ge(S("part_no_ready"), s + 1)
            for s in range(3):
                pool.dma_start(bias_raw[32 * s:32 * s + E, 0:2048], b_gate_up[0]).then_inc(S("bias_loaded"), 16)
                pool.dma_start(bias_raw[32 * s:32 * s + E, 2048:3072], b_down[0]).then_inc(S("bias_loaded"), 16)
            pool.wait_ge(S("bias_loaded"), 96)
            own(pool, nc.gpsimd.tensor_copy(bias_hi[0:96, :], bias_raw[0:96, :]), "pool_step")
            for part in (bias_hi, bias_mid):
                own(pool, nc.gpsimd.tensor_tensor(bias_raw[0:96, :], bias_raw[0:96, :], part[0:96, :],
                                                  ALU.subtract), "pool_step")
                if part is bias_hi:
                    own(pool, nc.gpsimd.tensor_copy(bias_mid[0:96, :], bias_raw[0:96, :]), "pool_step")
            own(pool, nc.gpsimd.tensor_copy(bias_hi[32:64, :], bias_mid[32:64, :]), "pool_step")
            nc.gpsimd.tensor_copy(bias_hi[64:96, :], bias_raw[64:96, :]).then_inc(S("biases_ready"), 1)

        @block.scalar
        def _(act):
            for name, src in (("mix", row(norm_mix_g)), ("mem", row(norm_mem_g)), ("xattn", row(norm_xattn_g)),
                              ("ffn", row(norm_ffn_g)), ("moba", row(moba_norm_g)), ("gdn", gdn_norm_g),
                              ("conv", gdn_conv_w[0].rearrange("j (c p) -> (j c) p", p=P))):
                r = ROWS[name]
                act.dma_start(rows[r:r + src.shape[0], :], src).then_inc(S("rows_loaded"), 16)
            act.dma_start(a_log, gdn_A_log[0].partition_broadcast(P)).then_inc(S("ab_loaded"), 16)
            act.dma_start(dt_bias, gdn_dt_bias[0].partition_broadcast(P)).then_inc(S("ab_loaded"), 16)
            act.dma_start(w_ba, w_in[0, :, 3584:3592].rearrange("(k p) n -> p k n", p=P)) \
                .then_inc(S("w_ba_loaded"), 16)
            for t in range(TILES):
                act.dma_start(mem_sb[:, t, :], mem[0, t * P:(t + 1) * P, :]).then_inc(S(f"mem_loaded{t}"), 16)

            def squares(src, junk, acc, t, name):
                nc.scalar.activation(junk, src[:, t, :], ACT.Square, accum_out=acc[:, t:t + 1]) \
                    .then_inc(S(name), 1)

            def root(v, after, count, name):
                act.wait_ge(S(after), count)
                nc.scalar.activation(v, v, ACT.Sqrt).then_inc(S(name), 1)

            def evacuate(name, dst, src):
                filled(act, name)
                drain_done(nc.scalar.copy(dst, src), name)

            by_tile = lambda v, t: v[:, t:t + 1]

            def load_table(func):
                own(act, nc.scalar.activation(table_out, cols[:, 0:1], func), "table_loaded")

            for t in range(TILES):
                act.wait_ge(S(f"x_loaded{t}"), 16)
                squares(x_sb, xn[:, t, :], ss, t, "x_squared")
            for t in range(TILES):
                root(by_tile(rstd, t), "x_mean", t + 1, "x_root")
            act.wait_ge(S("ab_loaded"), 32)
            nc.scalar.activation(a_log, a_log, ACT.Exp).then_inc(S("rate_ready"), 1)
            for t in range(TILES):
                act.wait_ge(S(f"mem_loaded{t}"), 16)
                squares(mem_sb, tok[:, 8 * t:8 * t + 8, :].rearrange("p a b -> p (a b)"), mem_ss, t, "mem_squared")
            root(mem_rstd, "mem_mean", 1, "mem_root")

            def silu_conv(n, name):
                drained(act, name)
                c = conv[:, 4 * n:4 * n + 4, :]
                nc.scalar.activation(c, c, ACT.Silu).then_inc(S("conv_silu"), 1)

            silu_conv(0, "gdn_k")
            silu_conv(1, "gdn_q")
            filled(act, "gdn_ba")
            ba = pair("gdn_ba").rearrange("p (t n) -> p t n", n=512)
            nc.scalar.activation(beta.rearrange("p (t n) -> p t n", n=GH), ba[:, :, 0:GH], ACT.Sigmoid) \
                .then_inc(S("beta_ready"), 1)
            act.wait_ge(S("softplus_arg"), 1)
            nc.scalar.activation(sp_e, sp_n, ACT.Exp).then_inc(S("softplus_exp"), 1)
            act.wait_ge(S("softplus_sum"), 1)
            nc.scalar.activation(sp_e, sp_e, ACT.Ln).then_inc(S("softplus_ln"), 1)
            evacuate("tok_k", tok_k, blocks("tok_k"))
            evacuate("tok_q", tok_q, blocks("tok_q"))
            silu_conv(2, "gdn_v")
            root(r16, "l2_sums", 1, "l2_root")
            evacuate("mem_k", km_T, pair("mem_k").rearrange("p (b n) -> p b n", n=SEQ))
            evacuate("tok_v", tok_v, blocks("tok_v"))
            drained(act, "cum_g")
            nc.scalar.activation(e_g, g_cum, ACT.Exp).then_inc(S("e_g_ready"), 1)
            evacuate("k_T", k_T, blocks("k_T"))
            evacuate("q_T", q_T, blocks("q_T"))
            evacuate("mem_v", vm_sb, halves("mem_v"))
            act.wait_ge(S("decay_args"), 1)
            nc.scalar.activation(decay, decay, ACT.Exp, scale=-1.0).then_inc(S("decay_ready"), 1)
            nc.scalar.activation(decay_T, decay_T, ACT.Exp).then_inc(S("decay_ready"), 1)
            nc.scalar.activation(k_decay, k_decay, ACT.Exp).then_inc(S("decay_ready"), 1)
            nc.scalar.activation(e_last, e_last, ACT.Exp).then_inc(S("decay_ready"), 1)

            def moba_probs(hp):
                act.wait_ge(S("moba_bias"), hp + 1)
                for h in range(2):
                    n = 2 * (2 * hp + h)
                    nc.scalar.activation(m_p[:, h, 0:P], m_p[:, h, 0:P], ACT.Exp, bias=m_bias[:, 2 * h:2 * h + 1],
                                         scale=MHD ** -0.5, accum_out=m_sum[:, n:n + 1])
                    last = nc.scalar.activation(m_p[:, h, P:384], m_p[:, h, P:384], ACT.Exp,
                                                bias=m_bias[:, 2 * h + 1:2 * h + 2], scale=MHD ** -0.5,
                                                accum_out=m_sum[:, n + 1:n + 2])
                last.then_inc(S("moba_exp"), 1)

            for name in MIDDLE:
                base = name.partition(".")[0]
                if name.startswith("score"):
                    moba_probs(int(name[-1]))
                elif name.startswith("probs_T"):
                    filled(act, name)
                    drain_done(nc.scalar.copy(m_pT, halves(name)[:, :, 0:384]), name)
                elif name.startswith("swap") and name != "swap0":
                    evacuate(name, swap, blocks(name))
                elif name == "moba_v.3":
                    evacuate(base, mv_sb, halves(base))
                elif name == "moba_q.3":
                    filled(act, base)
                    act.wait_ge(S("mq_zeroed"), 1)
                    mq4 = mq_z.rearrange("p (b h) n -> p b h n", h=2)
                    q4 = pair(base).rearrange("p (b n) -> p b n", n=SEQ)
                    nc.scalar.copy(mq4[0:HALF, :, 0, :], q4[0:HALF])
                    drain_done(nc.scalar.copy(mq4[HALF:P, :, 1, :], q4[HALF:P]), base)
                elif name == "moba_k.3":
                    evacuate(base, mk_T, pair(base).rearrange("p (b n) -> p b n", n=SEQ))
                elif name == "gdn_z.3":
                    filled(act, base)
                    drain_done(nc.scalar.activation(z_sb, blocks(base), ACT.Silu), base)
                elif name == "u":
                    evacuate("u", u_sb, blocks("u"))
                elif name == "w_T":
                    evacuate("w_T", w_T, blocks("w_T"))
                elif name == "intra0":
                    evacuate("intra0", o_gdn[:, 0:4, :], blocks("intra0")[:, 0:4, :])
                elif name == "intra1":
                    evacuate("intra1", o_gdn[:, 4:8, :], blocks("intra1")[:, 0:4, :])
            root(r16[:, 0:8], "gdn_mean", 1, "gdn_root")
            root(ss, "moba_mean", 1, "moba_root")
            act.wait_ge(S("gdn_gated"), 1)
            act.dma_start(router_sb, router_w[0].rearrange("(k p) n -> p k n", p=P)).then_inc(S("router_loaded"), 16)
            act.dma_start(router_bias, router_b[0].partition_broadcast(P)).then_inc(S("router_loaded"), 16)
            for t in range(TILES):
                drained(act, f"mix_out{t}")
                squares(x_sb, xn[:, t, :], ss, t, "x1_squared")
                root(by_tile(rstd, t), "x1_mean", t + 1, "x1_root")
            load_table(ACT.Exp)
            for t in range(TILES):
                evacuate(f"x_q{t}", xq_T[:, :, t * P:(t + 1) * P], blocks(f"x_q{t}")[:, 0:4, :])
            for t in range(TILES):
                act.wait_ge(S("x_bias_ready"), t + 1)
                filled(act, f"x_score{t}")
                sc = pair(f"x_score{t}").rearrange("p (b n) -> p b n", n=SEQ)
                for h in range(GH):
                    last = nc.scalar.activation(x_p[t][:, h, :], sc[:, h, :], ACT.Exp,
                                                bias=x_bias[:, 4 * t + h:4 * t + h + 1], scale=P ** -0.5,
                                                accum_out=x_sum[:, 4 * t + h:4 * t + h + 1])
                drain_done(last, f"x_score{t}")
            load_table(ACT.Sqrt)
            for t in range(TILES):
                evacuate(f"x_pv{t}", oT[:, 0:4, t * P:(t + 1) * P], blocks(f"x_pv{t}")[:, 0:4, :])

            def split_high(t):
                act.wait_ge(S("x2_normed"), t + 1)
                nc.scalar.copy(split[0][:, t, :], xn[:, t, :]).then_inc(S("split_high"), 1)

            def split_mid(t):
                act.wait_ge(S("split_rest"), t + 1)
                nc.scalar.copy(split[1][:, t, :], remainder[:, t, :]).then_inc(S("split_mid"), 1)

            def top_exp(t):
                act.wait_ge(S("top_bias_ready"), t + 1)
                nc.scalar.activation(top_e[:, t, 0:TOPK], top8[:, t, 0:TOPK], ACT.Exp, bias=top_bias[:, t:t + 1],
                                     accum_out=top_s[:, t:t + 1]).then_inc(S("top_exp"), 1)

            for t in range(TILES):
                drained(act, f"x_out{t}")
                squares(x_sb, xn[:, t, :], ss, t, "x2_squared")
                root(by_tile(rstd, t), "x2_mean", t + 1, "x2_root")
                if t == 0:
                    split_high(0)
            split_mid(0)
            split_high(1)
            top_exp(0)
            split_mid(1)
            top_exp(1)

            def expert(n, b):
                act.wait_ge(S("gate_clipped"), n)
                nc.scalar.activation(sig_sb, gate_sb, ACT.Sigmoid, scale=ALPHA).then_inc(S("gate_sigmoid"), 1)
                act.wait_ge(S("act_T_filled"), n + 1)
                nc.scalar.copy(act_T, bank(b).rearrange("p (b n) -> p b n", n=P)).then_inc(S("act_T_ready"), 1)

            def expert_pairs(base):
                with act.Fori(0, PAIRS) as i:
                    expert(act.snap(base + 2 * i + 1), ACT_T_BANK[0])
                    expert(act.snap(base + 2 * i + 2), ACT_T_BANK[1])

            act.wait_ge(S("count_ready"), 1)
            most = act.value_load(count_i[0:1, 0:1], min_val=0, max_val=SEQ)
            expert_pairs(0)
            with act.If(most > SLOTS):
                with act.Fori(1, PASSES) as r:
                    with act.If(most > r * SLOTS):
                        expert_pairs(r * E)
            act.dma_start(final_gain, final_norm_g.partition_broadcast(P)).then_inc(S("final_gain_loaded"), 16)
            load_table(ACT.Sqrt)
            act.wait_ge(S("x_final"), 1)
            for t in range(TILES):
                squares(x_sb, out_sb[:, t, :], ss, t, "x3_squared")
            for t in range(TILES):
                root(by_tile(rstd, t), "x3_mean", t + 1, "x3_root")

        @block.vector
        def _(v):
            def step(ins):
                own(v, ins, "dve_step")

            v.wait_ge(S("indices_ready"), 1)
            p_row, p_col, j_sh, i_sh, i_bit, j_f, i_f, b_f = idx_tiles()
            for l in range(LEVELS):
                nc.vector.tensor_single_scalar(i_sh[:, l:l + 1], p_col, l, ALU.logical_shift_right) \
                    .then_inc(S("dve_step"), 1)
            steps["dve_step"] = LEVELS
            v.wait_ge(S("dve_step"), LEVELS)
            step(nc.vector.tensor_single_scalar(i_bit, i_sh, 1, ALU.bitwise_and))
            nc.vector.tensor_copy(i_f, i_sh)
            step(nc.vector.tensor_copy(b_f, i_bit))
            for l in range(LEVELS):
                step(nc.vector.tensor_single_scalar(j_sh, p_row, l, ALU.logical_shift_right))
                step(nc.vector.tensor_copy(j_f, j_sh))
                step(nc.vector.tensor_scalar(j_f, j_f, i_f[:, l:l + 1], -1.0, ALU.subtract, ALU.is_equal))
                step(nc.vector.tensor_scalar(level_mask[:, l, :], j_f, b_f[:, l:l + 1], None, ALU.mult))

            def mean(acc, dst, n, after, count, name):
                v.wait_ge(S(after), count)
                nc.vector.tensor_scalar(dst, acc, 1.0 / n, EPS, ALU.mult, ALU.add).then_inc(S(name), 1)

            def invert(dst, after, count=1):
                v.wait_ge(S(after), count)
                step(nc.vector.reciprocal(dst, dst))

            def tile_mean(t, tag):
                mean(ss[:, t:t + 1], rstd[:, t:t + 1], D_MODEL, f"{tag}_squared", t + 1, f"{tag}_mean")

            def tile_normed(t, tag):
                invert(rstd[:, t:t + 1], f"{tag}_root", t + 1)
                nc.vector.tensor_scalar(xn[:, t, :], x_sb[:, t, :], rstd[:, t:t + 1], None, ALU.mult) \
                    .then_inc(S(f"{tag}_normed"), 1)

            def normalise(dst, src, r, name):
                for t in range(TILES):
                    nc.vector.tensor_scalar(dst[:, t, :], src[:, t, :], r[:, t:t + 1], None, ALU.mult) \
                        .then_inc(S(name), 1)

            def gained_T(name, dst, t, gain):
                filled(v, name)
                drain_done(nc.vector.tensor_tensor(
                    dst[:, :, t * P:(t + 1) * P], blocks(name),
                    spread(cols[:, ROWS[gain]:ROWS[gain] + KB], P), ALU.mult), name)

            filled(v, "const_cols")
            drain_done(nc.vector.tensor_copy(cols, pair("const_cols")[:, 0:N_ROWS]), "const_cols")
            for t in range(TILES):
                tile_mean(t, "x")
            for t in range(TILES):
                tile_normed(t, "x")
            drained(v, "const_cols")
            gained_T("x_T0", hT, 0, "mix")
            gained_T("x_T1", hT, 1, "mix")
            mean(mem_ss, mem_rstd, D_MODEL, "mem_squared", TILES, "mem_mean")
            invert(mem_rstd, "mem_root")
            normalise(mem_sb, mem_sb, mem_rstd, "memn_ready")

            def convolve(n, name):
                filled(v, name)
                src = pair(name).rearrange("p (b n) -> p b n", n=SEQ)
                for j in (3, 2, 1, 0):
                    back = 3 - j
                    for b in range(4):
                        blk = {"gdn_q": 0, "gdn_k": 4, "gdn_v": 8}[name] + b
                        c = ROWS["conv"] + 12 * j + blk
                        w = cols[:, c:c + 1]
                        dst = conv[:, 4 * n + b, back:SEQ]
                        if j == 3:
                            ins = nc.vector.tensor_scalar(dst, src[:, b, :], w, None, ALU.mult)
                        else:
                            ins = nc.vector.scalar_tensor_tensor(dst, src[:, b, 0:SEQ - back], w, dst,
                                                                 ALU.mult, ALU.add)
                        if b == 3 and j > 0:
                            step(ins)
                        elif b == 3:
                            drain_done(ins, name)

            convolve(0, "gdn_k")
            convolve(1, "gdn_q")
            filled(v, "gdn_ba")
            ba = pair("gdn_ba").rearrange("p (t n) -> p t n", n=512)
            v.wait_ge(S("ab_loaded"), 32)
            v.wait_ge(S("beta_ready"), 1)
            t8 = lambda q: q.rearrange("p (t n) -> p t n", n=GH)
            over_t = lambda q: q.unsqueeze(1).to_broadcast([P, TILES, GH])
            drain_done(nc.vector.tensor_tensor(t8(sp_v), ba[:, :, GH:2 * GH], over_t(dt_bias), ALU.add), "gdn_ba")
            drained(v, "gdn_ba")
            nc.vector.scalar_tensor_tensor(sp_n, sp_v, -1.0, sp_v, ALU.mult, ALU.min).then_inc(S("softplus_arg"), 1)
            gained_T("mem_T0", memT, 0, "mem")
            gained_T("mem_T1", memT, 1, "mem")
            v.wait_ge(S("softplus_exp"), 1)
            nc.vector.tensor_scalar(sp_e, sp_e, 1.0, None, ALU.add).then_inc(S("softplus_sum"), 1)
            v.wait_ge(S("softplus_ln"), 1)
            step(nc.vector.scalar_tensor_tensor(sp_v, sp_v, 0.0, sp_e, ALU.max, ALU.add))
            v.wait_ge(S("rate_ready"), 1)
            nc.vector.scalar_tensor_tensor(t8(g_log), t8(sp_v), -1.0, over_t(a_log), ALU.mult, ALU.mult) \
                .then_inc(S("g_ready"), 1)
            convolve(2, "gdn_v")
            drained(v, "tok_k")
            drained(v, "tok_q")
            step(nc.vector.tensor_tensor(square, tok[:, 0:16, :], tok[:, 0:16, :], ALU.mult))
            step(nc.vector.tensor_reduce(sum16, square, AX.X, ALU.add))
            nc.vector.tensor_scalar(r16, sum16, EPS, None, ALU.add).then_inc(S("l2_sums"), 1)
            v.wait_ge(S("g_ready"), 1)
            nc.vector.tensor_copy(g_rep, spread(g_log, P)).then_inc(S("g_rep_ready"), 1)
            invert(r16, "l2_root")
            step(nc.vector.tensor_scalar(r16[:, 8:16], r16[:, 8:16], P ** -0.5, None, ALU.mult))
            nc.vector.tensor_tensor(tok[:, 0:16, :], tok[:, 0:16, :], spread(r16, P), ALU.mult) \
                .then_inc(S("qk_normed"), 1)
            filled(v, "cum_g")
            drain_done(nc.vector.tensor_copy(g_cum, pair("cum_g")[:, 0:8]), "cum_g")
            drained(v, "cum_g")
            filled(v, "row_g")
            rg = blocks("row_g")
            step(nc.vector.tensor_tensor(g_diff, rg, spread(g_cum, P), ALU.subtract))
            nc.vector.tensor_tensor(k_decay[0:HALF].unsqueeze(2), rg[0:HALF, :, HALF - 1:HALF],
                                    g_cum[0:HALF].unsqueeze(2), ALU.subtract)
            nc.vector.tensor_tensor(k_decay[HALF:P].unsqueeze(2), rg[HALF:P, :, P - 1:P],
                                    g_cum[HALF:P].unsqueeze(2), ALU.subtract)
            drain_done(nc.vector.tensor_copy(e_last.rearrange("p (a b) -> p a b", b=2), rg[:, :, HALF - 1:P:HALF]),
                       "row_g")
            drained(v, "row_g")
            v.wait_ge(S("e_g_ready"), 1)
            step(nc.vector.tensor_tensor(beta_eg, beta, e_g, ALU.mult))
            v.wait_ge(S("qk_normed"), 1)
            nc.vector.tensor_tensor(kbg, tok_k, spread(beta_eg, P), ALU.mult).then_inc(S("kbg_ready"), 1)
            drained(v, "tok_v")
            nc.vector.tensor_tensor(tok_v, tok_v, spread(beta, P), ALU.mult).then_inc(S("vb_ready"), 1)
            filled(v, "mem_v")
            nc.vector.tensor_scalar(decay, g_diff, 0.0, None, ALU.max)
            nc.vector.tensor_scalar(decay_T, g_diff, 0.0, None, ALU.min).then_inc(S("decay_args"), 1)
            v.wait_ge(S("decay_ready"), 4)
            step(nc.vector.tensor_tensor(decay, decay, spread(beta, P), ALU.mult))
            filled(v, "kk")
            drain_done(nc.vector.tensor_tensor(a_mat, blocks("kk"), decay, ALU.mult), "kk")
            drained(v, "kk")

            def level_part(l):
                nc.vector.tensor_tensor(level_l, a_mat, level_mask[:, l, :].unsqueeze(1).to_broadcast([P, 8, P]),
                                        ALU.mult).then_inc(S("level_ready"), 1)

            level_part(0)
            v.wait_ge(S("tri_ready"), 1)
            step(nc.vector.tensor_tensor(decay_T, decay_T, tri.unsqueeze(1).to_broadcast([P, 8, P]), ALU.mult))
            filled(v, "qk")
            drain_done(nc.vector.tensor_tensor(qk_T, blocks("qk"), decay_T, ALU.mult), "qk")
            nc.vector.tensor_tensor(k_dec, tok_k, spread(k_decay, P), ALU.mult).then_inc(S("k_dec_ready"), 1)
            drained(v, "qk")
            v.wait_ge(S("level_ready"), 1)
            eye = ident.unsqueeze(1).to_broadcast([P, 8, P])
            v.wait_ge(S("ident_ready"), 1)
            nc.vector.tensor_tensor(inv, eye, level_l, ALU.subtract).then_inc(S("solved"), 1)
            v.wait_ge(S("causal_ready"), 2)

            def new_values(n):
                p = slice(HALF * (n % 2), HALF * (n % 2) + HALF)
                us = u_sb[p, 4 * (n // 2):4 * (n // 2) + 4, :]
                if n == 1:
                    drained(v, "u")
                filled(v, f"v{n}")
                drain_done(nc.vector.tensor_tensor(us, us, blocks(f"v{n}")[p, 0:4, :], ALU.subtract), f"v{n}")

            def next_state(n):
                if n:
                    t0 = 4 * (n // 2)
                    el = e_last.rearrange("p (a b) -> p a b", b=2)[:, t0:t0 + 4, n % 2]
                    step(nc.vector.tensor_tensor(state, state, spread(el, P), ALU.mult))
                    filled(v, f"state{n}")
                    drain_done(nc.vector.tensor_tensor(state, state, blocks(f"state{n}")[:, 0:4, :], ALU.add),
                               f"state{n}")
                else:
                    filled(v, "state0")
                    drain_done(nc.vector.tensor_copy(state, blocks("state0")[:, 0:4, :]), "state0")
                drained(v, f"state{n}")

            def inter(n):
                p = slice(HALF * (n % 2), HALF * (n % 2) + HALF)
                t0 = 4 * (n // 2)
                filled(v, f"inter{n}")
                drain_done(nc.vector.tensor_tensor(o_tmp[p], blocks(f"inter{n}")[p, 0:4, :],
                                                   spread(e_g[p, t0:t0 + 4], P), ALU.mult), f"inter{n}")
                drained(v, f"inter{n}")

            def add_inter(n):
                p = slice(HALF * (n % 2), HALF * (n % 2) + HALF)
                t0 = 4 * (n // 2)
                step(nc.vector.tensor_tensor(o_gdn[p, t0:t0 + 4, :], o_gdn[p, t0:t0 + 4, :], o_tmp[p], ALU.add))

            def moba_scores(name, n):
                filled(v, name)
                s3 = halves(name)[:, :, 0:384].rearrange("p h (b n) -> p h b n", n=P)
                p3 = m_p.rearrange("p h (b n) -> p h b n", n=P)
                if n:
                    drained(v, f"probs_T{n - 1}")
                for h in range(2):
                    ins = nc.vector.tensor_tensor(p3[:, h], s3[:, h], causal, ALU.add)
                drain_done(ins, name)
                drained(v, name)
                if n:
                    v.wait_ge(S("moba_exp"), n)
                nc.vector.tensor_reduce(m_max[:, 0:4:2], m_p[:, :, 0:P], AX.X, ALU.max)
                step(nc.vector.tensor_reduce(m_max[:, 1:4:2], m_p[:, :, P:384], AX.X, ALU.max))
                nc.vector.tensor_scalar(m_bias, m_max, -(MHD ** -0.5), None, ALU.mult).then_inc(S("moba_bias"), 1)

            def moba_outputs(name, n):
                v.wait_ge(S("moba_exp"), n + 1)
                step(nc.vector.reciprocal(m_inv[:, 4 * n:4 * n + 4], m_sum[:, 4 * n:4 * n + 4]))
                filled(v, name)
                for t in range(TILES):
                    dst = o_moba[:, t, P * n:P * n + P].rearrange("p (h d) -> p h d", d=MHD)
                    src = halves(name)[:, t, 0:P].rearrange("p (h d) -> p h d", d=MHD)
                    ins = nc.vector.tensor_tensor(dst, src, spread(m_inv[:, 4 * n + t:4 * n + 4:2], MHD), ALU.mult)
                drain_done(ins, name)

            for name in MIDDLE[:MIDDLE.index("gdn_oT")]:
                n = int(name[-1]) if name[-1].isdigit() else 0
                if name == "swap0":
                    filled(v, name)
                    drain_done(nc.vector.tensor_tensor(inv_T, eye, blocks(name), ALU.subtract), name)
                    v.wait_ge(S("solved"), 1)
                    level_part(1)
                    drained(v, name)
                elif name.startswith("swap"):
                    if n + 1 < LEVELS:
                        filled(v, name)
                        level_part(n + 1)
                elif name.startswith("solve_T"):
                    filled(v, name)
                    drain_done(nc.vector.tensor_tensor(inv_T, inv_T, blocks(name), ALU.subtract), name)
                    drained(v, name)
                elif name.startswith("solve"):
                    filled(v, name)
                    drain_done(nc.vector.tensor_tensor(inv, inv, blocks(name), ALU.subtract), name)
                    drained(v, name)
                elif name.startswith("score"):
                    moba_scores(name, n)
                elif name.startswith("pv"):
                    moba_outputs(name, n)
                elif name.startswith("v"):
                    new_values(n)
                elif name.startswith("inter"):
                    inter(n)
                elif name.startswith("state"):
                    next_state(n)
                elif name == "intra0":
                    drained(v, name)
                    add_inter(1)
                elif name == "intra1":
                    drained(v, name)
                    add_inter(2)
                    add_inter(3)
                    step(nc.vector.tensor_tensor(square[:, 0:8, :], o_gdn, o_gdn, ALU.mult))
                    step(nc.vector.tensor_reduce(sum16[:, 0:8], square[:, 0:8, :], AX.X, ALU.add))
                    nc.vector.tensor_scalar(r16[:, 0:8], sum16[:, 0:8], 1.0 / P, EPS, ALU.mult, ALU.add) \
                        .then_inc(S("gdn_mean"), 1)
            drained(v, "pv3")
            sq = m_pT.rearrange("p a b -> p (a b)")[:, 0:512]
            drained(v, "probs_T3")
            for t in range(TILES):
                step(nc.vector.tensor_tensor(sq, o_moba[:, t, :], o_moba[:, t, :], ALU.mult))
                step(nc.vector.tensor_reduce(sum16[:, 8 + t:9 + t], sq, AX.X, ALU.add))
            mean(sum16[:, 8:8 + TILES], ss, 512, "dve_step", steps["dve_step"], "moba_mean")
            drained(v, "gdn_z")
            invert(r16[:, 0:8], "gdn_root")
            step(nc.vector.tensor_tensor(o_gdn, o_gdn, spread(r16[:, 0:8], P), ALU.mult))
            nc.vector.tensor_tensor(o_gdn, o_gdn, z_sb, ALU.mult).then_inc(S("gdn_gated"), 1)
            invert(ss, "moba_root")
            normalise(o_moba, o_moba, ss, "moba_normed")
            filled(v, "gdn_oT")
            drain_done(nc.vector.tensor_scalar(oT[:, 4:8, :], pair("gdn_oT").rearrange("p (b n) -> p b n", n=SEQ),
                                               cols[:, ROWS["gdn"]:ROWS["gdn"] + 1], None, ALU.mult), "gdn_oT")
            filled(v, "moba_oT")
            drain_done(nc.vector.tensor_tensor(oT[:, 0:4, :], pair("moba_oT").rearrange("p (b n) -> p b n", n=SEQ),
                                               spread(cols[:, ROWS["moba"]:ROWS["moba"] + 4], SEQ), ALU.mult),
                       "moba_oT")

            def residual(name, t):
                filled(v, name)
                drain_done(nc.vector.tensor_tensor(x_sb[:, t, :], x_sb[:, t, :], pair(name), ALU.add), name)
                drained(v, name)

            for t in range(TILES):
                residual(f"mix_out{t}", t)
                tile_mean(t, "x1")
                tile_normed(t, "x1")
                gained_T(f"x_hT{t}", hT, t, "xattn")

            def x_largest(t):
                filled(v, f"x_score{t}")
                sc = pair(f"x_score{t}").rearrange("p (b n) -> p b n", n=SEQ)
                step(nc.vector.tensor_reduce(x_max[:, 4 * t:4 * t + 4], sc, AX.X, ALU.max))
                nc.vector.tensor_scalar(x_bias[:, 4 * t:4 * t + 4], x_max[:, 4 * t:4 * t + 4], -(P ** -0.5), None,
                                        ALU.mult).then_inc(S("x_bias_ready"), 1)

            def x_normed(t):
                drained(v, f"x_score{t}")
                step(nc.vector.reciprocal(x_inv[:, 4 * t:4 * t + 4], x_sum[:, 4 * t:4 * t + 4]))
                nc.vector.tensor_tensor(x_p[t], x_p[t], spread(x_inv[:, 4 * t:4 * t + 4], SEQ), ALU.mult) \
                    .then_inc(S("x_probs_ready"), 1)

            def x_turned(t):
                filled(v, f"x_probs_T{t}")
                drain_done(nc.vector.tensor_copy(x_pT[:, :, t * P:(t + 1) * P], blocks(f"x_probs_T{t}")),
                           f"x_probs_T{t}")

            x_largest(0)
            x_normed(0)
            x_largest(1)
            x_turned(0)
            x_normed(1)
            x_turned(1)

            def split_rest(t):
                v.wait_ge(S("split_high"), t + 1)
                v.wait_ge(S("x2_normed"), t + 1)
                nc.vector.tensor_tensor(remainder[:, t, :], xn[:, t, :], split[0][:, t, :], ALU.subtract) \
                    .then_inc(S("split_rest"), 1)

            def split_low(t):
                v.wait_ge(S("split_mid"), t + 1)
                nc.vector.tensor_tensor(split[2][:, t, :], remainder[:, t, :], split[1][:, t, :], ALU.subtract) \
                    .then_inc(S("split_low"), 1)

            def choose_experts(t):
                name = f"logits{t}"
                filled(v, name)
                drain_done(nc.vector.tensor_tensor(logits[:, t, :], pair(name)[:, 0:E], router_bias, ALU.add), name)
                drained(v, name)
                step(nc.vector.max(top8[:, t, :], logits[:, t, :]))
                nc.vector.tensor_scalar(top_bias[:, t:t + 1], top8[:, t, 0:1], -1.0, None, ALU.mult) \
                    .then_inc(S("top_bias_ready"), 1)
                step(nc.vector.max_index(top_i[:, t, :], top8[:, t, :], logits[:, t, :]))
                step(nc.vector.tensor_copy(top_f[:, t, :], top_i[:, t, :]))
                for j in range(TOPK):
                    ins = nc.vector.tensor_scalar(hit[:, TOPK * t + j, :], iota_e, top_f[:, t, j:j + 1], None,
                                                  ALU.is_equal)
                step(ins)
                step(nc.vector.tensor_reduce(chosen[:, t, :], hit[:, TOPK * t:TOPK * t + TOPK, :].rearrange(
                    "p j e -> p e j"), AX.X, ALU.add))
                nc.vector.tensor_copy(chosen_b[:, t, :], chosen[:, t, :]).then_inc(S("chosen_ready"), 1)

            residual("x_out0", 0)
            tile_mean(0, "x2")
            tile_normed(0, "x2")
            gained_T("f_T0", hT, 0, "ffn")
            residual("x_out1", 1)
            split_rest(0)
            tile_mean(1, "x2")
            tile_normed(1, "x2")
            v.wait_ge(S("router_loaded"), 32)
            v.wait_ge(S("iota_e_ready"), 1)
            choose_experts(0)
            gained_T("f_T1", hT, 1, "ffn")
            split_low(0)
            split_rest(1)
            choose_experts(1)
            split_low(1)
            step(nc.vector.memset(slot_m[:, :, E:E + 2], 0.0))
            filled(v, "slots")
            drain_done(nc.vector.scalar_tensor_tensor(
                slot_m[:, :, 0:E], pair("slots")[:, 0:TILES * E].rearrange("p (t e) -> p t e", e=E), 1.0, chosen,
                ALU.add, ALU.mult), "slots")
            drained(v, "slots")
            step(nc.vector.tensor_scalar(slot_m, slot_m, 1.0, None, ALU.subtract))

            def gates_and_count():
                v.wait_ge(S("top_exp"), TILES)
                step(nc.vector.memset(gates[:, :, E:E + 2], 0.0))
                step(nc.vector.reciprocal(top_s, top_s))
                step(nc.vector.tensor_tensor(top_w[:, :, 0:TOPK], top_e[:, :, 0:TOPK], spread(top_s, TOPK),
                                             ALU.mult))
                for j in range(TOPK):
                    for t in range(TILES):
                        if j == 0:
                            ins = nc.vector.tensor_scalar(gates[:, t, 0:E], hit[:, TOPK * t, :], top_w[:, t, 0:1],
                                                          None, ALU.mult)
                        else:
                            ins = nc.vector.scalar_tensor_tensor(
                                gates[:, t, 0:E], hit[:, TOPK * t + j, :], top_w[:, t, j:j + 1], gates[:, t, 0:E],
                                ALU.mult, ALU.add)
                    step(ins)
                filled(v, "count")
                drain_done(nc.vector.tensor_reduce(count_max, pair("count")[:, 0:E], AX.X, ALU.max), "count")
                drained(v, "count")
                nc.vector.tensor_copy(count_i, count_max).then_inc(S("count_ready"), 1)
                v.wait_ge(S("count_ready"), 1)
                return v.value_load(count_i[0:1, 0:1], min_val=0, max_val=SEQ)

            v.wait_ge(S("part_no_ready"), 3)
            v.wait_ge(S("iota_ready"), 1)

            def pick_pair(i):
                for k in range(2):
                    for t in range(TILES):
                        ins = nc.vector.tensor_scalar(pick[k][:, t, :], iota_s, slot_m[:, t, bass.ds(2 * i + k, 1)],
                                                      None, ALU.is_equal)
                ins.then_inc(S("picked"), 1)

            def pick_gated_pair(i):
                for t in range(TILES):
                    for q, k in enumerate((0, 1, 0)):
                        ins = nc.vector.tensor_scalar(
                            pick_gated[:, t, SLOTS * q:SLOTS * q + SLOTS], iota_s,
                            slot_m[:, t, bass.ds(2 * i + k, 1)], gates[:, t, bass.ds(2 * i + k, 1)],
                            ALU.is_equal, ALU.mult)
                ins.then_inc(S("gated_picked"), 1)

            def choose_pair(done):
                for k in range(2):
                    nc.vector.tensor_scalar(choose[0:96, k, :], part_no[0:96].to_broadcast([96, SLOTS]),
                                            expert_no[0:96], float(k), ALU.subtract, ALU.is_equal) \
                        .then_inc(S("expert_chosen"), 1)
                nc.vector.tensor_scalar(expert_no[0:96], expert_no[0:96], 2.0, None, ALU.add) \
                    .then_inc(S("expert_stepped"), 1)

            def gathered(k, n):
                v.wait_ge(S("gather_filled"), n)
                nc.vector.tensor_tensor(xg_T[k], bank(GATHER_BANK[k]).rearrange("p (b n) -> p b n", n=SLOTS),
                                        spread(cols[:, ROWS["ffn"]:ROWS["ffn"] + KB], SLOTS), ALU.mult) \
                    .then_inc(S("gathered"), 1)

            def swiglu(k, n):
                v.wait_ge(S("gate_up_filled"), n)
                v.wait_ge(S("act_T_filled"), n)
                nc.vector.tensor_scalar(gate_sb, bank(GATE_BANK[k]), LIMIT, None, ALU.min) \
                    .then_inc(S("gate_clipped"), 1)
                nc.vector.tensor_scalar(up_sb, bank(UP_BANK[k]), LIMIT, -LIMIT, ALU.min, ALU.max) \
                    .then_inc(S("up_clipped"), 1)
                v.wait_ge(S("gate_clipped"), n)
                v.wait_ge(S("up_clipped"), n)
                nc.vector.scalar_tensor_tensor(up_sb, up_sb, 1.0, gate_sb, ALU.add, ALU.mult) \
                    .then_inc(S("up_gated"), 1)
                v.wait_ge(S("up_gated"), n)
                v.wait_ge(S("gate_sigmoid"), n)
                nc.vector.tensor_tensor(up_sb, up_sb, sig_sb, ALU.mult).then_inc(S("act_ready"), 1)

            def expert_pass(r, before_gates):
                first = 2 * PICKS * r
                nc.vector.memset(expert_no[0:96], 0.0).then_inc(S("expert_reset"), 1)
                v.wait_ge(S("expert_reset"), r + 1)
                v.wait_ge(S("slots_moved"), r)
                pick_pair(0)
                most = before_gates()
                choose_pair(0)
                gathered(0, v.snap(first + 1))
                pick_gated_pair(0)
                gathered(1, v.snap(first + 2))
                with v.Fori(0, PAIRS) as i:
                    n = v.snap(r * E + 2 * i + 1)
                    m = v.snap(r * E + 2 * i + 2)
                    before = v.snap(r * PAIRS + i)
                    v.wait_ge(S("gated_T_filled"), before + 1)
                    nc.vector.tensor_copy(g_T, bank(GATED_BANK).rearrange("p (a b) -> p a b", b=SEQ)) \
                        .then_inc(S("gated_T_ready"), 1)
                    swiglu(0, n)
                    swiglu(1, m)
                    pick_pair(i + 1)
                    pick_gated_pair(i + 1)
                    v.wait_ge(S("down_filled"), m)
                    nc.vector.tensor_copy(y_sb, ps[:, 512 * Y_BANK:512 * Y_BANK + 1024].rearrange(
                        "p (a b) -> p a b", b=512)).then_inc(S("y_ready"), 1)
                    for k, t in enumerate((1, 0)):
                        v.wait_ge(S("combine_filled"), 2 * before + k + 1)
                        b = COMBINE_BANK[t]
                        nc.vector.tensor_tensor(x_sb[:, t, :], x_sb[:, t, :], ps[:, 512 * b:512 * b + 1024],
                                                ALU.add).then_inc(S("combined"), 1)
                        v.wait_ge(S("combined"), 2 * before + k + 2)
                    v.wait_ge(S("expert_stepped"), PICKS * r + i + 1)
                    choose_pair(i + 1)
                    gathered(0, v.snap(first + 2 * i + 3))
                    gathered(1, v.snap(first + 2 * i + 4))
                v.wait_ge(S("expert_stepped"), PICKS * r + PICKS)
                nc.vector.tensor_scalar(slot_m, slot_m, float(SLOTS), None, ALU.subtract) \
                    .then_inc(S("slots_moved"), 1)
                return most

            v.sem_inc(S("y_ready"), 1)
            v.sem_inc(S("combined"), 1)
            most = expert_pass(0, gates_and_count)
            with v.If(most > SLOTS):
                with v.Fori(1, PASSES) as r:
                    with v.If(most > r * SLOTS):
                        expert_pass(r, lambda: None)
            nc.vector.memset(count_max, 0.0).then_inc(S("x_final"), 1)
            for t in range(TILES):
                tile_mean(t, "x3")
            v.wait_ge(S("final_gain_loaded"), 16)
            for t in range(TILES):
                invert(rstd[:, t:t + 1], "x3_root", t + 1)
                nc.vector.scalar_tensor_tensor(out_sb[:, t, :], x_sb[:, t, :], rstd[:, t:t + 1], final_gain,
                                               ALU.mult, ALU.mult).then_inc(S("out_ready"), 1)

        @block.tensor
        def _(pe):
            def turn(name, dst, src, n_in=P):
                return nc.tensor.transpose(dst, src, ident[0:n_in, 0:n_in])

            def turn_tokens(name, src, after, count):
                take(pe, name)
                pe.wait_ge(S(after), count)
                t = int(name[-1])
                for k in range(KB):
                    last = turn(name, blocks(name)[:, k, :], src[:, t, k * P:(k + 1) * P])
                fill_done(last, name)

            def project_T(name, moving):
                take(pe, name)
                weights_landed(pe, name)
                w = weights(name).rearrange("p (k n) -> p k n", n=512)
                for b in range(4):
                    for k in range(KB):
                        last = nc.tensor.matmul(pair(name)[:, SEQ * b:SEQ * b + SEQ], w[:, k, b * P:(b + 1) * P],
                                                moving[:, k, :], start=(k == 0), stop=(k == KB - 1))
                return last

            def project(name, still):
                take(pe, name)
                weights_landed(pe, name)
                w = weights(name).rearrange("p (k n) -> p k n", n=512)
                for t in range(TILES):
                    for k in range(KB):
                        last = nc.tensor.matmul(halves(name)[:, t, :], still[:, k, t * P:(t + 1) * P], w[:, k, :],
                                                start=(k == 0), stop=(k == KB - 1))
                return last

            pe.wait_ge(S("ident_ready"), 1)
            take(pe, "const_cols")
            pe.wait_ge(S("rows_loaded"), 16 * len(ROWS))
            fill_done(turn("const_cols", pair("const_cols")[:, 0:N_ROWS], rows[0:N_ROWS, :], N_ROWS), "const_cols")
            for t in range(TILES):
                turn_tokens(f"x_T{t}", xn, "x_normed", t + 1)

            def projection(name, form, operand):
                last = form(name, operand)
                fill_done(last, name)
                filled(pe, name)
                pe.sem_inc(S(f"slot_free{W_ORDER.index(name) % RING}"), 1)

            for t in range(TILES):
                drained(pe, f"x_T{t}")
            for name in ("gdn_k", "gdn_q"):
                projection(name, project_T, hT)
            take(pe, "gdn_ba")
            pe.wait_ge(S("w_ba_loaded"), 16)
            for t in range(TILES):
                for k in range(KB):
                    last = nc.tensor.matmul(halves("gdn_ba")[:, t, 0:8], hT[:, k, t * P:(t + 1) * P], w_ba[:, k, :],
                                            start=(k == 0), stop=(k == KB - 1))
            fill_done(last, "gdn_ba")
            for t in range(TILES):
                turn_tokens(f"mem_T{t}", mem_sb, "memn_ready", t + 1)
            projection("gdn_v", project_T, hT)

            def to_tokens(n, name):
                take(pe, name)
                pe.wait_ge(S("conv_silu"), n + 1)
                for t in range(TILES):
                    for h in range(GH):
                        last = turn(name, blocks(name)[:, 4 * t + h, :], conv[:, 4 * n + h, t * P:(t + 1) * P])
                fill_done(last, name)

            to_tokens(0, "tok_k")
            to_tokens(1, "tok_q")
            for t in range(TILES):
                drained(pe, f"mem_T{t}")
            projection("mem_k", project_T, memT)
            to_tokens(2, "tok_v")
            pe.wait_ge(S("tri_ready"), 1)
            take(pe, "cum_g")
            pe.wait_ge(S("g_ready"), 1)
            fill_done(nc.tensor.matmul(pair("cum_g")[:, 0:8], tri, g_log, start=True, stop=True), "cum_g")

            def eight(name, product, n=8):
                take(pe, name)
                for b in range(n):
                    last = product(b, blocks(name)[:, b, :])
                fill_done(last, name)

            def mm(dst, still, moving):
                return nc.tensor.matmul(dst, still, moving, start=True, stop=True)

            pe.wait_ge(S("g_rep_ready"), 1)
            eight("row_g", lambda b, dst: mm(dst, g_rep[:, b, :], tri))
            pe.wait_ge(S("qk_normed"), 1)
            eight("k_T", lambda b, dst: turn("k_T", dst, tok_k[:, b, :]))
            eight("q_T", lambda b, dst: turn("q_T", dst, tok_q[:, b, :]))
            projection("mem_v", project, memT)
            drained(pe, "k_T")
            eight("kk", lambda b, dst: mm(dst, k_T[:, b, :], k_T[:, b, :]))
            drained(pe, "q_T")
            eight("qk", lambda b, dst: mm(dst, k_T[:, b, :], q_T[:, b, :]))

            def part(n):
                return slice(HALF * (n % 2), HALF * (n % 2) + HALF), 4 * (n // 2)

            def quarter(name, q):
                w = weights(name).rearrange("p (k n) -> p k n", n=512)
                if q == 0:
                    take(pe, name)
                    weights_landed(pe, name)
                for k in range(KB):
                    if name in ("moba_q", "moba_k"):
                        last = nc.tensor.matmul(pair(name)[:, SEQ * q:SEQ * q + SEQ], w[:, k, q * P:(q + 1) * P],
                                                hT[:, k, :], start=(k == 0), stop=(k == KB - 1))
                    else:
                        t, c = q // 2, 256 * (q % 2)
                        last = nc.tensor.matmul(halves(name)[:, t, c:c + 256], hT[:, k, t * P:(t + 1) * P],
                                                w[:, k, c:c + 256], start=(k == 0), stop=(k == KB - 1))
                if q == 3:
                    fill_done(last, name)

            def moba_score(name, n):
                take(pe, name)
                if n == 0:
                    drained(pe, "moba_k")
                for h in range(2):
                    q = mq_z[:, 2 * n + h, :]
                    mm(halves(name)[:, h, 0:P], q[:, 0:P], mk_T[:, n, 0:P])
                    last = mm(halves(name)[:, h, P:384], q[:, P:SEQ], mk_T[:, n, :])
                fill_done(last, name)

            def moba_probs_T(name, n):
                take(pe, name)
                pe.wait_ge(S("moba_exp"), n + 1)
                for h in range(2):
                    for b in range(3):
                        last = turn(name, halves(name)[:, h, P * b:P * b + P], m_p[:, h, P * b:P * b + P])
                fill_done(last, name)

            def moba_pv(name, n):
                take(pe, name)
                drained(pe, f"probs_T{n}")
                for h in range(2):
                    c = MHD * (2 * n + h)
                    o = slice(MHD * h, MHD * h + MHD)
                    mm(halves(name)[:, 0, o], m_pT[:, h, 0:P], mv_sb[:, 0, c:c + MHD])
                    nc.tensor.matmul(halves(name)[:, 1, o], m_pT[:, h, P:2 * P], mv_sb[:, 0, c:c + MHD],
                                     start=True, stop=False)
                    last = nc.tensor.matmul(halves(name)[:, 1, o], m_pT[:, h, 2 * P:384],
                                            mv_sb[:, 1, c:c + MHD], start=False, stop=True)
                fill_done(last, name)

            for name in MIDDLE:
                n = int(name[-1]) if name[-1].isdigit() else 0
                p, t0 = part(n)
                if "." in name:
                    quarter(name[:-2], n)
                    if n == 3:
                        filled(pe, name[:-2])
                        pe.sem_inc(S(f"slot_free{W_ORDER.index(name[:-2]) % RING}"), 1)
                elif name == "swap0":
                    pe.wait_ge(S("level_ready"), 1)
                    eight(name, lambda b, dst: mm(dst, level_l[:, b, :], ident))
                elif name.startswith("swap"):
                    pe.wait_ge(S("level_ready"), n + 1)
                    drained(pe, "swap0" if n == 1 else f"solve_T{n - 1}")
                    eight(name, lambda b, dst: mm(dst, level_l[:, b, :], inv_T[:, b, :]))
                elif name.startswith("solve_T"):
                    drained(pe, f"swap{n}")
                    if n == 1:
                        pe.wait_ge(S("solved"), 1)
                    else:
                        drained(pe, f"solve{n - 1}")
                    eight(name, lambda b, dst: mm(dst, inv[:, b, :], swap[:, b, :]))
                elif name.startswith("solve"):
                    eight(name, lambda b, dst: mm(dst, swap[:, b, :], inv[:, b, :]))
                elif name == "u":
                    drained(pe, f"solve_T{LEVELS - 1}")
                    pe.wait_ge(S("vb_ready"), 1)
                    eight(name, lambda b, dst: mm(dst, inv_T[:, b, :], tok_v[:, b, :]))
                elif name == "w_T":
                    pe.wait_ge(S("kbg_ready"), 1)
                    eight(name, lambda b, dst: mm(dst, kbg[:, b, :], inv_T[:, b, :]))
                elif name.startswith("state"):
                    pe.wait_ge(S("k_dec_ready"), 1)
                    drained(pe, "u" if n == 0 else f"v{n}")
                    eight(name, lambda b, dst: mm(dst, k_dec[p, t0 + b, :], u_sb[p, t0 + b, :]), GH)
                elif name.startswith("v"):
                    drained(pe, "w_T")
                    drained(pe, f"state{n - 1}")
                    eight(name, lambda b, dst: mm(dst[p], w_T[:, t0 + b, p], state[:, b, :]), GH)
                elif name.startswith("inter"):
                    eight(name, lambda b, dst: mm(dst[p], q_T[:, t0 + b, p], state[:, b, :]), GH)
                elif name.startswith("intra"):
                    drained(pe, f"v{2 * n + 1}")
                    eight(name, lambda b, dst: mm(dst, qk_T[:, 4 * n + b, :], u_sb[:, 4 * n + b, :]), GH)
                elif name.startswith("score"):
                    moba_score(name, n)
                elif name.startswith("probs_T"):
                    moba_probs_T(name, n)
                elif name.startswith("pv"):
                    moba_pv(name, n)

            def turn_out(name, src):
                take(pe, name)
                for b in range(4):
                    for t in range(TILES):
                        last = turn(name, pair(name)[:, SEQ * b + t * P:SEQ * b + (t + 1) * P], src(b, t))
                fill_done(last, name)

            pe.wait_ge(S("gdn_gated"), 1)
            turn_out("gdn_oT", lambda b, t: o_gdn[:, 4 * t + b, :])
            pe.wait_ge(S("moba_normed"), TILES)
            turn_out("moba_oT", lambda b, t: o_moba[:, t, b * P:(b + 1) * P])
            drained(pe, "moba_oT")
            drained(pe, "gdn_oT")
            weights_landed(pe, "out_a")
            weights_landed(pe, "out_b")

            def mix_out(t, between=None):
                name = f"mix_out{t}"
                take(pe, name)
                for half, w in enumerate(("out_a", "out_b")):
                    wv = weights(w).rearrange("p (k n) -> p k n", n=512)
                    for k in range(KB):
                        last = nc.tensor.matmul(halves(name)[:, half, :], oT[:, k, t * P:(t + 1) * P], wv[:, k, :],
                                                start=(k == 0), stop=(k == KB - 1))
                    if half == 0 and between:
                        between()
                fill_done(last, name)

            def x_turn(t):
                turn_tokens(f"x_hT{t}", xn, "x1_normed", t + 1)

            def x_query(t, between):
                name = f"x_q{t}"
                wv = weights("x_q").rearrange("p (k n) -> p k n", n=512)
                take(pe, name)
                drained(pe, f"x_hT{t}")
                for b in range(4):
                    for k in range(KB):
                        last = nc.tensor.matmul(blocks(name)[:, b, :], wv[:, k, b * P:(b + 1) * P],
                                                hT[:, k, t * P:(t + 1) * P], start=(k == 0), stop=(k == KB - 1))
                    if b == 2:
                        between()
                fill_done(last, name)

            def x_score(t):
                name = f"x_score{t}"
                take(pe, name)
                drained(pe, f"x_q{t}")
                for h in range(GH):
                    last = mm(pair(name)[:, SEQ * h:SEQ * h + SEQ], xq_T[:, h, t * P:(t + 1) * P], km_T[:, h, :])
                fill_done(last, name)

            def x_probs_turn(t):
                name = f"x_probs_T{t}"
                take(pe, name)
                pe.wait_ge(S("x_probs_ready"), t + 1)
                for h in range(GH):
                    for mt in range(TILES):
                        last = turn(name, blocks(name)[:, 2 * h + mt, :], x_p[t][:, h, mt * P:(mt + 1) * P])
                fill_done(last, name)

            def x_pv(t):
                name = f"x_pv{t}"
                drained(pe, f"x_probs_T{t}")
                take(pe, name)
                for h in range(GH):
                    for mt in range(TILES):
                        last = nc.tensor.matmul(blocks(name)[:, h, :], vm_sb[:, mt, h * P:(h + 1) * P],
                                                x_pT[:, 2 * h + mt, t * P:(t + 1) * P],
                                                start=(mt == 0), stop=(mt == TILES - 1))
                fill_done(last, name)

            def x_out(t, between):
                name = f"x_out{t}"
                wv = weights("x_o").rearrange("p (k n) -> p k n", n=D_MODEL)
                take(pe, name)
                drained(pe, f"x_pv{t}")
                for n in range(2 * GH):
                    half, h = n // GH, n % GH
                    if n in between:
                        between[n](1)
                    last = nc.tensor.matmul(halves(name)[:, half, :], oT[:, h, t * P:(t + 1) * P],
                                            wv[:, h, 512 * half:512 * half + 512],
                                            start=(h == 0), stop=(h == GH - 1))
                fill_done(last, name)

            def f_turn(t):
                turn_tokens(f"f_T{t}", xn, "x2_normed", t + 1)

            def router_logits(t):
                name = f"logits{t}"
                take(pe, name)
                drained(pe, f"f_T{t}")
                for k in range(KB):
                    last = nc.tensor.matmul(pair(name)[:, 0:E], hT[:, k, t * P:(t + 1) * P], router_sb[:, k, :],
                                            start=(k == 0), stop=(k == KB - 1))
                fill_done(last, name)

            mix_out(0)
            mix_out(1, lambda: x_turn(0))
            filled(pe, "mix_out1")
            for w in ("out_a", "out_b"):
                pe.sem_inc(S(f"slot_free{W_ORDER.index(w) % RING}"), 1)
            weights_landed(pe, "x_q")
            x_query(0, lambda: x_turn(1))
            drained(pe, "mem_k")
            x_query(1, lambda: x_score(0))
            x_score(1)
            filled(pe, "x_q1")
            pe.sem_inc(S(f"slot_free{W_ORDER.index('x_q') % RING}"), 1)
            drained(pe, "mem_v")
            x_probs_turn(0)
            x_pv(0)
            weights_landed(pe, "x_o")
            x_out(0, {2: x_probs_turn, 6: x_pv})
            x_out(1, {6: lambda t: f_turn(0)})
            filled(pe, "x_out1")
            pe.sem_inc(S(f"slot_free{W_ORDER.index('x_o') % RING}"), 1)
            pe.wait_ge(S("router_loaded"), 32)
            router_logits(0)
            f_turn(1)
            router_logits(1)
            pe.wait_ge(S("before_ready"), 2)
            pe.wait_ge(S("chosen_ready"), TILES)
            take(pe, "slots")
            mm(pair("slots")[:, 0:E], before, chosen_b[:, 0, :])
            nc.tensor.matmul(pair("slots")[:, E:2 * E], ones, chosen_b[:, 0, :], start=True, stop=False)
            fill_done(nc.tensor.matmul(pair("slots")[:, E:2 * E], before, chosen_b[:, 1, :],
                                       start=False, stop=True), "slots")
            take(pe, "count")
            for t in range(TILES):
                last = nc.tensor.matmul(pair("count")[:, 0:E], ones, chosen_b[:, t, :],
                                        start=(t == 0), stop=(t == TILES - 1))
            fill_done(last, "count")
            for name in ("f_T1", "logits1", "slots"):
                drained(pe, name)
            pe.wait_ge(S("split_low"), TILES)

            def gather(k, n):
                dst = bank(GATHER_BANK[k])
                for b in range(KB):
                    for s in range(3):
                        for t in range(TILES):
                            last = nc.tensor.matmul(dst[:, SLOTS * b:SLOTS * b + SLOTS],
                                                    split[s][:, t, b * P:(b + 1) * P], pick[k][:, t, :],
                                                    start=(s == 0 and t == 0), stop=(s == 2 and t == TILES - 1))
                last.then_inc(S("gather_filled"), 1)

            low, high = slice(0, HALF), slice(HALF, P)

            def gate_up(k, before):
                for c in range(4):
                    s, use = ring_use(4 * k + c)
                    pe.wait_ge(S(f"slot_loaded{s}"), 32 * before + 16 * (use + 1))
                    w = slot(s).rearrange("p (k n) -> p k n", n=2 * D_MODEL)
                    for kk in range(2):
                        kb = 2 * c + kk
                        for q, (b, p) in enumerate(((GATE_BANK[k], low), (GATE_BANK[k], high),
                                                    (UP_BANK[k], low), (UP_BANK[k], high))):
                            last = nc.tensor.matmul(bank(b)[p], xg_T[k][:, kb, :], w[:, kk, 512 * q:512 * q + 512],
                                                    start=(kb == 0), stop=False)
                    last.then_inc(S(f"slot_free{s}"), 1)
                for q, (b, p) in enumerate(((GATE_BANK[k], low), (GATE_BANK[k], high),
                                            (UP_BANK[k], low), (UP_BANK[k], high))):
                    last = nc.tensor.matmul(bank(b)[p], choose[0:96, k, :], bias_hi[0:96, 512 * q:512 * q + 512],
                                            start=False, stop=True)
                last.then_inc(S("gate_up_filled"), 1)

            def act_turned(k, n):
                pe.wait_ge(S("act_ready"), n)
                for b in range(4):
                    last = turn("", bank(ACT_T_BANK[k])[:, P * b:P * b + P], up_sb[:, P * b:P * b + P])
                last.then_inc(S("act_T_filled"), 1)

            def down(k, n, before):
                pe.wait_ge(S("act_T_ready"), n)
                places = ((0, low), (1, high)) if k == 0 else ((0, high), (1, low))
                for c in range(2):
                    s, use = ring_use(8 + 2 * k + c)
                    pe.wait_ge(S(f"slot_loaded{s}"), 32 * before + 16 * (use + 1))
                    w = slot(s).rearrange("p (k n) -> p k n", n=D_MODEL)
                    for b in range(4):
                        for q, (y, p) in enumerate(places):
                            last = nc.tensor.matmul(bank(Y_BANK + y)[p], act_T[:, b, HALF * c:HALF * c + HALF],
                                                    w[:, b, 512 * q:512 * q + 512],
                                                    start=(c == 0 and b == 0), stop=False)
                    last.then_inc(S(f"slot_free{s}"), 1)
                for q, (y, p) in enumerate(places):
                    last = nc.tensor.matmul(bank(Y_BANK + y)[p], choose[0:96, k, :],
                                            bias_hi[0:96, 2048 + 512 * q:2560 + 512 * q], start=False, stop=True)
                last.then_inc(S("down_filled"), 1)

            def expert_pass(r):
                pe.wait_ge(S("picked"), PICKS * r + 1)
                gather(0, 0)
                gather(1, 0)
                drained(pe, "count")
                pe.wait_ge(S("count_ready"), 1)
                pe.wait_ge(S("biases_ready"), 1)
                with pe.Fori(0, PAIRS) as i:
                    before = pe.snap(r * PAIRS + i)
                    n = pe.snap(r * E + 2 * i + 1)
                    m = pe.snap(r * E + 2 * i + 2)
                    pe.wait_ge(S("gathered"), 2 * PICKS * r + 2 * i + 1)
                    pe.wait_ge(S("expert_chosen"), 2 * PICKS * r + 2 * i + 2)
                    pe.wait_ge(S("combined"), 2 * before + 1)
                    gate_up(0, before)
                    pe.wait_ge(S("gated_picked"), PICKS * r + i + 1)
                    pe.wait_ge(S("y_ready"), before + 1)
                    for o in range(2):
                        for t in range(TILES):
                            last = turn("", bank(GATED_BANK)[:, SEQ * o + P * t:SEQ * o + P * t + P],
                                        pick_gated[:, t, HALF * o:HALF * o + P])
                    last.then_inc(S("gated_T_filled"), 1)
                    pe.wait_ge(S("gathered"), 2 * PICKS * r + 2 * i + 2)
                    gate_up(1, before)
                    act_turned(0, n)
                    pe.wait_ge(S("gated_T_ready"), before + 1)
                    down(0, n, before)
                    act_turned(1, m)
                    down(1, m, before)
                    pe.wait_ge(S("y_ready"), before + 2)
                    for t in (1, 0):
                        b = COMBINE_BANK[t]
                        for q in range(2):
                            last = nc.tensor.matmul(bank(b + q), g_T[:, q, P * t:P * t + P], y_sb[:, q, :],
                                                    start=True, stop=True)
                        last.then_inc(S("combine_filled"), 1)
                    pe.wait_ge(S("picked"), PICKS * r + i + 2)
                    gather(0, 0)
                    gather(1, 0)

            pe.sem_inc(S("act_T_filled"), 1)
            expert_pass(0)
            most = pe.value_load(count_i[0:1, 0:1], min_val=0, max_val=SEQ)
            with pe.If(most > SLOTS):
                with pe.Fori(1, PASSES) as r:
                    with pe.If(most > r * SLOTS):
                        expert_pass(r)


_INS = ["x", "mem", "norm_mix_g", "w_in", "gdn_conv_w", "gdn_A_log", "gdn_dt_bias", "gdn_norm_g", "moba_norm_g",
        "w_out", "norm_xattn_g", "norm_mem_g", "xattn_w_q", "xattn_w_kv", "xattn_w_o", "norm_ffn_g", "router_w",
        "router_b", "w_gate_up", "b_gate_up", "w_down", "b_down", "final_norm_g"]
_OUTS = [((1, SEQ, D_MODEL), "float32")]


def kernel(**inputs):
    import concourse.bacc as bacc
    from concourse.bass_utils import run_bass_kernel_spmd

    nc = bacc.Bacc("TRN2", target_bir_lowering=False, num_devices=1)
    arrays, args = {}, []
    for name in _INS:
        a = np.ascontiguousarray(inputs[name])
        arrays[f"in_{name}"] = a
        args.append(nc.dram_tensor(f"in_{name}", a.shape, mybir.dt.from_np(a.dtype), kind="ExternalInput").ap())
    for i, (shape, dtype) in enumerate(_OUTS):
        args.append(nc.dram_tensor(f"out_{i}", shape, mybir.dt.from_np(np.dtype(dtype)), kind="ExternalOutput").ap())
    bass_hybrid_block(nc, *args)
    r = run_bass_kernel_spmd(nc, [arrays], core_ids=[0])
    return r.results[0]["out_0"]
```

```python
from contextlib import ExitStack

import numpy as np

import concourse.bass as bass
from concourse import mybir

F32 = mybir.dt.float32
BF16 = mybir.dt.bfloat16
I32 = mybir.dt.int32
U32 = mybir.dt.uint32
ALU = mybir.AluOpType
ACT = mybir.ActivationFunctionType
AX = mybir.AxisListType

P = 128
HALF = 64
D_MODEL = 1024
SEQ = 256
TILES = SEQ // P
KB = D_MODEL // P
GH = 4
MH = 8
MHD = 64
LEVELS = 6
E = 32
TOPK = 4
SLOTS = 64
PASSES = SEQ // SLOTS
PAIRS = E // 2
RING = 6
SLOT = 4096
PAIR_CHUNKS = 12
EPS = 1e-6
NEG = -1.0e30
LIMIT = 7.0
GATHER_BANK, GATED_BANK, GATE_BANK, UP_BANK, ACT_T_BANK, Y_BANK = (0, 5), 6, (1, 3), (2, 4), (0, 5), 6
COMBINE_BANK = {1: 1, 0: 3}
ALPHA = 1.702

W_ORDER = ["gdn_k", "gdn_q", "gdn_v", "mem_k", "moba_v", "moba_q", "moba_k", "gdn_z", "mem_v",
           "out_a", "out_b", "x_q", "x_o"]
PRE = len(W_ORDER)

ROWS = {"mix": 0, "mem": 8, "xattn": 16, "ffn": 24, "moba": 32, "gdn": 36, "conv": 37}
N_ROWS = 37 + 4 * 12

EARLY = [("const_cols", 3), ("x_T0", 0), ("x_T1", 1), ("gdn_k", 2), ("gdn_ba", 3), ("gdn_q", 0), ("mem_T0", 1),
         ("tok_k", 3), ("mem_T1", 2), ("gdn_v", 3), ("tok_q", 1), ("cum_g", 2), ("row_g", 0), ("mem_k", 2),
         ("k_T", 1), ("q_T", 0), ("kk", 1), ("qk", 0), ("tok_v", 3)]
MIDDLE = ["swap0", "moba_v.0", "swap1", "moba_v.1", "solve_T1", "solve1", "moba_v.2", "swap2", "moba_v.3", "solve_T2",
          "solve2", "moba_q.0", "swap3", "moba_q.1", "solve_T3", "solve3", "moba_q.2", "swap4", "moba_q.3",
          "solve_T4", "solve4", "moba_k.0", "moba_k.1", "swap5", "moba_k.2", "solve_T5", "moba_k.3", "u",
          "w_T", "score0", "state0", "gdn_z.0", "v1", "inter1", "probs_T0", "state1", "gdn_z.1", "pv0",
          "intra0", "score1", "v2", "inter2", "gdn_z.2", "state2", "gdn_z.3", "probs_T1", "pv1", "score2",
          "v3", "inter3", "mem_v.0", "intra1", "probs_T2", "score3", "mem_v.1", "pv2", "probs_T3", "pv3",
          "mem_v.2", "gdn_oT", "mem_v.3", "moba_oT"]
LATE = ["mix_out0", "mix_out1", "x_hT0", "x_q0", "x_hT1", "x_q1", "x_score0", "x_score1", "x_probs_T0", "x_pv0",
        "x_out0", "x_probs_T1", "x_pv1", "x_out1", "f_T0", "logits0", "f_T1", "logits1", "slots", "count"]


def lay_out_jobs():
    jobs, chain = list(EARLY), 1
    for name in MIDDLE:
        base, _, quarter = name.partition(".")
        if quarter:
            if quarter == "0":
                jobs.append((base, 3))
        elif base.startswith(("score", "probs_T", "pv")):
            jobs.append((base, 2))
        else:
            jobs.append((base, chain % 2))
            chain += 1
    jobs += [(name, (n + 2) % 4) for n, name in enumerate(LATE)]
    uses, placed = [0] * 4, {}
    for name, p in jobs:
        placed[name] = (p, uses[p])
        uses[p] += 1
    return placed


JOBS = lay_out_jobs()


def bass_hybrid_block(nc, x, mem, norm_mix_g, w_in, gdn_conv_w, gdn_A_log, gdn_dt_bias, gdn_norm_g,
                      moba_norm_g, w_out, norm_xattn_g, norm_mem_g, xattn_w_q, xattn_w_kv, xattn_w_o,
                      norm_ffn_g, router_w, router_b, w_gate_up, b_gate_up, w_down, b_down, final_norm_g, out):
    with ExitStack() as ctx:
        sems = {}

        def S(name):
            if name not in sems:
                sems[name] = ctx.enter_context(nc.semaphore(name))
            return sems[name]

        ring = ctx.enter_context(nc.sbuf_tensor("ring", [P, RING * SLOT], F32))
        work = ctx.enter_context(nc.sbuf_tensor("work", [P, 27136], F32))
        small = ctx.enter_context(nc.sbuf_tensor("small", [P, 1440], F32))

        def area(at, *dims):
            n = int(np.prod(dims))
            v = work[:, at:at + n]
            if len(dims) == 2:
                return v.rearrange("p (a b) -> p a b", b=dims[1])
            if len(dims) == 3:
                return v.rearrange("p (a b c) -> p a b c", b=dims[1], c=dims[2])
            return v

        X, HT, M1, M2, M3, TOK, ZZ = 0, 2048, 4096, 8192, 10240, 13312, 16384
        QKT, MQ, MK, MV, OM, KM, VM, PP, PT = 17408, 18432, 20480, 21504, 22528, 23552, 24576, 25600, 26368
        x_sb = area(X, TILES, D_MODEL)
        hT = area(HT, KB, SEQ)
        oT = area(HT, KB, SEQ)
        mem_sb = area(M1, TILES, D_MODEL)
        memT = area(M1 + 2048, KB, SEQ)
        a_mat = area(M1, 8, P)
        level_l = area(M1 + 1024, 8, P)
        inv = area(M3, 8, P)
        inv_T = area(TOK, 8, P)
        decay_T = area(MK, 8, P)
        decay = area(OM, 8, P)
        u_sb = area(M1, 8, P)
        w_T = area(M1 + 1024, 8, P)
        square = area(M2, 16, P)
        g_rep = area(M2, 8, P)
        kbg = area(M2, 8, P)
        k_dec = area(M2 + 1024, 8, P)
        xn = area(M3, TILES, D_MODEL)
        conv = area(M3, 12, SEQ)
        k_T = area(M3, 8, P)
        q_T = area(M3 + 1024, 8, P)
        swap = area(M3 + 2048, 8, P)
        state = area(M3 + 2048, 4, P)
        o_tmp = area(M3 + 2560, 4, P)
        tok = area(TOK, 24, P)
        tok_k, tok_q, tok_v = tok[:, 0:8, :], tok[:, 8:16, :], tok[:, 16:24, :]
        o_gdn = tok_q
        rows = area(ZZ, P)
        z_sb = area(ZZ, 8, P)
        qk_T = area(QKT, 8, P)
        mq_z = area(MQ, MH, SEQ)
        mk_T = area(MK, 4, SEQ)
        mv_sb = area(MV, TILES, 512)
        o_moba = area(OM, TILES, 512)
        km_T = area(KM, 4, SEQ)
        vm_sb = area(VM, TILES, 512)
        m_p = area(PP, 2, 384)
        m_pT = area(PT, 2, 384)
        xq_T = area(MK, 4, SEQ)
        x_p = [area(M2, 4, SEQ), area(M2 + 1024, 4, SEQ)]
        x_pT = area(M1, 8, SEQ)
        bias_raw = area(TOK, 3072)
        bias_hi = work[:, MV:MV + 1536].bitcast(BF16)
        bias_mid = work[:, PP:PP + 1536].bitcast(BF16)
        split = [work[:, MQ + 1024 * s:MQ + 1024 * s + 1024].bitcast(BF16).rearrange("p (a b) -> p a b", b=D_MODEL)
                 for s in range(3)]
        remainder = area(M2, TILES, D_MODEL)
        xg_T = [area(M3 + 512 * s, KB, SLOTS) for s in range(2)]
        act_T = area(M3 + 1024, 4, P)
        gate_sb = area(M3 + 1536, 512)
        up_sb = area(M3 + 2048, 512)
        sig_sb = area(M3 + 2560, 512)
        y_sb = area(HT, 2, 512)
        g_T = area(HT + 1024, 2, SEQ)
        pick_gated = area(HT + 1536, TILES, 3 * SLOTS)
        pick = [work[:, HT + 1920 + 64 * s:HT + 1984 + 64 * s].bitcast(BF16).rearrange("p (a b) -> p a b", b=SLOTS)
                for s in range(2)]
        extra = {6: area(TOK, SLOT), 7: area(M1, SLOT), 8: area(MV + 1536, SLOT)}
        final_gain = area(M1, D_MODEL)
        out_sb = area(M2, TILES, D_MODEL)

        at = [0]

        def tiny(n, dt=F32):
            w = n if dt == F32 or dt == I32 or dt == U32 else (n + 1) // 2
            v = small[:, at[0]:at[0] + w]
            at[0] += w
            return v if dt == F32 else v.bitcast(dt)

        ident = tiny(P)
        cols = tiny(N_ROWS)
        tri = tiny(P)
        causal = tiny(384, BF16).rearrange("p (a b) -> p a b", b=P)
        level_mask = tiny(LEVELS * P, BF16).rearrange("p (a b) -> p a b", b=P)
        w_ba = tiny(64).rearrange("p (a b) -> p a b", b=8)
        iota_s = tiny(SLOTS)
        before = tiny(P, BF16)
        ones = tiny(P, BF16)
        ss, rstd = tiny(TILES), tiny(TILES)
        mem_ss, mem_rstd = tiny(TILES), tiny(TILES)
        sum16, r16 = tiny(16), tiny(16)
        a_log, dt_bias = tiny(GH), tiny(GH)
        beta, g_log, g_cum, e_g, beta_eg, k_decay = (tiny(8) for _ in range(6))
        sp_v, sp_n, sp_e = tiny(8), tiny(8), tiny(8)
        e_last = tiny(16)
        m_max, m_bias, m_sum, m_inv = tiny(4), tiny(4), tiny(16), tiny(16)
        x_max, x_bias, x_sum, x_inv = tiny(8), tiny(8), tiny(8), tiny(8)
        expert_no, part_no = tiny(1), tiny(1)
        table_out = tiny(1)
        count_max, count_i = tiny(1), tiny(1, I32)
        rt = [QKT]

        def routing(*dims):
            n = int(np.prod(dims))
            v = area(rt[0], *dims)
            rt[0] += n
            return v

        logits = routing(TILES, E)
        top8 = routing(TILES, 8)
        top_i = routing(TILES * 8).bitcast(U32).rearrange("p (a b) -> p a b", b=8)
        top_f = routing(TILES, 8)
        top_bias = routing(TILES)
        top_e = routing(TILES, 8)
        top_s = routing(TILES)
        top_w = routing(TILES, 8)
        hit = routing(TILES * TOPK, E)
        gates = routing(TILES, E)
        chosen = routing(TILES, E)
        chosen_b = routing(TILES * E // 2).bitcast(BF16).rearrange("p (a b) -> p a b", b=E)
        slot_m = routing(TILES, E)
        iota_e = routing(E)
        router_sb = routing(KB, E)
        router_bias = routing(E)
        choose = routing(SLOTS).bitcast(BF16).rearrange("p (a b) -> p a b", b=SLOTS)

        def idx_tiles():
            b = M2
            return (work[:, b:b + 128].bitcast(I32), work[:, b + 128:b + 129].bitcast(I32),
                    work[:, b + 256:b + 384].bitcast(I32), work[:, b + 384:b + 390].bitcast(I32),
                    work[:, b + 400:b + 406].bitcast(I32), area(b + 512, P), area(b + 640, 6), area(b + 650, 6))

        ps = ctx.enter_context(nc.psum_tensor("ps", [P, 4096], F32))

        def bank(b):
            return ps[:, 512 * b:512 * b + 512]

        def pair(name):
            p = JOBS[name][0]
            return ps[:, p * 1024:(p + 1) * 1024]

        def blocks(name):
            return pair(name).rearrange("p (b n) -> p b n", n=P)

        def halves(name):
            return pair(name).rearrange("p (b n) -> p b n", n=512)

        def take(pe, name):
            p, use = JOBS[name]
            if use:
                pe.wait_ge(S(f"pair_drained{p}"), use)

        def fill_done(ins, name):
            ins.then_inc(S(f"pair_filled{JOBS[name][0]}"), 1)

        def filled(eng, name):
            p, use = JOBS[name]
            eng.wait_ge(S(f"pair_filled{p}"), use + 1)

        def drain_done(ins, name):
            ins.then_inc(S(f"pair_drained{JOBS[name][0]}"), 1)

        def drained(eng, name):
            p, use = JOBS[name]
            eng.wait_ge(S(f"pair_drained{p}"), use + 1)

        steps = {}

        def own(eng, ins, name):
            steps[name] = steps.get(name, 0) + 1
            ins.then_inc(S(name), 1)
            eng.wait_ge(S(name), steps[name])

        def spread(v, n):
            return v.unsqueeze(2).to_broadcast([v.shape[0], v.shape[1], n])

        def slot(s):
            return ring[:, s * SLOT:(s + 1) * SLOT]

        def weights(name):
            n = W_ORDER.index(name)
            return slot(n % RING)

        def weights_landed(pe, name):
            n = W_ORDER.index(name)
            pe.wait_ge(S(f"slot_loaded{n % RING}"), 16 * (n // RING + 1))

        FIRST_RING = PAIR_CHUNKS - len(extra)

        def chunk_place(c, first):
            if first and c in extra:
                return extra[c], f"extra_loaded{c}", None, 0
            if first:
                n = PRE + c - sum(e < c for e in extra)
            else:
                n = PRE + FIRST_RING + c - PAIR_CHUNKS
            return slot(n % RING), f"slot_loaded{n % RING}", f"slot_free{n % RING}", n // RING

        row = lambda v: v.rearrange("a (b n) -> (a b) n", n=P)
        block = ctx.enter_context(nc.Block())

        @block.sync
        def _(sp):
            wi = w_in[0].rearrange("(k p) n -> p k n", p=P)
            kv = xattn_w_kv[0].rearrange("(k p) n -> p k n", p=P)
            wo = w_out[0].rearrange("(k p) n -> p k n", p=P)
            source = {"moba_q": wi[:, :, 0:512], "moba_k": wi[:, :, 512:1024], "moba_v": wi[:, :, 1024:1536],
                      "gdn_q": wi[:, :, 1536:2048], "gdn_k": wi[:, :, 2048:2560], "gdn_v": wi[:, :, 2560:3072],
                      "gdn_z": wi[:, :, 3072:3584], "mem_k": kv[:, :, 0:512], "mem_v": kv[:, :, 512:1024],
                      "out_a": wo[:, :, 0:512], "out_b": wo[:, :, 512:1024],
                      "x_q": xattn_w_q[0].rearrange("(k p) n -> p k n", p=P),
                      "x_o": xattn_w_o[0].rearrange("(k p) n -> p k n", p=P)}
            for t in range(TILES):
                sp.dma_start(x_sb[:, t, :], x[0, t * P:(t + 1) * P, :]).then_inc(S(f"x_loaded{t}"), 16)
            for name, src in (("mix", row(norm_mix_g)), ("mem", row(norm_mem_g)), ("xattn", row(norm_xattn_g)),
                              ("ffn", row(norm_ffn_g)), ("moba", row(moba_norm_g)), ("gdn", gdn_norm_g),
                              ("conv", gdn_conv_w[0].rearrange("j (c p) -> (j c) p", p=P))):
                r = ROWS[name]
                sp.dma_start(rows[r:r + src.shape[0], :], src).then_inc(S("rows_loaded"), 16)
            for n, name in enumerate(W_ORDER):
                s = n % RING
                if n >= RING:
                    sp.wait_ge(S(f"slot_free{s}"), n // RING)
                src = source[name]
                sp.dma_start(slot(s).rearrange("p (k n) -> p k n", n=src.shape[2]), src) \
                    .then_inc(S(f"slot_loaded{s}"), 16)
                if n == 0:
                    sp.dma_start(w_ba, w_in[0, :, 3584:3592].rearrange("(k p) n -> p k n", p=P)) \
                        .then_inc(S("w_ba_loaded"), 16)
                    sp.dma_start(a_log, gdn_A_log[0].partition_broadcast(P)).then_inc(S("ab_loaded"), 16)
                    sp.dma_start(dt_bias, gdn_dt_bias[0].partition_broadcast(P)).then_inc(S("ab_loaded"), 16)
                    for t in range(TILES):
                        sp.dma_start(mem_sb[:, t, :], mem[0, t * P:(t + 1) * P, :]) \
                            .then_inc(S(f"mem_loaded{t}"), 16)

            def load_pair(i, before, first=False):
                gu = [w_gate_up[0, bass.ds(2 * i + k, 1)].rearrange("e (k p) n -> p (e k) n", p=P) for k in range(2)]
                dn = [w_down[0, bass.ds(2 * i + k, 1)].rearrange("e (k p) n -> p (e k) n", p=P) for k in range(2)]
                for c in (0, 1, 2, 3, 6, 4, 7, 8, 5, 9, 10, 11) if first else range(PAIR_CHUNKS):
                    dst, loaded, free, use = chunk_place(c, first)
                    if c < 8:
                        src = gu[c // 4][:, 2 * (c % 4):2 * (c % 4) + 2, :]
                    else:
                        src = dn[(c - 8) // 2][:, 4 * (c % 2):4 * (c % 2) + 4, :]
                    if free:
                        sp.wait_ge(S(free), 2 * before + use)
                    else:
                        sp.wait_ge(S("biases_ready"), 1)
                        if c > min(extra):
                            drained(sp, "x_pv1")
                    sp.dma_start(dst.rearrange("p (k n) -> p k n", n=src.shape[2]), src).then_inc(S(loaded), 16)

            load_pair(0, 0, first=True)
            with sp.Fori(1, PAIRS) as i:
                load_pair(i, i)
            sp.wait_ge(S("count_ready"), 1)
            most = sp.value_load(count_i[0:1, 0:1], min_val=0, max_val=SEQ)
            with sp.If(most > SLOTS):
                with sp.Fori(1, PASSES) as r:
                    with sp.If(most > r * SLOTS):
                        with sp.Fori(0, PAIRS) as i:
                            load_pair(i, sp.snap(r * PAIRS + i))
            for t in range(TILES):
                sp.wait_ge(S("out_ready"), t + 1)
                sp.dma_start(out[0, t * P:(t + 1) * P, :], out_sb[:, t, :]).then_inc(S("out_stored"), 16)
            sp.wait_ge(S("out_stored"), 16 * TILES)

        @block.gpsimd
        def _(pool):
            p_row, p_col = idx_tiles()[0:2]
            own(pool, nc.gpsimd.memset(ident, 0.0), "pool_step")
            nc.gpsimd.affine_select(out=ident, in_=ident, compare_op=ALU.not_equal, fill=1.0, base=0,
                                    pattern=[[-1, P]], channel_multiplier=1).then_inc(S("ident_ready"), 1)
            nc.gpsimd.iota(p_row, pattern=[[1, P]], base=0, channel_multiplier=0)
            nc.gpsimd.iota(p_col, pattern=[[0, 1]], base=0, channel_multiplier=1).then_inc(S("indices_ready"), 1)
            own(pool, nc.gpsimd.memset(tri, 1.0), "pool_step")
            own(pool, nc.gpsimd.affine_select(out=tri, in_=tri, compare_op=ALU.is_ge, fill=0.0, base=0,
                                              pattern=[[1, P]], channel_multiplier=-1), "pool_step")
            nc.gpsimd.memset(tri[0:HALF, HALF:P], 0.0).then_inc(S("tri_ready"), 1)
            own(pool, nc.gpsimd.memset(causal, 0.0), "pool_step")
            for b in (0, 2):
                nc.gpsimd.affine_select(out=causal[:, b, :], in_=causal[:, b, :], compare_op=ALU.is_ge,
                                        fill=NEG, base=0, pattern=[[-1, P]], channel_multiplier=1) \
                    .then_inc(S("causal_ready"), 1)
            nc.gpsimd.memset(mq_z, 0.0).then_inc(S("mq_zeroed"), 1)
            nc.gpsimd.iota(iota_s, pattern=[[1, SLOTS]], base=0, channel_multiplier=0,
                           allow_small_or_imprecise_dtypes=True).then_inc(S("iota_ready"), 1)
            own(pool, nc.gpsimd.memset(before, 1.0), "pool_step")
            nc.gpsimd.affine_select(out=before, in_=before, compare_op=ALU.is_gt, fill=0.0, base=0,
                                    pattern=[[1, P]], channel_multiplier=-1).then_inc(S("before_ready"), 1)
            nc.gpsimd.memset(ones, 1.0).then_inc(S("before_ready"), 1)
            drained(pool, "intra1")
            nc.gpsimd.iota(iota_e, pattern=[[1, E]], base=0, channel_multiplier=0,
                           allow_small_or_imprecise_dtypes=True).then_inc(S("iota_e_ready"), 1)
            pool.wait_ge(S("iota_e_ready"), 1)
            for s in range(3):
                nc.gpsimd.iota(part_no[32 * s:32 * s + 32], pattern=[[0, 1]], base=0, channel_multiplier=1,
                               allow_small_or_imprecise_dtypes=True).then_inc(S("part_no_ready"), 1)
                pool.wait_ge(S("part_no_ready"), s + 1)

        @block.scalar
        def _(act):
            def squares(src, junk, acc, t, name):
                nc.scalar.activation(junk, src[:, t, :], ACT.Square, accum_out=acc[:, t:t + 1]) \
                    .then_inc(S(name), 1)

            def root(v, after, count, name):
                act.wait_ge(S(after), count)
                nc.scalar.activation(v, v, ACT.Sqrt).then_inc(S(name), 1)

            def evacuate(name, dst, src):
                filled(act, name)
                drain_done(nc.scalar.copy(dst, src), name)

            by_tile = lambda v, t: v[:, t:t + 1]

            def load_table(func):
                own(act, nc.scalar.activation(table_out, ident[:, 0:1], func), "table_loaded")

            act.wait_ge(S("ident_ready"), 1)
            load_table(ACT.Sqrt)
            for t in range(TILES):
                act.wait_ge(S(f"x_loaded{t}"), 16)
                squares(x_sb, xn[:, t, :], ss, t, "x_squared")
                root(by_tile(rstd, t), "x_mean", t + 1, "x_root")
            act.wait_ge(S("ab_loaded"), 32)
            nc.scalar.activation(a_log, a_log, ACT.Exp).then_inc(S("rate_ready"), 1)
            for t in range(TILES):
                act.wait_ge(S(f"mem_loaded{t}"), 16)
                squares(mem_sb, tok[:, 8 * t:8 * t + 8, :].rearrange("p a b -> p (a b)"), mem_ss, t, "mem_squared")
            root(mem_rstd, "mem_mean", 1, "mem_root")

            def silu_conv(n, name):
                drained(act, name)
                c = conv[:, 4 * n:4 * n + 4, :]
                nc.scalar.activation(c, c, ACT.Silu).then_inc(S("conv_silu"), 1)

            silu_conv(0, "gdn_k")
            filled(act, "gdn_ba")
            ba = pair("gdn_ba").rearrange("p (t n) -> p t n", n=512)
            nc.scalar.activation(beta.rearrange("p (t n) -> p t n", n=GH), ba[:, :, 0:GH], ACT.Sigmoid) \
                .then_inc(S("beta_ready"), 1)
            act.wait_ge(S("softplus_arg"), 1)
            nc.scalar.activation(sp_e, sp_n, ACT.Exp).then_inc(S("softplus_exp"), 1)
            act.wait_ge(S("softplus_sum"), 1)
            nc.scalar.activation(sp_e, sp_e, ACT.Ln).then_inc(S("softplus_ln"), 1)
            evacuate("tok_k", tok_k, blocks("tok_k"))
            silu_conv(1, "gdn_q")
            evacuate("tok_q", tok_q, blocks("tok_q"))
            drained(act, "cum_g")
            nc.scalar.activation(e_g, g_cum, ACT.Exp).then_inc(S("e_g_ready"), 1)
            root(r16, "l2_sums", 1, "l2_root")
            evacuate("k_T", k_T, blocks("k_T"))
            evacuate("q_T", q_T, blocks("q_T"))
            act.wait_ge(S("decay_args"), 1)
            nc.scalar.activation(decay, decay, ACT.Exp, scale=-1.0).then_inc(S("decay_ready"), 1)
            nc.scalar.activation(decay_T, decay_T, ACT.Exp).then_inc(S("decay_ready"), 1)
            nc.scalar.activation(k_decay, k_decay, ACT.Exp).then_inc(S("decay_ready"), 1)
            nc.scalar.activation(e_last, e_last, ACT.Exp).then_inc(S("decay_ready"), 1)
            silu_conv(2, "gdn_v")
            evacuate("mem_k", km_T, pair("mem_k").rearrange("p (b n) -> p b n", n=SEQ))
            evacuate("tok_v", tok_v, blocks("tok_v"))

            def moba_probs(hp):
                act.wait_ge(S("moba_bias"), hp + 1)
                for h in range(2):
                    n = 2 * (2 * hp + h)
                    nc.scalar.activation(m_p[:, h, 0:P], m_p[:, h, 0:P], ACT.Exp, bias=m_bias[:, 2 * h:2 * h + 1],
                                         scale=MHD ** -0.5, accum_out=m_sum[:, n:n + 1])
                    last = nc.scalar.activation(m_p[:, h, P:384], m_p[:, h, P:384], ACT.Exp,
                                                bias=m_bias[:, 2 * h + 1:2 * h + 2], scale=MHD ** -0.5,
                                                accum_out=m_sum[:, n + 1:n + 2])
                last.then_inc(S("moba_exp"), 1)

            for name in MIDDLE:
                base = name.partition(".")[0]
                if name.startswith("score"):
                    moba_probs(int(name[-1]))
                elif name.startswith("probs_T"):
                    filled(act, name)
                    drain_done(nc.scalar.copy(m_pT, halves(name)[:, :, 0:384]), name)
                elif name.startswith("swap") and name != "swap0":
                    evacuate(name, swap, blocks(name))
                elif name == "moba_v.3":
                    evacuate(base, mv_sb, halves(base))
                elif name == "moba_q.3":
                    filled(act, base)
                    act.wait_ge(S("mq_zeroed"), 1)
                    mq4 = mq_z.rearrange("p (b h) n -> p b h n", h=2)
                    q4 = pair(base).rearrange("p (b n) -> p b n", n=SEQ)
                    nc.scalar.copy(mq4[0:HALF, :, 0, :], q4[0:HALF])
                    drain_done(nc.scalar.copy(mq4[HALF:P, :, 1, :], q4[HALF:P]), base)
                elif name == "moba_k.3":
                    evacuate(base, mk_T, pair(base).rearrange("p (b n) -> p b n", n=SEQ))
                elif name == "gdn_z.3":
                    filled(act, base)
                    drain_done(nc.scalar.activation(z_sb, blocks(base), ACT.Silu), base)
                elif name == "u":
                    evacuate("u", u_sb, blocks("u"))
                elif name == "w_T":
                    evacuate("w_T", w_T, blocks("w_T"))
                elif name == "intra0":
                    evacuate("intra0", o_gdn[:, 0:4, :], blocks("intra0")[:, 0:4, :])
                elif name == "intra1":
                    evacuate("intra1", o_gdn[:, 4:8, :], blocks("intra1")[:, 0:4, :])
            root(r16[:, 0:8], "gdn_mean", 1, "gdn_root")
            drained(act, "pv3")
            for t in range(TILES):
                squares(o_moba, work[:, PP + 512 * t:PP + 512 * t + 512], sum16[:, 8:8 + TILES], t, "moba_squared")
            root(ss, "moba_mean", 1, "moba_root")
            evacuate("mem_v", vm_sb, halves("mem_v"))
            drained(act, "gdn_oT")
            drained(act, "moba_oT")
            for s in range(3):
                act.dma_start(bias_raw[32 * s:32 * s + E, 0:2048], b_gate_up[0]).then_inc(S("bias_loaded"), 16)
                act.dma_start(bias_raw[32 * s:32 * s + E, 2048:3072], b_down[0]).then_inc(S("bias_loaded"), 16)
            act.dma_start(router_sb, router_w[0].rearrange("(k p) n -> p k n", p=P)).then_inc(S("router_loaded"), 16)
            act.dma_start(router_bias, router_b[0].partition_broadcast(P)).then_inc(S("router_loaded"), 16)
            act.wait_ge(S("bias_loaded"), 96)
            nc.scalar.copy(bias_hi[0:96, :], bias_raw[0:96, :]).then_inc(S("bias_high"), 1)
            for t in range(TILES):
                drained(act, f"mix_out{t}")
                squares(x_sb, xn[:, t, :], ss, t, "x1_squared")
                root(by_tile(rstd, t), "x1_mean", t + 1, "x1_root")
                if t == 0:
                    act.wait_ge(S("bias_rest"), 1)
                    nc.scalar.copy(bias_mid[0:96, :], bias_raw[0:96, :]).then_inc(S("bias_mid"), 1)
                    act.wait_ge(S("bias_mid"), 1)
                    nc.scalar.copy(bias_hi[32:64, :], bias_mid[32:64, :]).then_inc(S("bias_placed"), 1)
                    act.wait_ge(S("bias_rest"), 2)
                    nc.scalar.copy(bias_hi[64:96, :], bias_raw[64:96, :]).then_inc(S("biases_ready"), 1)
            load_table(ACT.Exp)
            for t in range(TILES):
                evacuate(f"x_q{t}", xq_T[:, :, t * P:(t + 1) * P], blocks(f"x_q{t}")[:, 0:4, :])
            for t in range(TILES):
                act.wait_ge(S("x_bias_ready"), t + 1)
                filled(act, f"x_score{t}")
                sc = pair(f"x_score{t}").rearrange("p (b n) -> p b n", n=SEQ)
                for h in range(GH):
                    last = nc.scalar.activation(x_p[t][:, h, :], sc[:, h, :], ACT.Exp,
                                                bias=x_bias[:, 4 * t + h:4 * t + h + 1], scale=P ** -0.5,
                                                accum_out=x_sum[:, 4 * t + h:4 * t + h + 1])
                drain_done(last, f"x_score{t}")
            load_table(ACT.Sqrt)
            for t in range(TILES):
                evacuate(f"x_pv{t}", oT[:, 0:4, t * P:(t + 1) * P], blocks(f"x_pv{t}")[:, 0:4, :])

            def split_high(t):
                act.wait_ge(S("x2_normed"), t + 1)
                nc.scalar.copy(split[0][:, t, :], xn[:, t, :]).then_inc(S("split_high"), 1)

            def split_mid(t):
                act.wait_ge(S("split_rest"), t + 1)
                nc.scalar.copy(split[1][:, t, :], remainder[:, t, :]).then_inc(S("split_mid"), 1)

            def top_exp(t):
                act.wait_ge(S("top_bias_ready"), t + 1)
                nc.scalar.activation(top_e[:, t, 0:TOPK], top8[:, t, 0:TOPK], ACT.Exp, bias=top_bias[:, t:t + 1],
                                     accum_out=top_s[:, t:t + 1]).then_inc(S("top_exp"), 1)

            for t in range(TILES):
                drained(act, f"x_out{t}")
                squares(x_sb, xn[:, t, :], ss, t, "x2_squared")
                root(by_tile(rstd, t), "x2_mean", t + 1, "x2_root")
                if t == 0:
                    split_high(0)
            split_mid(0)
            split_high(1)
            top_exp(0)
            split_mid(1)
            top_exp(1)

            def expert(n, b):
                act.wait_ge(S("gate_clipped"), n)
                nc.scalar.activation(sig_sb, gate_sb, ACT.Sigmoid, scale=ALPHA).then_inc(S("gate_sigmoid"), 1)
                act.wait_ge(S("act_T_filled"), n + 1)
                nc.scalar.copy(act_T, bank(b).rearrange("p (b n) -> p b n", n=P)).then_inc(S("act_T_ready"), 1)

            def expert_pairs(base):
                with act.Fori(0, PAIRS) as i:
                    expert(act.snap(base + 2 * i + 1), ACT_T_BANK[0])
                    expert(act.snap(base + 2 * i + 2), ACT_T_BANK[1])

            act.wait_ge(S("count_ready"), 1)
            most = act.value_load(count_i[0:1, 0:1], min_val=0, max_val=SEQ)
            expert_pairs(0)
            with act.If(most > SLOTS):
                with act.Fori(1, PASSES) as r:
                    with act.If(most > r * SLOTS):
                        expert_pairs(r * E)
            act.dma_start(final_gain, final_norm_g.partition_broadcast(P)).then_inc(S("final_gain_loaded"), 16)
            load_table(ACT.Sqrt)
            act.wait_ge(S("x_final"), 1)
            for t in range(TILES):
                squares(x_sb, out_sb[:, t, :], ss, t, "x3_squared")
                root(by_tile(rstd, t), "x3_mean", t + 1, "x3_root")

        @block.vector
        def _(v):
            def step(ins):
                own(v, ins, "dve_step")

            def mean(acc, dst, n, after, count, name):
                v.wait_ge(S(after), count)
                nc.vector.tensor_scalar(dst, acc, 1.0 / n, EPS, ALU.mult, ALU.add).then_inc(S(name), 1)

            def invert(dst, after, count=1):
                v.wait_ge(S(after), count)
                step(nc.vector.reciprocal(dst, dst))

            def tile_mean(t, tag):
                mean(ss[:, t:t + 1], rstd[:, t:t + 1], D_MODEL, f"{tag}_squared", t + 1, f"{tag}_mean")

            def tile_normed(t, tag):
                invert(rstd[:, t:t + 1], f"{tag}_root", t + 1)
                nc.vector.tensor_scalar(xn[:, t, :], x_sb[:, t, :], rstd[:, t:t + 1], None, ALU.mult) \
                    .then_inc(S(f"{tag}_normed"), 1)

            def normalise(dst, src, r, name):
                for t in range(TILES):
                    nc.vector.tensor_scalar(dst[:, t, :], src[:, t, :], r[:, t:t + 1], None, ALU.mult) \
                        .then_inc(S(name), 1)

            def gained_T(name, dst, t, gain):
                filled(v, name)
                drain_done(nc.vector.tensor_tensor(
                    dst[:, :, t * P:(t + 1) * P], blocks(name),
                    spread(cols[:, ROWS[gain]:ROWS[gain] + KB], P), ALU.mult), name)

            for t in range(TILES):
                tile_mean(t, "x")
                tile_normed(t, "x")
            filled(v, "const_cols")
            drain_done(nc.vector.tensor_copy(cols, pair("const_cols")[:, 0:N_ROWS]), "const_cols")
            drained(v, "const_cols")
            gained_T("x_T0", hT, 0, "mix")
            gained_T("x_T1", hT, 1, "mix")
            mean(mem_ss, mem_rstd, D_MODEL, "mem_squared", TILES, "mem_mean")
            invert(mem_rstd, "mem_root")
            normalise(mem_sb, mem_sb, mem_rstd, "memn_ready")

            v.wait_ge(S("indices_ready"), 1)
            p_row, p_col, j_sh, i_sh, i_bit, j_f, i_f, b_f = idx_tiles()
            for l in range(LEVELS):
                nc.vector.tensor_single_scalar(i_sh[:, l:l + 1], p_col, l, ALU.logical_shift_right) \
                    .then_inc(S("dve_step"), 1)
            steps["dve_step"] += LEVELS
            v.wait_ge(S("dve_step"), steps["dve_step"])
            step(nc.vector.tensor_single_scalar(i_bit, i_sh, 1, ALU.bitwise_and))
            nc.vector.tensor_copy(i_f, i_sh)
            step(nc.vector.tensor_copy(b_f, i_bit))
            for l in range(LEVELS):
                step(nc.vector.tensor_single_scalar(j_sh, p_row, l, ALU.logical_shift_right))
                step(nc.vector.tensor_copy(j_f, j_sh))
                step(nc.vector.tensor_scalar(j_f, j_f, i_f[:, l:l + 1], -1.0, ALU.subtract, ALU.is_equal))
                step(nc.vector.tensor_scalar(level_mask[:, l, :], j_f, b_f[:, l:l + 1], None, ALU.mult))

            def convolve(n, name):
                filled(v, name)
                src = pair(name).rearrange("p (b n) -> p b n", n=SEQ)
                for j in (3, 2, 1, 0):
                    back = 3 - j
                    for b in range(4):
                        blk = {"gdn_q": 0, "gdn_k": 4, "gdn_v": 8}[name] + b
                        c = ROWS["conv"] + 12 * j + blk
                        w = cols[:, c:c + 1]
                        dst = conv[:, 4 * n + b, back:SEQ]
                        if j == 3:
                            ins = nc.vector.tensor_scalar(dst, src[:, b, :], w, None, ALU.mult)
                        else:
                            ins = nc.vector.scalar_tensor_tensor(dst, src[:, b, 0:SEQ - back], w, dst,
                                                                 ALU.mult, ALU.add)
                        if b == 3 and j > 0:
                            step(ins)
                        elif b == 3:
                            drain_done(ins, name)

            convolve(0, "gdn_k")
            filled(v, "gdn_ba")
            ba = pair("gdn_ba").rearrange("p (t n) -> p t n", n=512)
            v.wait_ge(S("ab_loaded"), 32)
            v.wait_ge(S("beta_ready"), 1)
            t8 = lambda q: q.rearrange("p (t n) -> p t n", n=GH)
            over_t = lambda q: q.unsqueeze(1).to_broadcast([P, TILES, GH])
            drain_done(nc.vector.tensor_tensor(t8(sp_v), ba[:, :, GH:2 * GH], over_t(dt_bias), ALU.add), "gdn_ba")
            drained(v, "gdn_ba")
            nc.vector.scalar_tensor_tensor(sp_n, sp_v, -1.0, sp_v, ALU.mult, ALU.min).then_inc(S("softplus_arg"), 1)
            v.wait_ge(S("softplus_exp"), 1)
            nc.vector.tensor_scalar(sp_e, sp_e, 1.0, None, ALU.add).then_inc(S("softplus_sum"), 1)
            v.wait_ge(S("softplus_ln"), 1)
            step(nc.vector.scalar_tensor_tensor(sp_v, sp_v, 0.0, sp_e, ALU.max, ALU.add))
            v.wait_ge(S("rate_ready"), 1)
            nc.vector.scalar_tensor_tensor(t8(g_log), t8(sp_v), -1.0, over_t(a_log), ALU.mult, ALU.mult) \
                .then_inc(S("g_ready"), 1)
            v.wait_ge(S("g_ready"), 1)
            nc.vector.tensor_copy(g_rep, spread(g_log, P)).then_inc(S("g_rep_ready"), 1)
            convolve(1, "gdn_q")
            gained_T("mem_T0", memT, 0, "mem")
            gained_T("mem_T1", memT, 1, "mem")
            filled(v, "cum_g")
            drain_done(nc.vector.tensor_copy(g_cum, pair("cum_g")[:, 0:8]), "cum_g")
            drained(v, "cum_g")
            filled(v, "row_g")
            rg = blocks("row_g")
            nc.vector.tensor_tensor(k_decay[0:HALF].unsqueeze(2), rg[0:HALF, :, HALF - 1:HALF],
                                    g_cum[0:HALF].unsqueeze(2), ALU.subtract)
            nc.vector.tensor_tensor(k_decay[HALF:P].unsqueeze(2), rg[HALF:P, :, P - 1:P],
                                    g_cum[HALF:P].unsqueeze(2), ALU.subtract)
            nc.vector.tensor_copy(e_last.rearrange("p (a b) -> p a b", b=2), rg[:, :, HALF - 1:P:HALF])
            drain_done(nc.vector.tensor_tensor(decay, rg, spread(g_cum, P), ALU.subtract), "row_g")
            drained(v, "row_g")
            drained(v, "tok_k")
            drained(v, "tok_q")
            step(nc.vector.tensor_tensor(square, tok[:, 0:16, :], tok[:, 0:16, :], ALU.mult))
            step(nc.vector.tensor_reduce(sum16, square, AX.X, ALU.add))
            nc.vector.tensor_scalar(r16, sum16, EPS, None, ALU.add).then_inc(S("l2_sums"), 1)
            step(nc.vector.tensor_scalar(decay_T, decay, 0.0, None, ALU.min))
            nc.vector.tensor_scalar(decay, decay, 0.0, None, ALU.max).then_inc(S("decay_args"), 1)
            invert(r16, "l2_root")
            step(nc.vector.tensor_scalar(r16[:, 8:16], r16[:, 8:16], P ** -0.5, None, ALU.mult))
            nc.vector.tensor_tensor(tok[:, 0:16, :], tok[:, 0:16, :], spread(r16, P), ALU.mult) \
                .then_inc(S("qk_normed"), 1)
            convolve(2, "gdn_v")
            v.wait_ge(S("decay_ready"), 4)
            step(nc.vector.tensor_tensor(decay, decay, spread(beta, P), ALU.mult))
            filled(v, "kk")
            drain_done(nc.vector.tensor_tensor(a_mat, blocks("kk"), decay, ALU.mult), "kk")
            drained(v, "kk")

            def level_part(l):
                nc.vector.tensor_tensor(level_l, a_mat, level_mask[:, l, :].unsqueeze(1).to_broadcast([P, 8, P]),
                                        ALU.mult).then_inc(S("level_ready"), 1)

            level_part(0)
            v.wait_ge(S("tri_ready"), 1)
            v.wait_ge(S("qk_normed"), 1)
            v.wait_ge(S("e_g_ready"), 1)
            step(nc.vector.tensor_tensor(beta_eg, beta, e_g, ALU.mult))
            nc.vector.tensor_tensor(k_dec, tok_k, spread(k_decay, P), ALU.mult).then_inc(S("k_dec_ready"), 1)
            nc.vector.tensor_tensor(kbg, tok_k, spread(beta_eg, P), ALU.mult).then_inc(S("kbg_ready"), 1)
            step(nc.vector.tensor_tensor(decay_T, decay_T, tri.unsqueeze(1).to_broadcast([P, 8, P]), ALU.mult))
            filled(v, "qk")
            drain_done(nc.vector.tensor_tensor(qk_T, blocks("qk"), decay_T, ALU.mult), "qk")
            drained(v, "qk")
            v.wait_ge(S("k_dec_ready"), 1)
            v.wait_ge(S("kbg_ready"), 1)
            v.wait_ge(S("level_ready"), 1)
            eye = ident.unsqueeze(1).to_broadcast([P, 8, P])
            v.wait_ge(S("ident_ready"), 1)
            nc.vector.tensor_tensor(inv, eye, level_l, ALU.subtract).then_inc(S("solved"), 1)
            drained(v, "tok_v")
            nc.vector.tensor_tensor(tok_v, tok_v, spread(beta, P), ALU.mult).then_inc(S("vb_ready"), 1)
            v.wait_ge(S("causal_ready"), 2)

            def new_values(n):
                p = slice(HALF * (n % 2), HALF * (n % 2) + HALF)
                us = u_sb[p, 4 * (n // 2):4 * (n // 2) + 4, :]
                if n == 1:
                    drained(v, "u")
                filled(v, f"v{n}")
                drain_done(nc.vector.tensor_tensor(us, us, blocks(f"v{n}")[p, 0:4, :], ALU.subtract), f"v{n}")

            def next_state(n):
                if n:
                    t0 = 4 * (n // 2)
                    el = e_last.rearrange("p (a b) -> p a b", b=2)[:, t0:t0 + 4, n % 2]
                    step(nc.vector.tensor_tensor(state, state, spread(el, P), ALU.mult))
                    filled(v, f"state{n}")
                    drain_done(nc.vector.tensor_tensor(state, state, blocks(f"state{n}")[:, 0:4, :], ALU.add),
                               f"state{n}")
                else:
                    filled(v, "state0")
                    drain_done(nc.vector.tensor_copy(state, blocks("state0")[:, 0:4, :]), "state0")
                drained(v, f"state{n}")

            def inter(n):
                p = slice(HALF * (n % 2), HALF * (n % 2) + HALF)
                t0 = 4 * (n // 2)
                filled(v, f"inter{n}")
                drain_done(nc.vector.tensor_tensor(o_tmp[p], blocks(f"inter{n}")[p, 0:4, :],
                                                   spread(e_g[p, t0:t0 + 4], P), ALU.mult), f"inter{n}")
                drained(v, f"inter{n}")

            def add_inter(n):
                p = slice(HALF * (n % 2), HALF * (n % 2) + HALF)
                t0 = 4 * (n // 2)
                step(nc.vector.tensor_tensor(o_gdn[p, t0:t0 + 4, :], o_gdn[p, t0:t0 + 4, :], o_tmp[p], ALU.add))

            def moba_scores(name, n):
                filled(v, name)
                s3 = halves(name)[:, :, 0:384].rearrange("p h (b n) -> p h b n", n=P)
                p3 = m_p.rearrange("p h (b n) -> p h b n", n=P)
                if n:
                    drained(v, f"probs_T{n - 1}")
                for h in range(2):
                    ins = nc.vector.tensor_tensor(p3[:, h], s3[:, h], causal, ALU.add)
                drain_done(ins, name)
                drained(v, name)
                if n:
                    v.wait_ge(S("moba_exp"), n)
                nc.vector.tensor_reduce(m_max[:, 0:4:2], m_p[:, :, 0:P], AX.X, ALU.max)
                step(nc.vector.tensor_reduce(m_max[:, 1:4:2], m_p[:, :, P:384], AX.X, ALU.max))
                nc.vector.tensor_scalar(m_bias, m_max, -(MHD ** -0.5), None, ALU.mult).then_inc(S("moba_bias"), 1)

            def moba_outputs(name, n):
                v.wait_ge(S("moba_exp"), n + 1)
                step(nc.vector.reciprocal(m_inv[:, 4 * n:4 * n + 4], m_sum[:, 4 * n:4 * n + 4]))
                filled(v, name)
                for t in range(TILES):
                    dst = o_moba[:, t, P * n:P * n + P].rearrange("p (h d) -> p h d", d=MHD)
                    src = halves(name)[:, t, 0:P].rearrange("p (h d) -> p h d", d=MHD)
                    ins = nc.vector.tensor_tensor(dst, src, spread(m_inv[:, 4 * n + t:4 * n + 4:2], MHD), ALU.mult)
                drain_done(ins, name)

            for name in MIDDLE[:MIDDLE.index("gdn_oT")]:
                n = int(name[-1]) if name[-1].isdigit() else 0
                if name == "swap0":
                    filled(v, name)
                    drain_done(nc.vector.tensor_tensor(inv_T, eye, blocks(name), ALU.subtract), name)
                    v.wait_ge(S("solved"), 1)
                    level_part(1)
                    drained(v, name)
                elif name.startswith("swap"):
                    if n + 1 < LEVELS:
                        filled(v, name)
                        level_part(n + 1)
                elif name.startswith("solve_T"):
                    filled(v, name)
                    drain_done(nc.vector.tensor_tensor(inv_T, inv_T, blocks(name), ALU.subtract), name)
                    drained(v, name)
                elif name.startswith("solve"):
                    filled(v, name)
                    drain_done(nc.vector.tensor_tensor(inv, inv, blocks(name), ALU.subtract), name)
                    drained(v, name)
                elif name.startswith("score"):
                    moba_scores(name, n)
                elif name.startswith("pv"):
                    moba_outputs(name, n)
                elif name.startswith("v"):
                    new_values(n)
                elif name.startswith("inter"):
                    inter(n)
                elif name.startswith("state"):
                    next_state(n)
                elif name == "intra0":
                    drained(v, name)
                    add_inter(1)
                elif name == "intra1":
                    drained(v, name)
                    add_inter(2)
                    add_inter(3)
                if name == "score3":
                    step(nc.vector.tensor_tensor(square[:, 0:8, :], o_gdn, o_gdn, ALU.mult))
                    step(nc.vector.tensor_reduce(sum16[:, 0:8], square[:, 0:8, :], AX.X, ALU.add))
                    nc.vector.tensor_scalar(r16[:, 0:8], sum16[:, 0:8], 1.0 / P, EPS, ALU.mult, ALU.add) \
                        .then_inc(S("gdn_mean"), 1)
            drained(v, "gdn_z")
            invert(r16[:, 0:8], "gdn_root")
            step(nc.vector.tensor_tensor(o_gdn, o_gdn, spread(r16[:, 0:8], P), ALU.mult))
            mean(sum16[:, 8:8 + TILES], ss, 512, "moba_squared", TILES, "moba_mean")
            nc.vector.tensor_tensor(o_gdn, o_gdn, z_sb, ALU.mult).then_inc(S("gdn_gated"), 1)
            invert(ss, "moba_root")
            normalise(o_moba, o_moba, ss, "moba_normed")
            filled(v, "gdn_oT")
            drain_done(nc.vector.tensor_scalar(oT[:, 4:8, :], pair("gdn_oT").rearrange("p (b n) -> p b n", n=SEQ),
                                               cols[:, ROWS["gdn"]:ROWS["gdn"] + 1], None, ALU.mult), "gdn_oT")
            filled(v, "moba_oT")
            drain_done(nc.vector.tensor_tensor(oT[:, 0:4, :], pair("moba_oT").rearrange("p (b n) -> p b n", n=SEQ),
                                               spread(cols[:, ROWS["moba"]:ROWS["moba"] + 4], SEQ), ALU.mult),
                       "moba_oT")

            v.wait_ge(S("bias_high"), 1)
            nc.vector.tensor_tensor(bias_raw[0:96, :], bias_raw[0:96, :], bias_hi[0:96, :], ALU.subtract) \
                .then_inc(S("bias_rest"), 1)
            def residual(name, t):
                filled(v, name)
                drain_done(nc.vector.tensor_tensor(x_sb[:, t, :], x_sb[:, t, :], pair(name), ALU.add), name)
                drained(v, name)

            for t in range(TILES):
                residual(f"mix_out{t}", t)
                tile_mean(t, "x1")
                tile_normed(t, "x1")
                gained_T(f"x_hT{t}", hT, t, "xattn")
                if t == 0:
                    v.wait_ge(S("bias_mid"), 1)
                    nc.vector.tensor_tensor(bias_raw[0:96, :], bias_raw[0:96, :], bias_mid[0:96, :], ALU.subtract) \
                        .then_inc(S("bias_rest"), 1)

            def x_largest(t):
                filled(v, f"x_score{t}")
                sc = pair(f"x_score{t}").rearrange("p (b n) -> p b n", n=SEQ)
                step(nc.vector.tensor_reduce(x_max[:, 4 * t:4 * t + 4], sc, AX.X, ALU.max))
                nc.vector.tensor_scalar(x_bias[:, 4 * t:4 * t + 4], x_max[:, 4 * t:4 * t + 4], -(P ** -0.5), None,
                                        ALU.mult).then_inc(S("x_bias_ready"), 1)

            def x_normed(t):
                drained(v, f"x_score{t}")
                step(nc.vector.reciprocal(x_inv[:, 4 * t:4 * t + 4], x_sum[:, 4 * t:4 * t + 4]))
                nc.vector.tensor_tensor(x_p[t], x_p[t], spread(x_inv[:, 4 * t:4 * t + 4], SEQ), ALU.mult) \
                    .then_inc(S("x_probs_ready"), 1)

            def x_turned(t):
                filled(v, f"x_probs_T{t}")
                drain_done(nc.vector.tensor_copy(x_pT[:, :, t * P:(t + 1) * P], blocks(f"x_probs_T{t}")),
                           f"x_probs_T{t}")

            x_largest(0)
            x_normed(0)
            x_largest(1)
            x_turned(0)
            x_normed(1)
            x_turned(1)

            def split_rest(t):
                v.wait_ge(S("split_high"), t + 1)
                v.wait_ge(S("x2_normed"), t + 1)
                nc.vector.tensor_tensor(remainder[:, t, :], xn[:, t, :], split[0][:, t, :], ALU.subtract) \
                    .then_inc(S("split_rest"), 1)

            def split_low(t):
                v.wait_ge(S("split_mid"), t + 1)
                nc.vector.tensor_tensor(split[2][:, t, :], remainder[:, t, :], split[1][:, t, :], ALU.subtract) \
                    .then_inc(S("split_low"), 1)

            def choose_experts(t):
                name = f"logits{t}"
                filled(v, name)
                drain_done(nc.vector.tensor_tensor(logits[:, t, :], pair(name)[:, 0:E], router_bias, ALU.add), name)
                drained(v, name)
                step(nc.vector.max(top8[:, t, :], logits[:, t, :]))
                nc.vector.tensor_scalar(top_bias[:, t:t + 1], top8[:, t, 0:1], -1.0, None, ALU.mult) \
                    .then_inc(S("top_bias_ready"), 1)
                step(nc.vector.max_index(top_i[:, t, :], top8[:, t, :], logits[:, t, :]))
                step(nc.vector.tensor_copy(top_f[:, t, :], top_i[:, t, :]))
                for j in range(TOPK):
                    ins = nc.vector.tensor_scalar(hit[:, TOPK * t + j, :], iota_e, top_f[:, t, j:j + 1], None,
                                                  ALU.is_equal)
                step(ins)
                step(nc.vector.tensor_reduce(chosen[:, t, :], hit[:, TOPK * t:TOPK * t + TOPK, :].rearrange(
                    "p j e -> p e j"), AX.X, ALU.add))
                nc.vector.tensor_copy(chosen_b[:, t, :], chosen[:, t, :]).then_inc(S("chosen_ready"), 1)

            residual("x_out0", 0)
            tile_mean(0, "x2")
            tile_normed(0, "x2")
            gained_T("f_T0", hT, 0, "ffn")
            residual("x_out1", 1)
            split_rest(0)
            tile_mean(1, "x2")
            tile_normed(1, "x2")
            v.wait_ge(S("router_loaded"), 32)
            v.wait_ge(S("iota_e_ready"), 1)
            choose_experts(0)
            gained_T("f_T1", hT, 1, "ffn")
            split_low(0)
            split_rest(1)
            choose_experts(1)
            split_low(1)
            filled(v, "slots")
            drain_done(nc.vector.scalar_tensor_tensor(
                slot_m, pair("slots")[:, 0:TILES * E].rearrange("p (t e) -> p t e", e=E), 1.0, chosen,
                ALU.add, ALU.mult), "slots")
            drained(v, "slots")
            step(nc.vector.tensor_scalar(slot_m, slot_m, 1.0, None, ALU.subtract))

            def gates_and_count():
                v.wait_ge(S("top_exp"), TILES)
                step(nc.vector.reciprocal(top_s, top_s))
                step(nc.vector.tensor_tensor(top_w[:, :, 0:TOPK], top_e[:, :, 0:TOPK], spread(top_s, TOPK),
                                             ALU.mult))
                for j in range(TOPK):
                    for t in range(TILES):
                        if j == 0:
                            ins = nc.vector.tensor_scalar(gates[:, t, :], hit[:, TOPK * t, :], top_w[:, t, 0:1],
                                                          None, ALU.mult)
                        else:
                            ins = nc.vector.scalar_tensor_tensor(
                                gates[:, t, :], hit[:, TOPK * t + j, :], top_w[:, t, j:j + 1], gates[:, t, :],
                                ALU.mult, ALU.add)
                    step(ins)
                filled(v, "count")
                drain_done(nc.vector.tensor_reduce(count_max, pair("count")[:, 0:E], AX.X, ALU.max), "count")
                drained(v, "count")
                nc.vector.tensor_copy(count_i, count_max).then_inc(S("count_ready"), 1)
                v.wait_ge(S("count_ready"), 1)
                return v.value_load(count_i[0:1, 0:1], min_val=0, max_val=SEQ)

            v.wait_ge(S("part_no_ready"), 3)
            v.wait_ge(S("iota_ready"), 1)

            def pick_pair(i):
                for k in range(2):
                    for t in range(TILES):
                        ins = nc.vector.tensor_scalar(pick[k][:, t, :], iota_s, slot_m[:, t, bass.ds(2 * i + k, 1)],
                                                      None, ALU.is_equal)
                ins.then_inc(S("picked"), 1)

            def pick_gated_pair(i):
                for t in range(TILES):
                    for q, k in enumerate((0, 1, 0)):
                        ins = nc.vector.tensor_scalar(
                            pick_gated[:, t, SLOTS * q:SLOTS * q + SLOTS], iota_s,
                            slot_m[:, t, bass.ds(2 * i + k, 1)], gates[:, t, bass.ds(2 * i + k, 1)],
                            ALU.is_equal, ALU.mult)
                ins.then_inc(S("gated_picked"), 1)

            def choose_pair(done):
                for k in range(2):
                    nc.vector.tensor_scalar(choose[0:96, k, :], part_no[0:96].to_broadcast([96, SLOTS]),
                                            expert_no[0:96], float(k), ALU.subtract, ALU.is_equal) \
                        .then_inc(S("expert_chosen"), 1)
                nc.vector.tensor_scalar(expert_no[0:96], expert_no[0:96], 2.0, None, ALU.add) \
                    .then_inc(S("expert_stepped"), 1)

            def gathered(k, n):
                v.wait_ge(S("gather_filled"), n)
                nc.vector.tensor_tensor(xg_T[k], bank(GATHER_BANK[k]).rearrange("p (b n) -> p b n", n=SLOTS),
                                        spread(cols[:, ROWS["ffn"]:ROWS["ffn"] + KB], SLOTS), ALU.mult) \
                    .then_inc(S("gathered"), 1)

            def swiglu(k, n):
                v.wait_ge(S("gate_up_filled"), n)
                v.wait_ge(S("act_T_filled"), n)
                nc.vector.tensor_scalar(gate_sb, bank(GATE_BANK[k]), LIMIT, None, ALU.min) \
                    .then_inc(S("gate_clipped"), 1)
                nc.vector.tensor_scalar(up_sb, bank(UP_BANK[k]), LIMIT, -LIMIT, ALU.min, ALU.max) \
                    .then_inc(S("up_clipped"), 1)
                v.wait_ge(S("gate_clipped"), n)
                v.wait_ge(S("up_clipped"), n)
                nc.vector.scalar_tensor_tensor(up_sb, up_sb, 1.0, gate_sb, ALU.add, ALU.mult) \
                    .then_inc(S("up_gated"), 1)
                v.wait_ge(S("up_gated"), n)
                v.wait_ge(S("gate_sigmoid"), n)
                nc.vector.tensor_tensor(up_sb, up_sb, sig_sb, ALU.mult).then_inc(S("act_ready"), 1)

            def pair_of_experts(r, i, before, n, m, last):
                v.wait_ge(S("gated_T_filled"), before + 1)
                nc.vector.tensor_copy(g_T, bank(GATED_BANK).rearrange("p (a b) -> p a b", b=SEQ)) \
                    .then_inc(S("gated_T_ready"), 1)
                swiglu(0, n)
                swiglu(1, m)
                if not last:
                    pick_pair(i + 1)
                    pick_gated_pair(i + 1)
                v.wait_ge(S("down_filled"), m)
                nc.vector.tensor_copy(y_sb, ps[:, 512 * Y_BANK:512 * Y_BANK + 1024].rearrange(
                    "p (a b) -> p a b", b=512)).then_inc(S("y_ready"), 1)
                for k, t in enumerate((1, 0)):
                    v.wait_ge(S("combine_filled"), 2 * before + k + 1)
                    b = COMBINE_BANK[t]
                    nc.vector.tensor_tensor(x_sb[:, t, :], x_sb[:, t, :], ps[:, 512 * b:512 * b + 1024],
                                            ALU.add).then_inc(S("combined"), 1)
                    v.wait_ge(S("combined"), 2 * before + k + 2)
                if not last:
                    v.wait_ge(S("expert_stepped"), PAIRS * r + i + 1)
                    choose_pair(i + 1)
                    gathered(0, v.snap(E * r + 2 * i + 3))
                    gathered(1, v.snap(E * r + 2 * i + 4))

            def expert_pass(r, before_gates):
                first = E * r
                nc.vector.memset(expert_no[0:96], 0.0).then_inc(S("expert_reset"), 1)
                v.wait_ge(S("expert_reset"), r + 1)
                v.wait_ge(S("slots_moved"), r)
                pick_pair(0)
                most = before_gates()
                choose_pair(0)
                gathered(0, v.snap(first + 1))
                pick_gated_pair(0)
                gathered(1, v.snap(first + 2))
                with v.Fori(0, PAIRS - 1) as i:
                    pair_of_experts(r, i, v.snap(r * PAIRS + i), v.snap(r * E + 2 * i + 1),
                                    v.snap(r * E + 2 * i + 2), False)
                i = PAIRS - 1
                pair_of_experts(r, i, v.snap(r * PAIRS + i), v.snap(r * E + 2 * i + 1), v.snap(r * E + 2 * i + 2),
                                True)
                v.wait_ge(S("expert_stepped"), PAIRS * r + PAIRS)
                nc.vector.tensor_scalar(slot_m, slot_m, float(SLOTS), None, ALU.subtract) \
                    .then_inc(S("slots_moved"), 1)
                return most

            v.sem_inc(S("y_ready"), 1)
            v.sem_inc(S("combined"), 1)
            most = expert_pass(0, gates_and_count)
            with v.If(most > SLOTS):
                with v.Fori(1, PASSES) as r:
                    with v.If(most > r * SLOTS):
                        expert_pass(r, lambda: None)
            nc.vector.memset(count_max, 0.0).then_inc(S("x_final"), 1)
            v.wait_ge(S("final_gain_loaded"), 16)
            for t in range(TILES):
                tile_mean(t, "x3")
                invert(rstd[:, t:t + 1], "x3_root", t + 1)
                nc.vector.scalar_tensor_tensor(out_sb[:, t, :], x_sb[:, t, :], rstd[:, t:t + 1], final_gain,
                                               ALU.mult, ALU.mult).then_inc(S("out_ready"), 1)

        @block.tensor
        def _(pe):
            def turn(name, dst, src, n_in=P):
                return nc.tensor.transpose(dst, src, ident[0:n_in, 0:n_in])

            def turn_tokens(name, src, after, count):
                take(pe, name)
                pe.wait_ge(S(after), count)
                t = int(name[-1])
                for k in range(KB):
                    last = turn(name, blocks(name)[:, k, :], src[:, t, k * P:(k + 1) * P])
                fill_done(last, name)

            def project_T(name, moving, between=None):
                take(pe, name)
                weights_landed(pe, name)
                w = weights(name).rearrange("p (k n) -> p k n", n=512)
                for b in range(4):
                    for k in range(KB):
                        last = nc.tensor.matmul(pair(name)[:, SEQ * b:SEQ * b + SEQ], w[:, k, b * P:(b + 1) * P],
                                                moving[:, k, :], start=(k == 0), stop=(k == KB - 1))
                    if between and b in between:
                        between[b]()
                fill_done(last, name)
                filled(pe, name)
                pe.sem_inc(S(f"slot_free{W_ORDER.index(name) % RING}"), 1)

            pe.wait_ge(S("ident_ready"), 1)
            take(pe, "const_cols")
            pe.wait_ge(S("rows_loaded"), 16 * len(ROWS))
            fill_done(turn("const_cols", pair("const_cols")[:, 0:N_ROWS], rows[0:N_ROWS, :], N_ROWS), "const_cols")
            for t in range(TILES):
                turn_tokens(f"x_T{t}", xn, "x_normed", t + 1)

            for t in range(TILES):
                drained(pe, f"x_T{t}")

            def decay_inputs():
                take(pe, "gdn_ba")
                pe.wait_ge(S("w_ba_loaded"), 16)
                for t in range(TILES):
                    for k in range(KB):
                        last = nc.tensor.matmul(halves("gdn_ba")[:, t, 0:8], hT[:, k, t * P:(t + 1) * P],
                                                w_ba[:, k, :], start=(k == 0), stop=(k == KB - 1))
                fill_done(last, "gdn_ba")

            def to_tokens(n, name):
                take(pe, name)
                pe.wait_ge(S("conv_silu"), n + 1)
                for t in range(TILES):
                    for h in range(GH):
                        last = turn(name, blocks(name)[:, 4 * t + h, :], conv[:, 4 * n + h, t * P:(t + 1) * P])
                fill_done(last, name)

            def eight(name, product, n=8):
                take(pe, name)
                for b in range(n):
                    last = product(b, blocks(name)[:, b, :])
                fill_done(last, name)

            def mm(dst, still, moving):
                return nc.tensor.matmul(dst, still, moving, start=True, stop=True)

            def turn_memory(t):
                turn_tokens(f"mem_T{t}", mem_sb, "memn_ready", t + 1)

            def decay_sums():
                pe.wait_ge(S("tri_ready"), 1)
                take(pe, "cum_g")
                pe.wait_ge(S("g_ready"), 1)
                fill_done(nc.tensor.matmul(pair("cum_g")[:, 0:8], tri, g_log, start=True, stop=True), "cum_g")
                pe.wait_ge(S("g_rep_ready"), 1)
                eight("row_g", lambda b, dst: mm(dst, g_rep[:, b, :], tri))

            def queries_keys_turned():
                pe.wait_ge(S("qk_normed"), 1)
                eight("k_T", lambda b, dst: turn("k_T", dst, tok_k[:, b, :]))
                eight("q_T", lambda b, dst: turn("q_T", dst, tok_q[:, b, :]))

            def queries_keys_products():
                drained(pe, "k_T")
                eight("kk", lambda b, dst: mm(dst, k_T[:, b, :], k_T[:, b, :]))
                drained(pe, "q_T")
                eight("qk", lambda b, dst: mm(dst, k_T[:, b, :], q_T[:, b, :]))

            project_T("gdn_k", hT)
            decay_inputs()
            project_T("gdn_q", hT, {1: lambda: turn_memory(0), 2: lambda: to_tokens(0, "tok_k")})
            turn_memory(1)

            def sums_and_queries():
                to_tokens(1, "tok_q")
                decay_sums()

            project_T("gdn_v", hT, {1: sums_and_queries})
            for t in range(TILES):
                drained(pe, f"mem_T{t}")
            project_T("mem_k", memT, {1: queries_keys_turned, 2: queries_keys_products})
            to_tokens(2, "tok_v")

            def part(n):
                return slice(HALF * (n % 2), HALF * (n % 2) + HALF), 4 * (n // 2)

            def quarter(name, q):
                w = weights(name).rearrange("p (k n) -> p k n", n=512)
                tokens = memT if name == "mem_v" else hT
                if q == 0:
                    take(pe, name)
                    weights_landed(pe, name)
                for k in range(KB):
                    if name in ("moba_q", "moba_k"):
                        last = nc.tensor.matmul(pair(name)[:, SEQ * q:SEQ * q + SEQ], w[:, k, q * P:(q + 1) * P],
                                                hT[:, k, :], start=(k == 0), stop=(k == KB - 1))
                    else:
                        t, c = q // 2, 256 * (q % 2)
                        last = nc.tensor.matmul(halves(name)[:, t, c:c + 256], tokens[:, k, t * P:(t + 1) * P],
                                                w[:, k, c:c + 256], start=(k == 0), stop=(k == KB - 1))
                if q == 3:
                    fill_done(last, name)

            def moba_score(name, n):
                take(pe, name)
                if n == 0:
                    drained(pe, "moba_k")
                for h in range(2):
                    q = mq_z[:, 2 * n + h, :]
                    mm(halves(name)[:, h, 0:P], q[:, 0:P], mk_T[:, n, 0:P])
                    last = mm(halves(name)[:, h, P:384], q[:, P:SEQ], mk_T[:, n, :])
                fill_done(last, name)

            def moba_probs_T(name, n):
                take(pe, name)
                pe.wait_ge(S("moba_exp"), n + 1)
                for h in range(2):
                    for b in range(3):
                        last = turn(name, halves(name)[:, h, P * b:P * b + P], m_p[:, h, P * b:P * b + P])
                fill_done(last, name)

            def moba_pv(name, n):
                take(pe, name)
                drained(pe, f"probs_T{n}")
                for h in range(2):
                    c = MHD * (2 * n + h)
                    o = slice(MHD * h, MHD * h + MHD)
                    mm(halves(name)[:, 0, o], m_pT[:, h, 0:P], mv_sb[:, 0, c:c + MHD])
                    nc.tensor.matmul(halves(name)[:, 1, o], m_pT[:, h, P:2 * P], mv_sb[:, 0, c:c + MHD],
                                     start=True, stop=False)
                    last = nc.tensor.matmul(halves(name)[:, 1, o], m_pT[:, h, 2 * P:384],
                                            mv_sb[:, 1, c:c + MHD], start=False, stop=True)
                fill_done(last, name)

            def turn_out(name, src):
                take(pe, name)
                for b in range(4):
                    for t in range(TILES):
                        last = turn(name, pair(name)[:, SEQ * b + t * P:SEQ * b + (t + 1) * P], src(b, t))
                fill_done(last, name)

            for name in MIDDLE:
                n = int(name[-1]) if name[-1].isdigit() else 0
                p, t0 = part(n)
                if "." in name:
                    quarter(name[:-2], n)
                    if n == 3:
                        filled(pe, name[:-2])
                        pe.sem_inc(S(f"slot_free{W_ORDER.index(name[:-2]) % RING}"), 1)
                elif name == "swap0":
                    pe.wait_ge(S("level_ready"), 1)
                    eight(name, lambda b, dst: mm(dst, level_l[:, b, :], ident))
                elif name.startswith("swap"):
                    pe.wait_ge(S("level_ready"), n + 1)
                    drained(pe, "swap0" if n == 1 else f"solve_T{n - 1}")
                    eight(name, lambda b, dst: mm(dst, level_l[:, b, :], inv_T[:, b, :]))
                elif name.startswith("solve_T"):
                    drained(pe, f"swap{n}")
                    if n == 1:
                        pe.wait_ge(S("solved"), 1)
                    else:
                        drained(pe, f"solve{n - 1}")
                    eight(name, lambda b, dst: mm(dst, inv[:, b, :], swap[:, b, :]))
                elif name.startswith("solve"):
                    eight(name, lambda b, dst: mm(dst, swap[:, b, :], inv[:, b, :]))
                elif name == "u":
                    drained(pe, f"solve_T{LEVELS - 1}")
                    pe.wait_ge(S("vb_ready"), 1)
                    eight(name, lambda b, dst: mm(dst, inv_T[:, b, :], tok_v[:, b, :]))
                elif name == "w_T":
                    pe.wait_ge(S("kbg_ready"), 1)
                    eight(name, lambda b, dst: mm(dst, kbg[:, b, :], inv_T[:, b, :]))
                elif name.startswith("state"):
                    pe.wait_ge(S("k_dec_ready"), 1)
                    drained(pe, "u" if n == 0 else f"v{n}")
                    eight(name, lambda b, dst: mm(dst, k_dec[p, t0 + b, :], u_sb[p, t0 + b, :]), GH)
                elif name.startswith("v"):
                    drained(pe, "w_T")
                    drained(pe, f"state{n - 1}")
                    eight(name, lambda b, dst: mm(dst[p], w_T[:, t0 + b, p], state[:, b, :]), GH)
                elif name.startswith("inter"):
                    eight(name, lambda b, dst: mm(dst[p], q_T[:, t0 + b, p], state[:, b, :]), GH)
                elif name.startswith("intra"):
                    drained(pe, f"v{2 * n + 1}")
                    eight(name, lambda b, dst: mm(dst, qk_T[:, 4 * n + b, :], u_sb[:, 4 * n + b, :]), GH)
                elif name.startswith("score"):
                    moba_score(name, n)
                elif name.startswith("probs_T"):
                    moba_probs_T(name, n)
                elif name.startswith("pv"):
                    moba_pv(name, n)
                elif name == "gdn_oT":
                    pe.wait_ge(S("gdn_gated"), 1)
                    turn_out(name, lambda b, t: o_gdn[:, 4 * t + b, :])
                elif name == "moba_oT":
                    pe.wait_ge(S("moba_normed"), TILES)
                    turn_out(name, lambda b, t: o_moba[:, t, b * P:(b + 1) * P])

            drained(pe, "moba_oT")
            drained(pe, "gdn_oT")
            weights_landed(pe, "out_a")
            weights_landed(pe, "out_b")

            def mix_out(t, between=None):
                name = f"mix_out{t}"
                take(pe, name)
                for half, w in enumerate(("out_a", "out_b")):
                    wv = weights(w).rearrange("p (k n) -> p k n", n=512)
                    for k in range(KB):
                        last = nc.tensor.matmul(halves(name)[:, half, :], oT[:, k, t * P:(t + 1) * P], wv[:, k, :],
                                                start=(k == 0), stop=(k == KB - 1))
                    if half == 0 and between:
                        between()
                fill_done(last, name)

            def x_turn(t):
                turn_tokens(f"x_hT{t}", xn, "x1_normed", t + 1)

            def x_query(t, between):
                name = f"x_q{t}"
                wv = weights("x_q").rearrange("p (k n) -> p k n", n=512)
                take(pe, name)
                drained(pe, f"x_hT{t}")
                for b in range(4):
                    for k in range(KB):
                        last = nc.tensor.matmul(blocks(name)[:, b, :], wv[:, k, b * P:(b + 1) * P],
                                                hT[:, k, t * P:(t + 1) * P], start=(k == 0), stop=(k == KB - 1))
                    if b == 2:
                        between()
                fill_done(last, name)

            def x_score(t):
                name = f"x_score{t}"
                take(pe, name)
                drained(pe, f"x_q{t}")
                for h in range(GH):
                    last = mm(pair(name)[:, SEQ * h:SEQ * h + SEQ], xq_T[:, h, t * P:(t + 1) * P], km_T[:, h, :])
                fill_done(last, name)

            def x_probs_turn(t):
                name = f"x_probs_T{t}"
                take(pe, name)
                pe.wait_ge(S("x_probs_ready"), t + 1)
                for h in range(GH):
                    for mt in range(TILES):
                        last = turn(name, blocks(name)[:, 2 * h + mt, :], x_p[t][:, h, mt * P:(mt + 1) * P])
                fill_done(last, name)

            def x_pv(t):
                name = f"x_pv{t}"
                drained(pe, f"x_probs_T{t}")
                take(pe, name)
                for h in range(GH):
                    for mt in range(TILES):
                        last = nc.tensor.matmul(blocks(name)[:, h, :], vm_sb[:, mt, h * P:(h + 1) * P],
                                                x_pT[:, 2 * h + mt, t * P:(t + 1) * P],
                                                start=(mt == 0), stop=(mt == TILES - 1))
                fill_done(last, name)

            def x_out(t, between):
                name = f"x_out{t}"
                wv = weights("x_o").rearrange("p (k n) -> p k n", n=D_MODEL)
                take(pe, name)
                drained(pe, f"x_pv{t}")
                for n in range(2 * GH):
                    half, h = n // GH, n % GH
                    if n in between:
                        between[n](1)
                    last = nc.tensor.matmul(halves(name)[:, half, :], oT[:, h, t * P:(t + 1) * P],
                                            wv[:, h, 512 * half:512 * half + 512],
                                            start=(h == 0), stop=(h == GH - 1))
                fill_done(last, name)

            def f_turn(t):
                turn_tokens(f"f_T{t}", xn, "x2_normed", t + 1)

            def router_logits(t):
                name = f"logits{t}"
                take(pe, name)
                drained(pe, f"f_T{t}")
                for k in range(KB):
                    last = nc.tensor.matmul(pair(name)[:, 0:E], hT[:, k, t * P:(t + 1) * P], router_sb[:, k, :],
                                            start=(k == 0), stop=(k == KB - 1))
                fill_done(last, name)

            mix_out(0)
            mix_out(1, lambda: x_turn(0))
            filled(pe, "mix_out1")
            for w in ("out_a", "out_b"):
                pe.sem_inc(S(f"slot_free{W_ORDER.index(w) % RING}"), 1)
            weights_landed(pe, "x_q")
            x_query(0, lambda: x_turn(1))
            drained(pe, "mem_k")
            x_query(1, lambda: x_score(0))
            x_score(1)
            filled(pe, "x_q1")
            pe.sem_inc(S(f"slot_free{W_ORDER.index('x_q') % RING}"), 1)
            drained(pe, "mem_v")
            x_probs_turn(0)
            x_pv(0)
            weights_landed(pe, "x_o")
            x_out(0, {2: x_probs_turn, 6: x_pv})
            x_out(1, {6: lambda t: f_turn(0)})
            filled(pe, "x_out1")
            pe.sem_inc(S(f"slot_free{W_ORDER.index('x_o') % RING}"), 1)
            pe.wait_ge(S("router_loaded"), 32)
            router_logits(0)
            f_turn(1)
            router_logits(1)
            pe.wait_ge(S("before_ready"), 2)
            pe.wait_ge(S("chosen_ready"), TILES)
            take(pe, "slots")
            mm(pair("slots")[:, 0:E], before, chosen_b[:, 0, :])
            nc.tensor.matmul(pair("slots")[:, E:2 * E], ones, chosen_b[:, 0, :], start=True, stop=False)
            fill_done(nc.tensor.matmul(pair("slots")[:, E:2 * E], before, chosen_b[:, 1, :],
                                       start=False, stop=True), "slots")
            take(pe, "count")
            for t in range(TILES):
                last = nc.tensor.matmul(pair("count")[:, 0:E], ones, chosen_b[:, t, :],
                                        start=(t == 0), stop=(t == TILES - 1))
            fill_done(last, "count")
            for name in ("f_T1", "logits1", "slots"):
                drained(pe, name)
            pe.wait_ge(S("split_low"), TILES)

            def gather(k, n):
                dst = bank(GATHER_BANK[k])
                for b in range(KB):
                    for s in range(3):
                        for t in range(TILES):
                            last = nc.tensor.matmul(dst[:, SLOTS * b:SLOTS * b + SLOTS],
                                                    split[s][:, t, b * P:(b + 1) * P], pick[k][:, t, :],
                                                    start=(s == 0 and t == 0), stop=(s == 2 and t == TILES - 1))
                last.then_inc(S("gather_filled"), 1)

            low, high = slice(0, HALF), slice(HALF, P)

            def chunk_landed(c, before, first):
                place, loaded, free, use = chunk_place(c, first)
                pe.wait_ge(S(loaded), 32 * before + 16 * (use + 1))
                return place, free

            def gate_up(k, before, first):
                for c in range(4):
                    place, free = chunk_landed(4 * k + c, before, first)
                    w = place.rearrange("p (k n) -> p k n", n=2 * D_MODEL)
                    for kk in range(2):
                        kb = 2 * c + kk
                        for q, (b, p) in enumerate(((GATE_BANK[k], low), (GATE_BANK[k], high),
                                                    (UP_BANK[k], low), (UP_BANK[k], high))):
                            last = nc.tensor.matmul(bank(b)[p], xg_T[k][:, kb, :], w[:, kk, 512 * q:512 * q + 512],
                                                    start=(kb == 0), stop=False)
                    if free:
                        last.then_inc(S(free), 1)
                for q, (b, p) in enumerate(((GATE_BANK[k], low), (GATE_BANK[k], high),
                                            (UP_BANK[k], low), (UP_BANK[k], high))):
                    last = nc.tensor.matmul(bank(b)[p], choose[0:96, k, :], bias_hi[0:96, 512 * q:512 * q + 512],
                                            start=False, stop=True)
                last.then_inc(S("gate_up_filled"), 1)

            def act_turned(k, n):
                pe.wait_ge(S("act_ready"), n)
                for b in range(4):
                    last = turn("", bank(ACT_T_BANK[k])[:, P * b:P * b + P], up_sb[:, P * b:P * b + P])
                last.then_inc(S("act_T_filled"), 1)

            def down(k, n, before, first):
                pe.wait_ge(S("act_T_ready"), n)
                places = ((0, low), (1, high)) if k == 0 else ((0, high), (1, low))
                for c in range(2):
                    place, free = chunk_landed(8 + 2 * k + c, before, first)
                    w = place.rearrange("p (k n) -> p k n", n=D_MODEL)
                    for b in range(4):
                        for q, (y, p) in enumerate(places):
                            last = nc.tensor.matmul(bank(Y_BANK + y)[p], act_T[:, b, HALF * c:HALF * c + HALF],
                                                    w[:, b, 512 * q:512 * q + 512],
                                                    start=(c == 0 and b == 0), stop=False)
                    if free:
                        last.then_inc(S(free), 1)
                for q, (y, p) in enumerate(places):
                    last = nc.tensor.matmul(bank(Y_BANK + y)[p], choose[0:96, k, :],
                                            bias_hi[0:96, 2048 + 512 * q:2560 + 512 * q], start=False, stop=True)
                last.then_inc(S("down_filled"), 1)

            def pair_of_experts(r, i, before, n, m, first=False, final=False):
                pe.wait_ge(S("gathered"), E * r + 2 * i + 1)
                pe.wait_ge(S("expert_chosen"), E * r + 2 * i + 2)
                pe.wait_ge(S("combined"), 2 * before + 1)
                gate_up(0, before, first)
                pe.wait_ge(S("gated_picked"), PAIRS * r + i + 1)
                pe.wait_ge(S("y_ready"), before + 1)
                for o in range(2):
                    for t in range(TILES):
                        last = turn("", bank(GATED_BANK)[:, SEQ * o + P * t:SEQ * o + P * t + P],
                                    pick_gated[:, t, HALF * o:HALF * o + P])
                last.then_inc(S("gated_T_filled"), 1)
                pe.wait_ge(S("gathered"), E * r + 2 * i + 2)
                gate_up(1, before, first)
                act_turned(0, n)
                pe.wait_ge(S("gated_T_ready"), before + 1)
                down(0, n, before, first)
                act_turned(1, m)
                down(1, m, before, first)
                pe.wait_ge(S("y_ready"), before + 2)
                for t in (1, 0):
                    b = COMBINE_BANK[t]
                    for q in range(2):
                        last = nc.tensor.matmul(bank(b + q), g_T[:, q, P * t:P * t + P], y_sb[:, q, :],
                                                start=True, stop=True)
                    last.then_inc(S("combine_filled"), 1)
                if not final:
                    pe.wait_ge(S("picked"), PAIRS * r + i + 2)
                    gather(0, 0)
                    gather(1, 0)

            def expert_pass(r, first=False):
                pe.wait_ge(S("picked"), PAIRS * r + 1)
                gather(0, 0)
                gather(1, 0)
                drained(pe, "count")
                pe.wait_ge(S("count_ready"), 1)
                pe.wait_ge(S("biases_ready"), 1)
                if first:
                    pair_of_experts(r, 0, 0, 1, 2, first=True)
                with pe.Fori(1 if first else 0, PAIRS - 1) as i:
                    pair_of_experts(r, i, pe.snap(r * PAIRS + i), pe.snap(r * E + 2 * i + 1),
                                    pe.snap(r * E + 2 * i + 2))
                i = PAIRS - 1
                pair_of_experts(r, i, pe.snap(r * PAIRS + i), pe.snap(r * E + 2 * i + 1), pe.snap(r * E + 2 * i + 2),
                                final=True)

            pe.sem_inc(S("act_T_filled"), 1)
            expert_pass(0, first=True)
            most = pe.value_load(count_i[0:1, 0:1], min_val=0, max_val=SEQ)
            with pe.If(most > SLOTS):
                with pe.Fori(1, PASSES) as r:
                    with pe.If(most > r * SLOTS):
                        expert_pass(r)


_INS = ["x", "mem", "norm_mix_g", "w_in", "gdn_conv_w", "gdn_A_log", "gdn_dt_bias", "gdn_norm_g", "moba_norm_g",
        "w_out", "norm_xattn_g", "norm_mem_g", "xattn_w_q", "xattn_w_kv", "xattn_w_o", "norm_ffn_g", "router_w",
        "router_b", "w_gate_up", "b_gate_up", "w_down", "b_down", "final_norm_g"]
_OUTS = [((1, SEQ, D_MODEL), "float32")]


def kernel(**inputs):
    import concourse.bacc as bacc
    from concourse.bass_utils import run_bass_kernel_spmd

    nc = bacc.Bacc("TRN2", target_bir_lowering=False, num_devices=1)
    arrays, args = {}, []
    for name in _INS:
        a = np.ascontiguousarray(inputs[name])
        arrays[f"in_{name}"] = a
        args.append(nc.dram_tensor(f"in_{name}", a.shape, mybir.dt.from_np(a.dtype), kind="ExternalInput").ap())
    for i, (shape, dtype) in enumerate(_OUTS):
        args.append(nc.dram_tensor(f"out_{i}", shape, mybir.dt.from_np(np.dtype(dtype)), kind="ExternalOutput").ap())
    bass_hybrid_block(nc, *args)
    r = run_bass_kernel_spmd(nc, [arrays], core_ids=[0])
    return r.results[0]["out_0"]
```
